# Optimizing a Trainium2 kernel written in Bass

```python
import jax, jax.numpy as jnp
from jax import lax
import numpy as np
import math

D_MODEL = 1024
BATCH = 1
SEQ = 1024
DEPTH = 1

CONV_WIDTH = D_MODEL
CONV_K = 3
N_Q_HEADS = 16
N_KV_HEADS = 4
HEAD_DIM = 64
ATTN_WIDTH = N_Q_HEADS * HEAD_DIM
KV_WIDTH = N_KV_HEADS * HEAD_DIM
WINDOW = 128
BLOCK = 128
N_BRANCHES = 2
EPS = 1e-6
NEG_INF = -1e30

IN_SIZES = (CONV_WIDTH, CONV_WIDTH, CONV_WIDTH, CONV_WIDTH,
            ATTN_WIDTH, KV_WIDTH, KV_WIDTH, ATTN_WIDTH,
            N_BRANCHES * D_MODEL)
IN_COLS = sum(IN_SIZES)
SPLIT_POINTS = tuple(int(c) for c in np.cumsum(IN_SIZES)[:-1])


def rms_norm(x, g):
    xf = x.astype(jnp.float32)
    y = xf * lax.rsqrt(jnp.mean(xf * xf, axis=-1, keepdims=True) + EPS)
    return (y * g.astype(jnp.float32)).astype(x.dtype)

def causal_depthwise_conv(u, w):
    s = u.shape[1]
    up = jnp.pad(u, ((0, 0), (CONV_K - 1, 0), (0, 0)))
    y = up[:, 0:s] * w[0]
    for k in range(1, CONV_K):
        y = y + up[:, k:k + s] * w[k]
    return y

def sliding_window_attention(q, k, v, sinks):
    b, s = q.shape[0], q.shape[1]
    nb = s // BLOCK
    g = N_Q_HEADS // N_KV_HEADS
    qb = q.reshape(b, nb, BLOCK, N_KV_HEADS, g, HEAD_DIM)

    def band(t):
        tb = t.reshape(b, nb, BLOCK, N_KV_HEADS, HEAD_DIM)
        prev = jnp.pad(tb[:, :-1], ((0, 0), (1, 0), (0, 0), (0, 0), (0, 0)))
        return jnp.concatenate([prev, tb], axis=2)

    kb, vb = band(k), band(v)
    scale = HEAD_DIM ** -0.5
    scores = jnp.einsum('bnqhgd,bnkhd->bnhgqk', qb.astype(jnp.float32),
                        kb.astype(jnp.float32)) * scale
    blk = jnp.arange(nb)[:, None, None]
    q_pos = blk * BLOCK + jnp.arange(BLOCK)[None, :, None]
    k_pos = (blk - 1) * BLOCK + jnp.arange(2 * BLOCK)[None, None, :]
    diff = q_pos - k_pos
    valid = (diff >= 0) & (diff < WINDOW) & (k_pos >= 0)
    scores = jnp.where(valid[None, :, None, None], scores, NEG_INF)
    sink = sinks.astype(jnp.float32).reshape(N_KV_HEADS, g)[None, None, :, :, None, None]
    m = jnp.maximum(jnp.max(scores, axis=-1, keepdims=True), sink)
    p = jnp.exp(scores - m)
    p = p / (jnp.sum(p, axis=-1, keepdims=True) + jnp.exp(sink - m))
    out = jnp.einsum('bnhgqk,bnkhd->bnqhgd', p.astype(v.dtype), vb)
    return out.reshape(b, s, ATTN_WIDTH)

def hybrid_layer(x, norm_g, w_in, conv_w, q_norm_g, k_norm_g, sinks,
                 w_conv_out, w_attn_out, gate_b, w_out):
    b, s, _ = x.shape
    h = rms_norm(x, norm_g)
    u = jnp.einsum('bsd,dc->bsc', h, w_in)
    v_c, b_c, c_c, z_c, q, k, v, z_a, gate_logits = jnp.split(u, SPLIT_POINTS, axis=-1)

    y_c = b_c * causal_depthwise_conv(c_c * v_c, conv_w)
    y_c = y_c * jax.nn.silu(z_c)
    y_a = jnp.einsum('bsc,cd->bsd', y_c, w_conv_out)

    q = rms_norm(q.reshape(b, s, N_Q_HEADS, HEAD_DIM), q_norm_g)
    k = rms_norm(k.reshape(b, s, N_KV_HEADS, HEAD_DIM), k_norm_g)
    v = v.reshape(b, s, N_KV_HEADS, HEAD_DIM)
    o = sliding_window_attention(q, k, v, sinks) * jax.nn.silu(z_a)
    y_b = jnp.einsum('bsc,cd->bsd', o, w_attn_out)

    gates = jax.nn.sigmoid(gate_logits + gate_b)
    g_a, g_b = jnp.split(gates, N_BRANCHES, axis=-1)
    merged = g_a * y_a + g_b * y_b
    return x + jnp.einsum('bsd,de->bse', merged, w_out)

def first_inputs(seed: int = 0) -> dict:
    key = jax.random.key(seed)
    ks = jax.random.split(key, 12)
    f32 = jnp.float32
    x = jax.random.normal(ks[0], (BATCH, SEQ, D_MODEL), f32)
    norm_g = 1.0 + 0.05 * jax.random.normal(ks[1], (DEPTH, D_MODEL), f32)
    w_in = jax.random.normal(ks[2], (DEPTH, D_MODEL, IN_COLS), f32) * D_MODEL ** -0.5
    conv_w = jax.random.normal(ks[3], (DEPTH, CONV_K, CONV_WIDTH), f32) * CONV_K ** -0.5
    q_norm_g = 1.0 + 0.05 * jax.random.normal(ks[4], (DEPTH, HEAD_DIM), f32)
    k_norm_g = 1.0 + 0.05 * jax.random.normal(ks[5], (DEPTH, HEAD_DIM), f32)
    sinks = 0.5 * jax.random.normal(ks[6], (DEPTH, N_Q_HEADS), f32)
    w_conv_out = jax.random.normal(ks[7], (DEPTH, CONV_WIDTH, D_MODEL), f32) * CONV_WIDTH ** -0.5
    w_attn_out = jax.random.normal(ks[8], (DEPTH, ATTN_WIDTH, D_MODEL), f32) * ATTN_WIDTH ** -0.5
    gate_b = 0.02 * jax.random.normal(ks[9], (DEPTH, N_BRANCHES * D_MODEL), f32)
    w_out = jax.random.normal(ks[10], (DEPTH, D_MODEL, D_MODEL), f32) * D_MODEL ** -0.5
    return {"x": x, "norm_g": norm_g, "w_in": w_in, "conv_w": conv_w,
            "q_norm_g": q_norm_g, "k_norm_g": k_norm_g, "sinks": sinks,
            "w_conv_out": w_conv_out, "w_attn_out": w_attn_out,
            "gate_b": gate_b, "w_out": w_out}

def first_block(x, norm_g, w_in, conv_w, q_norm_g, k_norm_g, sinks,
              w_conv_out, w_attn_out, gate_b, w_out):
    for l in range(DEPTH):
        x = hybrid_layer(x, norm_g[l], w_in[l], conv_w[l], q_norm_g[l], k_norm_g[l],
                         sinks[l], w_conv_out[l], w_attn_out[l], gate_b[l], w_out[l])
    return x


N_MIXERS = 2
N_ATTN_LAYERS = (DEPTH + N_MIXERS - 1) // N_MIXERS
N_SSM_LAYERS = DEPTH // N_MIXERS

ATTN_HEAD_DIM = 64
ATTN_HEADS = D_MODEL // ATTN_HEAD_DIM
Q_BLOCK = 128
SSM_EXPAND = 2
SSM_D_INNER = SSM_EXPAND * D_MODEL
SSM_HEAD_DIM = 64
SSM_HEADS = SSM_D_INNER // SSM_HEAD_DIM
SSM_GROUPS = 8
SSM_STATE = 128
SSM_CONV = 4
SSM_CHUNK = 128
SSM_XBC = SSM_D_INNER + 2 * SSM_GROUPS * SSM_STATE
FFN_DIM = 2816
FFN_CONV = 3
PLE_DIM = 256

LN_EPS = 1e-5
RMS_EPS = 1e-5
DEEPNORM_ALPHA = (2 * DEPTH) ** 0.25
DEEPNORM_BETA = (8 * DEPTH) ** -0.25


def layer_norm(x, g, b):
    xf = x.astype(jnp.float32)
    mu = jnp.mean(xf, axis=-1, keepdims=True)
    var = jnp.mean(jnp.square(xf - mu), axis=-1, keepdims=True)
    return ((xf - mu) * lax.rsqrt(var + LN_EPS) * g + b).astype(x.dtype)

def causal_dwconv(u, w, b):
    K = w.shape[0]
    S = u.shape[1]
    up = jnp.pad(u, ((0, 0), (K - 1, 0), (0, 0)))
    out = b
    for k in range(K):
        out = out + up[:, k:k + S] * w[k]
    return out

def fox_mixer(x, w_in, b_f, w_out):
    Bsz, S, _ = x.shape
    H, Dh = ATTN_HEADS, ATTN_HEAD_DIM
    proj = x @ w_in
    q, k, v, f_logit = jnp.split(proj, [D_MODEL, 2 * D_MODEL, 3 * D_MODEL], axis=-1)
    q = q.reshape(Bsz, S, H, Dh).transpose(0, 2, 1, 3)
    k = k.reshape(Bsz, S, H, Dh).transpose(0, 2, 1, 3)
    v = v.reshape(Bsz, S, H, Dh).transpose(0, 2, 1, 3)
    log_f = jax.nn.log_sigmoid(f_logit.astype(jnp.float32) + b_f)
    c = jnp.cumsum(log_f, axis=1).transpose(0, 2, 1)
    nb = S // Q_BLOCK
    qb = q.reshape(Bsz, H, nb, Q_BLOCK, Dh).transpose(2, 0, 1, 3, 4)
    cqb = c.reshape(Bsz, H, nb, Q_BLOCK).transpose(2, 0, 1, 3)
    kpos = jnp.arange(S)
    scale = 1.0 / math.sqrt(Dh)

    def block(args):
        qi, cqi, bi = args
        s = jnp.einsum('bhqd,bhkd->bhqk', qi, k).astype(jnp.float32) * scale
        s = s + cqi[..., None] - c[:, :, None, :]
        qpos = bi * Q_BLOCK + jnp.arange(Q_BLOCK)
        s = jnp.where(kpos[None, :] <= qpos[:, None], s, -jnp.inf)
        pr = jax.nn.softmax(s, axis=-1)
        return jnp.einsum('bhqk,bhkd->bhqd', pr.astype(v.dtype), v)

    o = lax.map(block, (qb, cqb, jnp.arange(nb)))
    o = o.transpose(1, 0, 3, 2, 4).reshape(Bsz, S, D_MODEL)
    return o @ w_out

def ssd_scan(xh, dt, A, Bm, Cm):
    Bsz, S = xh.shape[0], xh.shape[1]
    G, R, P, N, Q = SSM_GROUPS, SSM_HEADS // SSM_GROUPS, SSM_HEAD_DIM, SSM_STATE, SSM_CHUNK
    nc = S // Q

    def to_chunks(t):
        return jnp.moveaxis(t.reshape((Bsz, nc, Q) + t.shape[2:]), 1, 0)

    xc = to_chunks(xh.reshape(Bsz, S, G, R, P))
    dtc = to_chunks(dt.reshape(Bsz, S, G, R))
    Bc = to_chunks(Bm)
    Cc = to_chunks(Cm)
    A_g = A.reshape(G, R)
    tri = jnp.tril(jnp.ones((Q, Q), dtype=bool))[None, :, :, None, None]

    def step(state, inp):
        x_, dt_, B_, C_ = inp
        acum = jnp.cumsum(dt_ * A_g, axis=1)
        seg = acum[:, :, None] - acum[:, None, :]
        L = jnp.exp(jnp.where(tri, seg, -jnp.inf))
        CB = jnp.einsum('btgn,bsgn->btsg', C_, B_)
        y_intra = jnp.einsum('btsg,btsgr,bsgr,bsgrp->btgrp', CB, L, dt_, x_)
        y_inter = jnp.einsum('btgn,bgrpn,btgr->btgrp', C_, state, jnp.exp(acum))
        w_end = jnp.exp(acum[:, -1:] - acum) * dt_
        new_state = state * jnp.exp(acum[:, -1])[..., None, None] + \
            jnp.einsum('bsgn,bsgr,bsgrp->bgrpn', B_, w_end, x_)
        return new_state, (y_intra + y_inter).astype(jnp.float32)

    state0 = jnp.zeros((Bsz, G, R, P, N), jnp.float32)
    _, y = lax.scan(step, state0, (xc, dtc, Bc, Cc))
    return jnp.moveaxis(y, 0, 1).reshape(Bsz, S, SSM_HEADS, P)

def ssd_mixer(x, w_in, conv_w, conv_b, dt_bias, A_log, D_skip, norm_w, w_out):
    Bsz, S, _ = x.shape
    GN = SSM_GROUPS * SSM_STATE
    proj = x @ w_in
    z, xBC, dt_raw = jnp.split(proj, [SSM_D_INNER, SSM_D_INNER + SSM_XBC], axis=-1)
    xBC = jax.nn.silu(causal_dwconv(xBC, conv_w, conv_b))
    xs, Bm, Cm = jnp.split(xBC, [SSM_D_INNER, SSM_D_INNER + GN], axis=-1)
    dt = jax.nn.softplus(dt_raw.astype(jnp.float32) + dt_bias)
    A = -jnp.exp(A_log.astype(jnp.float32))
    xh = xs.reshape(Bsz, S, SSM_HEADS, SSM_HEAD_DIM)
    y = ssd_scan(xh, dt, A,
                 Bm.reshape(Bsz, S, SSM_GROUPS, SSM_STATE),
                 Cm.reshape(Bsz, S, SSM_GROUPS, SSM_STATE))
    y = y + D_skip[:, None] * xh
    y = y.reshape(Bsz, S, SSM_D_INNER) * jax.nn.silu(z.astype(jnp.float32))
    yg = y.reshape(Bsz, S, SSM_GROUPS, SSM_D_INNER // SSM_GROUPS)
    yg = yg * lax.rsqrt(jnp.mean(jnp.square(yg), axis=-1, keepdims=True) + RMS_EPS)
    y = yg.reshape(Bsz, S, SSM_D_INNER) * norm_w
    return y.astype(x.dtype) @ w_out

def conv_ffn(x, w_up, conv_w, conv_b, w_down):
    u, g = jnp.split(x @ w_up, [FFN_DIM], axis=-1)
    g = causal_dwconv(g, conv_w, conv_b)
    return (jax.nn.gelu(g, approximate=False) * u) @ w_down

def second_inputs(seed: int = 0) -> dict:
    key = jax.random.key(seed)
    ks = iter(jax.random.split(key, 40))

    def nrm(shape, scale):
        return jax.random.normal(next(ks), shape, jnp.float32) * scale

    D, H = D_MODEL, ATTN_HEADS
    NA, NB = N_ATTN_LAYERS, N_SSM_LAYERS
    beta = DEEPNORM_BETA
    x = nrm((BATCH, SEQ, D), 1.0)
    p = nrm((DEPTH, BATCH, SEQ, PLE_DIM), 1.0)
    attn_w_in = nrm((NA, D, 3 * D + H), D ** -0.5)
    attn_w_in = attn_w_in.at[:, :, 2 * D:3 * D].multiply(beta)
    attn_b_f = jax.random.uniform(next(ks), (NA, H), jnp.float32, 1.0, 6.0)
    attn_w_out = nrm((NA, D, D), beta * D ** -0.5)
    ssm_in_dim = 2 * SSM_D_INNER + 2 * SSM_GROUPS * SSM_STATE + SSM_HEADS
    ssm_w_in = nrm((NB, D, ssm_in_dim), D ** -0.5)
    ssm_conv_w = nrm((NB, SSM_CONV, SSM_XBC), SSM_CONV ** -0.5)
    ssm_conv_b = nrm((NB, SSM_XBC), 0.02)
    dt0 = jnp.exp(jax.random.uniform(next(ks), (NB, SSM_HEADS), jnp.float32,
                                     math.log(1e-3), math.log(1e-1)))
    ssm_dt_bias = dt0 + jnp.log(-jnp.expm1(-dt0))
    ssm_A_log = jnp.log(jax.random.uniform(next(ks), (NB, SSM_HEADS), jnp.float32, 1.0, 16.0))
    ssm_D = 1.0 + nrm((NB, SSM_HEADS), 0.1)
    ssm_norm_w = 1.0 + nrm((NB, SSM_D_INNER), 0.05)
    ssm_w_out = nrm((NB, SSM_D_INNER, D), beta * SSM_D_INNER ** -0.5)
    ln_mix_g = 1.0 + nrm((DEPTH, D), 0.05)
    ln_mix_b = nrm((DEPTH, D), 0.02)
    ffn_w_up = nrm((DEPTH, D, 2 * FFN_DIM), D ** -0.5)
    ffn_conv_w = nrm((DEPTH, FFN_CONV, FFN_DIM), FFN_CONV ** -0.5)
    ffn_conv_b = nrm((DEPTH, FFN_DIM), 0.02)
    ffn_w_down = nrm((DEPTH, FFN_DIM, D), beta * FFN_DIM ** -0.5)
    ln_ffn_g = 1.0 + nrm((DEPTH, D), 0.05)
    ln_ffn_b = nrm((DEPTH, D), 0.02)
    ple_w_proj = nrm((DEPTH, PLE_DIM, D), beta * PLE_DIM ** -0.5)
    ple_w_gate = nrm((DEPTH, D, D), D ** -0.5)
    ple_b_gate = nrm((DEPTH, D), 0.02)
    return {"x": x, "p": p,
            "attn_w_in": attn_w_in, "attn_b_f": attn_b_f, "attn_w_out": attn_w_out,
            "ssm_w_in": ssm_w_in, "ssm_conv_w": ssm_conv_w, "ssm_conv_b": ssm_conv_b,
            "ssm_dt_bias": ssm_dt_bias, "ssm_A_log": ssm_A_log, "ssm_D": ssm_D,
            "ssm_norm_w": ssm_norm_w, "ssm_w_out": ssm_w_out,
            "ln_mix_g": ln_mix_g, "ln_mix_b": ln_mix_b,
            "ffn_w_up": ffn_w_up, "ffn_conv_w": ffn_conv_w, "ffn_conv_b": ffn_conv_b,
            "ffn_w_down": ffn_w_down, "ln_ffn_g": ln_ffn_g, "ln_ffn_b": ln_ffn_b,
            "ple_w_proj": ple_w_proj, "ple_w_gate": ple_w_gate, "ple_b_gate": ple_b_gate}

def second_block(x, p, attn_w_in, attn_b_f, attn_w_out, ssm_w_in, ssm_conv_w, ssm_conv_b,
              ssm_dt_bias, ssm_A_log, ssm_D, ssm_norm_w, ssm_w_out, ln_mix_g, ln_mix_b,
              ffn_w_up, ffn_conv_w, ffn_conv_b, ffn_w_down, ln_ffn_g, ln_ffn_b,
              ple_w_proj, ple_w_gate, ple_b_gate):
    for i in range(DEPTH):
        j = i // N_MIXERS
        if i % N_MIXERS == 0:
            mix = fox_mixer(x, attn_w_in[j], attn_b_f[j], attn_w_out[j])
        else:
            mix = ssd_mixer(x, ssm_w_in[j], ssm_conv_w[j], ssm_conv_b[j], ssm_dt_bias[j],
                            ssm_A_log[j], ssm_D[j], ssm_norm_w[j], ssm_w_out[j])
        x = layer_norm(DEEPNORM_ALPHA * x + mix, ln_mix_g[i], ln_mix_b[i])
        ffn = conv_ffn(x, ffn_w_up[i], ffn_conv_w[i], ffn_conv_b[i], ffn_w_down[i])
        x = layer_norm(DEEPNORM_ALPHA * x + ffn, ln_ffn_g[i], ln_ffn_b[i])
        gate = jax.nn.sigmoid(x @ ple_w_gate[i] + ple_b_gate[i])
        x = x + gate * (p[i] @ ple_w_proj[i])
    return x


def setup_inputs(seed=0):
    out = dict(first_inputs(seed))
    for name, value in second_inputs(seed + 1).items():
        if name != "x":
            out[name + "_2"] = value
    return out


def reference(
    x, norm_g, w_in, conv_w, q_norm_g, k_norm_g, sinks, w_conv_out, w_attn_out, gate_b, w_out,
    p_2, attn_w_in_2, attn_b_f_2, attn_w_out_2, ssm_w_in_2, ssm_conv_w_2, ssm_conv_b_2,
    ssm_dt_bias_2, ssm_A_log_2, ssm_D_2, ssm_norm_w_2, ssm_w_out_2, ln_mix_g_2, ln_mix_b_2,
    ffn_w_up_2, ffn_conv_w_2, ffn_conv_b_2, ffn_w_down_2, ln_ffn_g_2, ln_ffn_b_2, ple_w_proj_2,
    ple_w_gate_2, ple_b_gate_2,
):
    x = first_block(
        x, norm_g, w_in, conv_w, q_norm_g, k_norm_g, sinks, w_conv_out, w_attn_out, gate_b,
        w_out,
    )
    return second_block(
        x, p_2, attn_w_in_2, attn_b_f_2, attn_w_out_2, ssm_w_in_2, ssm_conv_w_2, ssm_conv_b_2,
        ssm_dt_bias_2, ssm_A_log_2, ssm_D_2, ssm_norm_w_2, ssm_w_out_2, ln_mix_g_2, ln_mix_b_2,
        ffn_w_up_2, ffn_conv_w_2, ffn_conv_b_2, ffn_w_down_2, ln_ffn_g_2, ln_ffn_b_2,
        ple_w_proj_2, ple_w_gate_2, ple_b_gate_2,
    )


_drawn_inputs = setup_inputs


def setup_inputs(seed=0):
    import zlib

    import numpy as np

    out = dict(_drawn_inputs(seed))
    spreads = {}
    factors = {'q_norm_g': 8.0,
     'k_norm_g': 8.0,
     'sinks': 200.0,
     'gate_b': 8.0,
     'ln_mix_b_2': 2.84,
     'ffn_conv_b_2': 8.0,
     'ln_ffn_b_2': 2.953,
     'ple_b_gate_2': 23.955}
    for name, (base, spread) in spreads.items():
        noise = np.random.default_rng([zlib.crc32(name.encode()), seed]).standard_normal(out[name].shape)
        drawn = base * np.exp(spread * noise) if base else spread * noise
        out[name] = __import__('jax').numpy.asarray(drawn.astype(out[name].dtype))
    for name, factor in factors.items():
        out[name] = (out[name] * factor).astype(out[name].dtype)
    return out
```

```python
from contextlib import ExitStack

import numpy as np
import concourse.bass as bass
import concourse.mybir as mybir

F32 = mybir.dt.float32
F32R = mybir.dt.float32r
ALU = mybir.AluOpType
ACT = mybir.ActivationFunctionType
AX = mybir.AxisListType.X

P = 128
D = 1024
S = 1024
KT = D // P
HALF = 512
DH = 64
NPAIR = 8
NB = S // P
FFN = 2816
FT = FFN // P
NGRP = FT // 2
PLE_KT = 2
NEG = -1e30
SCALE = DH ** -0.5
ALPHA = 2.0 ** 0.25
RMS_EPS, LN_EPS = 1e-6, 1e-5

U_CONV = 0
U_MIX = U_CONV + 4 * KT
U_SWA = U_MIX + 2 * KT
SWA_KV = 2 + 4 * 3
U_AOUT = U_SWA + 2 * SWA_KV
U_OUT = U_AOUT + KT
U_F = U_OUT + KT
U_FOX = U_F + 1
U_FOUT = U_FOX + 3 * NPAIR
U_FFN = U_FOUT + KT
U_PLE = U_FFN + 6 * NGRP
U_GATE = U_PLE + 2
U_END = U_GATE + KT
T_FFN = U_FFN
T_PLE = T_FFN + 12 * NGRP
T_GATE = T_PLE + KT
T_END = T_GATE + KT

C_NORM = 0
C_CONV = C_NORM + KT
C_QG = C_CONV + 3 * KT
C_KG = C_QG + 1
C_GATEB = C_KG + 1
C_FCW = C_GATEB + 2 * KT
C_FCB = C_FCW + 3 * FT
C_LN1G = C_FCB + FT
C_LN1B = C_LN1G + KT
C_LN2G = C_LN1B + KT
C_LN2B = C_LN2G + KT
C_PLEB = C_LN2B + KT
C_BF = C_PLEB + KT
C_SINK = C_BF + 1
N_COLS = C_SINK + 2 * NPAIR


class NormSemaphores:

    def __init__(self, sem, n):
        self.x_in = sem(n + "_x_in")
        self.acc = sem(n + "_acc")
        self.mean = sem(n + "_mean")
        self.centred = sem(n + "_centred")
        self.sq = sem(n + "_sq")
        self.sq_used = sem(n + "_sq_used")
        self.std = sem(n + "_std")
        self.rstd = sem(n + "_rstd")
        self.y = sem(n + "_y")
        self.yb = sem(n + "_yb")
        self.hi = sem(n + "_hi")
        self.lo = sem(n + "_lo")


class AttentionSemaphores:

    def __init__(self, sem, n):
        self.q_sq = sem(n + "_q_sq")
        self.q_ms = sem(n + "_q_ms")
        self.q_std = sem(n + "_q_std")
        self.q_rstd = sem(n + "_q_rstd")
        self.q_n = sem(n + "_q_n")
        self.q_hi = sem(n + "_q_hi")
        self.q_lo = sem(n + "_q_lo")
        self.v_flip = sem(n + "_v_flip")
        self.v_hi = sem(n + "_v_hi")
        self.v_lo = sem(n + "_v_lo")
        self.scored = sem(n + "_scored")
        self.max = sem(n + "_max")
        self.neg_max = sem(n + "_neg_max")
        self.exp = sem(n + "_exp")
        self.sink = sem(n + "_sink")
        self.total = sem(n + "_total")
        self.inv = sem(n + "_inv")
        self.prob = sem(n + "_prob")
        self.flipped = sem(n + "_flipped")
        self.hi = sem(n + "_hi")
        self.lo = sem(n + "_lo")
        self.pv = sem(n + "_pv")
        self.fold = sem(n + "_fold")
        self.o = sem(n + "_o")
        self.og = sem(n + "_og")
        self.o_hi = sem(n + "_o_hi")
        self.o_lo = sem(n + "_o_lo")
        self.g_out = sem(n + "_g_out")
        self.c_in = sem(n + "_c_in")


def attention_plan(window):
    steps, chunks, ends = [], [], []
    for hh in range(2):
        for qb in range(NB):
            k0 = max(0, qb - 1) * P if window else 0
            w = (qb + 1) * P - k0
            s = len(steps)
            steps.append((hh, qb, k0, w))
            for c in range(0, w, HALF):
                chunks.append((s, c, min(HALF, w - c), c == 0, c + HALF >= w))
            ends.append(len(chunks))
    return steps, chunks, ends


def build(nc, xT, weights, cols, pT, out, t_scr, g_scr, c_scr):
    ctx = ExitStack()
    with ctx:
        top = [0]
        base = -(-nc.sbuf_base // 32) * 32

        def fixed(name, shape, dt):
            n = int(np.prod(shape[1:])) * 4
            t = nc.alloc_sbuf_tensor_at(name, [P, *shape[1:]], dt, offset=base + top[0])
            top[0] += -(-n // 32) * 32
            return t

        total = 207 * 1024 + 512

        raw = [fixed(f"raw{b}", [P, HALF], F32) for b in range(2)]
        whi = [fixed(f"whi{s}", [P, KT, P], F32R) for s in range(2)]
        wlo = [fixed(f"wlo{s}", [P, KT, P], F32R) for s in range(2)]
        ident = fixed("ident", [P, P], F32)
        ident_r = fixed("ident_r", [P, P], F32R)
        mask_r = fixed("mask_r", [P, 2 * P], F32R)
        head_mean = fixed("head_mean", [P, P], F32)
        feat_mean = fixed("feat_mean", [P, P], F32)
        cst = fixed("cst", [P, N_COLS], F32)
        eps_rms = fixed("eps_rms", [P, 1], F32)
        eps_ln = fixed("eps_ln", [P, 1], F32)
        neg_sink = fixed("neg_sink", [P, 2 * NPAIR], F32)
        mx = fixed("mx", [P, 2], F32)
        neg_max = fixed("neg_max", [P, 2], F32)
        row_sum = fixed("row_sum", [P, 2], F32)
        sink_exp = fixed("sink_exp", [P, 2], F32)
        row_inv = fixed("row_inv", [P, 2], F32)
        a_hi = fixed("a_hi", [P, KT, S], F32R)
        a_lo = fixed("a_lo", [P, KT, S], F32R)
        b_hi_at = top[0]
        b_hi = fixed("b_hi", [P, KT, S], F32R)
        b_lo_at = top[0]
        b_lo = fixed("b_lo", [P, KT, S], F32R)
        over_at = top[0]

        def overlay(at, *specs):
            top[0] = at
            made = [fixed(*x) for x in specs]
            assert top[0] <= total, (top[0], total)
            return made

        z, sq0, sq1, nrm, acc = overlay(over_at, ("z", [P, KT, S], F32), ("sq0", [P, S], F32), ("sq1", [P, S], F32),
                                        ("nrm", [P, S], F32), ("acc", [P, S], F32))
        sq = [sq0, sq1]
        (mask_f,) = overlay(b_hi_at, ("mask_f", [P, 2 * P], F32))
        cv_v, cv_u, cv_y, cv_g, cv_o = overlay(over_at, ("cv_v", [P, S], F32), ("cv_u", [P, S + 2], F32),
                                               ("cv_y", [P, S], F32), ("cv_g", [P, S], F32), ("cv_o", [P, S], F32))
        mix_y, mix_g, mix_t = overlay(over_at, ("mix_y", [P, S], F32), ("mix_g", [P, S], F32), ("mix_t", [P, S], F32))
        (sk_hi, sk_lo, sq_hi, sq_lo, sv, sp0, sp1, sph0, sph1, spl0, spl1, s_fold, s_o, s_z, s_g, s_raw, s_sq) = overlay(
            over_at, ("sk_hi", [P, S], F32R), ("sk_lo", [P, S], F32R), ("sq_hi", [P, S], F32R), ("sq_lo", [P, S], F32R),
            ("sv", [P, NB, 2, P], F32R), ("sp0", [P, 2 * P], F32), ("sp1", [P, 2 * P], F32),
            ("sph0", [P, 2 * P], F32R), ("sph1", [P, 2 * P], F32R), ("spl0", [P, 2 * P], F32R), ("spl1", [P, 2 * P], F32R),
            ("s_fold", [P, HALF], F32), ("s_o", [P, S], F32), ("s_z", [P, S], F32), ("s_g", [P, S], F32),
            ("s_raw", [P, S], F32), ("s_sq", [P, S], F32))
        m_t0, m_t1, m_g0, m_g1, m_m = overlay(over_at, ("m_t0", [P, S], F32), ("m_t1", [P, S], F32),
                                              ("m_g0", [P, S], F32), ("m_g1", [P, S], F32), ("m_m", [P, S], F32))
        x_in0, x_in1, x_sum = overlay(over_at + 20 * 1024, ("x_in0", [P, S], F32), ("x_in1", [P, S], F32),
                                      ("x_sum", [P, S], F32))
        (fk_hi, fk_lo, fq_hi, fq_lo, fv, fp0, fp1, fph0, fph1, fpl0, fpl1, fc0, fc1, f_fold, f_o) = overlay(
            over_at, ("fk_hi", [P, S], F32R), ("fk_lo", [P, S], F32R), ("fq_hi", [P, S], F32R), ("fq_lo", [P, S], F32R),
            ("fv", [P, NB, 2, P], F32R), ("fp0", [P, S], F32), ("fp1", [P, S], F32),
            ("fph0", [P, HALF], F32R), ("fph1", [P, HALF], F32R), ("fpl0", [P, HALF], F32R), ("fpl1", [P, HALF], F32R),
            ("fc0", [P, S], F32), ("fc1", [P, S], F32), ("f_fold", [P, HALF], F32), ("f_o", [P, S], F32))
        _, up_u, up_g, up_y, up_o = overlay(over_at, ("z_again", [P, KT, S], F32), ("up_u", [P, S], F32),
                                            ("up_g", [P, S + 2], F32), ("up_y", [P, S], F32), ("up_o", [P, S], F32))
        (ple,) = overlay(b_hi_at, ("ple", [P, KT, S], F32))
        p_raw, p_hi, p_lo, g_sig, g_out = overlay(
            b_lo_at, ("p_raw", [P, PLE_KT, S], F32), ("p_hi", [P, PLE_KT, S], F32R), ("p_lo", [P, PLE_KT, S], F32R),
            ("g_sig", [P, S], F32), ("g_out", [P, S], F32))

        def psum(name, n):
            return ctx.enter_context(nc.psum_tensor(name, [P, n], F32))

        bank = [psum(f"bank{h}", HALF) for h in range(2)]
        score = [psum(f"score{s}", S) for s in range(2)]
        flip = psum("flip", HALF)
        pv = psum("pv", HALF)

        def sem(name):
            return ctx.enter_context(nc.semaphore(name))

        cols_in = sem("cols_in")
        const_made = sem("const_made")
        raw_in = [sem(f"raw_in{b}") for b in range(2)]
        w_hi = sem("w_hi")
        w_lo = sem("w_lo")
        tile_done = [sem(f"tile_done{h}") for h in range(2)]
        tile_out = [sem(f"tile_out{h}") for h in range(2)]

        n0, n1, n2 = NormSemaphores(sem, "n0"), NormSemaphores(sem, "n1"), NormSemaphores(sem, "n2")
        sw, fx = AttentionSemaphores(sem, "sw"), AttentionSemaphores(sem, "fx")
        conv_step = sem("conv_step")
        conv_o = sem("conv_o")
        conv_hi = sem("conv_hi")
        conv_lo = sem("conv_lo")
        mix_done = sem("mix_done")
        t_stored = sem("t_stored")
        mt_in = [sem(f"mt_in{s}") for s in range(2)]
        mg_in = [sem(f"mg_in{s}") for s in range(2)]
        m_sum = sem("m_sum")
        m_hi = sem("m_hi")
        m_lo = sem("m_lo")
        x_in = [sem(f"x_in_{s}") for s in range(2)]
        x_hi = sem("x_hi")
        x_lo = sem("x_lo")
        f_step = sem("f_step")
        c_stored = sem("c_stored")
        z_part = sem("z_part")
        ffn_pad = sem("ffn_pad")
        up_conv = sem("up_conv")
        up_gelu = sem("up_gelu")
        up_prod = sem("up_prod")
        up_hi = sem("up_hi")
        up_lo = sem("up_lo")
        z_alpha = sem("z_alpha")
        p_in = sem("p_in")
        ple_hi = sem("ple_hi")
        ple_lo = sem("ple_lo")
        g_done = sem("g_done")
        g_sum = sem("g_sum")
        out_stored = sem("out_stored")

        passed = sem("passed")

        def settler(engine):
            def settle():
                engine.sem_inc(passed, 1)
            return settle

        block = ctx.enter_context(nc.Block())

        def hs(h):
            return slice(h * HALF, (h + 1) * HALF)

        def col(c):
            return cst[:, bass.ds(c, 1)] if not isinstance(c, int) else cst[:, c:c + 1]

        s_steps, s_chunks, s_ends = attention_plan(True)
        f_steps, f_chunks, f_ends = attention_plan(False)
        NST, NGR = len(s_steps), 4
        NCS, NCF = len(s_chunks), len(f_chunks)

        @block.sync
        def _(sp):
            for b in range(2):
                sp.dma_start(raw[b][:], weights[0, :, hs(b)]).then_inc(raw_in[b], 16)
            with sp.Fori(1, U_END) as u:
                for b in range(2):
                    sp.wait_ge(w_lo, u * 2 + (b - 1))
                    sp.dma_start(raw[b][:], weights[u, :, hs(b)]).then_inc(raw_in[b], 16)

        @block.gpsimd
        def _(pool):
            nc.gpsimd.memset(ident[:], 0.0).then_inc(const_made, 1)
            nc.gpsimd.memset(mask_f[:], 0.0).then_inc(const_made, 1)
            nc.gpsimd.memset(head_mean[:], 0.0).then_inc(const_made, 1)
            nc.gpsimd.memset(feat_mean[:], 1.0 / D).then_inc(const_made, 1)
            pool.wait_ge(const_made, 4)
            nc.gpsimd.affine_select(out=ident[:], in_=ident[:], compare_op=ALU.not_equal, fill=1.0, base=0,
                                    pattern=[[-1, P]], channel_multiplier=1).then_inc(const_made, 1)
            nc.gpsimd.affine_select(out=mask_f[:, 0:P], in_=mask_f[:, 0:P], compare_op=ALU.is_gt, fill=NEG, base=0,
                                    pattern=[[1, P]], channel_multiplier=-1).then_inc(const_made, 1)
            nc.gpsimd.affine_select(out=mask_f[:, P:2 * P], in_=mask_f[:, P:2 * P], compare_op=ALU.is_ge, fill=NEG,
                                    base=0, pattern=[[-1, P]], channel_multiplier=1).then_inc(const_made, 1)
            pool.wait_ge(const_made, 7)
            for h in range(2):
                nc.gpsimd.memset(head_mean[h * DH:(h + 1) * DH, h * DH:(h + 1) * DH], 1.0 / DH).then_inc(const_made, 1)
            pool.wait_ge(const_made, 9)
            nc.gpsimd.tensor_scalar(ident_r[:], ident[:], 1.0, 1.0, ALU.mult, ALU.mult).then_inc(const_made, 1)
            nc.gpsimd.tensor_scalar(mask_r[:], mask_f[:], 1.0, 1.0, ALU.mult, ALU.mult).then_inc(const_made, 1)
            nc.gpsimd.memset(eps_rms[:], RMS_EPS).then_inc(const_made, 1)
            nc.gpsimd.memset(eps_ln[:], LN_EPS).then_inc(const_made, 1)

            settle = settler(pool)

            def split(u, slot, freed):
                for b in range(2):
                    if freed is not None and b == 0:
                        pool.wait_ge(tile_done[1], freed)
                    pool.wait_ge(raw_in[b], u * 16 + 16)
                    settle()
                    hi, lo = whi[slot][:, 4 * b:4 * b + 4, :], wlo[slot][:, 4 * b:4 * b + 4, :]
                    src = raw[b][:].rearrange("p (k c) -> p k c", c=P)
                    nc.gpsimd.tensor_scalar(hi, src, 1.0, 1.0, ALU.mult, ALU.mult).then_inc(w_hi, 1)
                    pool.wait_ge(w_hi, u * 2 + (b + 1))
                    nc.gpsimd.tensor_tensor(lo, src, hi.bitcast(F32), ALU.subtract).then_inc(w_lo, 1)

            split(0, 0, None)
            split(1, 1, None)
            assert (U_FFN + 4 - 2) % 2 == 1
            with pool.Fori(0, (U_FFN + 4 - 3) // 2) as it:
                for c in range(2):
                    split(it * 2 + (2 + c), c, it * 2 + (1 + c))
            u = U_FFN + 3
            split(u, u % 2, u - 1)
            freed = (-1, 0, 1, 2, 3, 4)
            with pool.Fori(0, NGRP - 1) as it:
                for c in range(6):
                    split(it * 6 + (U_FFN + 4 + c), (U_FFN + c) % 2, it * 12 + (T_FFN + 4 + freed[c]))
            t = T_FFN + 4 + 12 * (NGRP - 1)
            for c, freed in enumerate((t - 4, t, t + 4, t + 8)):
                u = U_FFN + 4 + 6 * (NGRP - 1) + c
                split(u, u % 2, freed)
            for c in range(KT):
                u = U_GATE + c
                split(u, u % 2, (T_PLE + 4, T_PLE + 8)[c] if c < 2 else T_GATE + c - 1)

        @block.tensor
        def _(pe):
            def product(psum_ap, w, hi, lo, kts, wk, h):
                n = len(kts)
                for i, (kt, k) in enumerate(zip(kts, wk)):
                    for j, (ws, a) in enumerate(((whi, hi), (whi, lo), (wlo, hi))):
                        last = nc.tensor.matmul(psum_ap, ws[w][:, k, :], a[:, kt, hs(h)],
                                                start=(i == 0 and j == 0), stop=(i == n - 1 and j == 2))
                return last

            def tile(u, t, slot, hi, lo):
                pe.wait_ge(w_lo, u * 2 + 2)
                for h in range(2):
                    pe.wait_ge(tile_out[h], t)
                    product(bank[h][:], slot, hi, lo, range(KT), range(KT), h).then_inc(tile_done[h], 1)

            def quarter_tiles(u, t, slot, hi, lo, kts):
                pe.wait_ge(w_lo, u * 2 + 2)
                for m in range(4):
                    for h in range(2):
                        pe.wait_ge(tile_out[h], t + m)
                        product(bank[h][:], slot, hi, lo, kts, (2 * m, 2 * m + 1), h).then_inc(tile_done[h], 1)

            def norm(ns, mean):
                if mean:
                    for h in range(2):
                        if h == 0:
                            pe.wait_ge(ns.acc, 2 * KT)
                        nc.tensor.matmul(score[0][:, hs(h)], feat_mean[:], acc[:, hs(h)],
                                         start=True, stop=True).then_inc(ns.mean, 1)
                for j in range(KT):
                    pe.wait_ge(ns.sq, j + 1)
                    for h in range(2):
                        last = nc.tensor.matmul(score[1][:, hs(h)], feat_mean[:], sq[j % 2][:, hs(h)],
                                                start=(j == 0), stop=(j == KT - 1))
                    last.then_inc(ns.sq_used, 1)

            def head_norm(at, n):
                for h in range(2):
                    pe.wait_ge(at.q_sq, n * 2 + (h + 1))
                    nc.tensor.matmul(score[0][:, hs(h)], head_mean[:], s_sq[:, hs(h)],
                                     start=True, stop=True).then_inc(at.q_ms, 1)

            def flip_v(at, src, n, seen, ready):
                for h in range(2):
                    pe.wait_ge(tile_out[h], ready)
                    if h == 0:
                        pe.wait_ge(at.lo, n)
                    else:
                        pe.wait_ge(at.v_lo, seen)
                    for b in range(4):
                        last = nc.tensor.transpose(flip[:, b * P:(b + 1) * P],
                                                   src[:, (4 * h + b) * P:(4 * h + b + 1) * P], ident[:])
                    last.then_inc(at.v_flip, 1)

            def attention(at, plan, q_hi, q_lo, k_hi, k_lo, v, prob, pt_hi, pt_lo, st, ch, gr):
                steps, chunks, ends = plan

                def scores(s):
                    hh, qb, k0, w = steps[s]
                    rows = slice(hh * DH, (hh + 1) * DH)
                    q = slice(qb * P, (qb + 1) * P)
                    if s >= 2:
                        pe.wait_ge(at.exp if at is sw else at.max, st + (s - 1))
                    for c in range(0, w, HALF):
                        n = min(HALF, w - c)
                        ks = slice(k0 + c, k0 + c + n)
                        dst = score[s % 2][:, c:c + n]
                        last = c + n == w
                        nc.tensor.matmul(dst, q_hi[rows, q], k_hi[rows, ks], start=True, stop=False)
                        nc.tensor.matmul(dst, q_hi[rows, q], k_lo[rows, ks], start=False, stop=False)
                        if last:
                            m = min(w, 2 * P) if at is sw else P
                            nc.tensor.matmul(score[s % 2][:, w - m:w], ident_r[:], mask_r[:, 2 * P - m:2 * P],
                                             start=False, stop=False)
                        mm = nc.tensor.matmul(dst, q_lo[rows, q], k_hi[rows, ks], start=False, stop=True)
                    mm.then_inc(at.scored, 1)

                def values(n):
                    s, c, w, first, last = chunks[n]
                    hh, qb, k0, wide = steps[s]
                    pe.wait_ge(at.lo, ch + (n + 1))
                    if first and s % 4 == 0:
                        pe.wait_ge(at.o, gr + s // 4)
                    for b in range(w // P):
                        blk = (k0 + c) // P + b
                        for pt in (pt_hi, pt_lo):
                            mm = nc.tensor.matmul(pv[:, (s % 4) * P:(s % 4 + 1) * P], v[:, blk, hh, :],
                                                  pt[n % 2][:, b * P:(b + 1) * P],
                                                  start=(first and b == 0 and pt is pt_hi),
                                                  stop=(last and b == w // P - 1 and pt is pt_lo))
                    mm.then_inc(at.pv, 1)

                scores(0)
                scores(1)
                for n, (s, c, w, first, last) in enumerate(chunks):
                    if first:
                        pe.wait_ge(at.prob, st + (s + 1))
                    if n:
                        pe.wait_ge(at.lo, ch + n)
                    for b in range(w // P):
                        mm = nc.tensor.transpose(flip[:, b * P:(b + 1) * P],
                                                 prob[s % 2][:, c + b * P:c + (b + 1) * P], ident[:])
                    mm.then_inc(at.flipped, 1)
                    if last and s + 2 < NST:
                        scores(s + 2)
                    if n:
                        values(n - 1)
                values(len(chunks) - 1)

            pe.wait_ge(const_made, 13)
            norm(n0, False)
            pe.wait_ge(n0.lo, KT)
            with pe.Fori(0, KT) as i:
                for c in range(4):
                    tile(i * 4 + c, i * 4 + c, c % 2, a_hi, a_lo)
            pe.wait_ge(conv_lo, 2 * KT)
            with pe.Fori(0, KT) as j:
                for c, (hi, lo) in enumerate(((b_hi, b_lo), (a_hi, a_lo))):
                    tile(j * 2 + (U_MIX + c), j * 2 + (U_MIX + c), c, hi, lo)
            for kv in range(2):
                u0 = U_SWA + kv * SWA_KV
                tile(u0, u0, u0 % 2, a_hi, a_lo)
                tile(u0 + 1, u0 + 1, (u0 + 1) % 2, a_hi, a_lo)
                head_norm(sw, 5 * kv)
                flip_v(sw, s_o, kv * 4 * NCS, 2 * kv + 1, u0 + 2)
                pe.wait_ge(sw.v_lo, 2 * kv + 2)
                with pe.Fori(0, 2) as it:
                    for pp in range(2):
                        u = u0 + 2 + 3 * pp
                        n = 5 * kv + 1 + pp
                        pair = 4 * kv + pp
                        tile(it * 6 + u, it * 6 + u, u % 2, a_hi, a_lo)
                        tile(it * 6 + (u + 1), it * 6 + (u + 1), (u + 1) % 2, a_hi, a_lo)
                        head_norm(sw, it * 2 + n)
                        tile(it * 6 + (u + 2), it * 6 + (u + 2), u % 2, a_hi, a_lo)
                        pe.wait_ge(sw.q_lo, it * 2 + (n + 1))
                        attention(sw, (s_steps, s_chunks, s_ends), sq_hi, sq_lo, sk_hi, sk_lo, sv, (sp0, sp1),
                                  (sph0, sph1), (spl0, spl1), it * (2 * NST) + pair * NST,
                                  it * (2 * NCS) + pair * NCS, it * (2 * NGR) + pair * NGR)
            pe.wait_ge(sw.o_lo, NPAIR)
            with pe.Fori(0, KT // 2) as j:
                for c in range(2):
                    tile(j * 2 + (U_AOUT + c), j * 2 + (U_AOUT + c), (U_AOUT + c) % 2, b_hi, b_lo)
            pe.wait_ge(m_lo, 2 * KT)
            with pe.Fori(0, KT // 2) as j:
                for c in range(2):
                    tile(j * 2 + (U_OUT + c), j * 2 + (U_OUT + c), (U_OUT + c) % 2, a_hi, a_lo)
            pe.wait_ge(x_lo, 2 * KT)
            tile(U_F, U_F, U_F % 2, b_hi, b_lo)
            with pe.Fori(0, NPAIR // 2) as it:
                for pp in range(2):
                    u = U_FOX + 3 * pp
                    for c in range(3):
                        tile(it * 6 + (u + c), it * 6 + (u + c), (u + c) % 2, b_hi, b_lo)
                    flip_v(fx, f_o, it * (2 * NCF) + pp * NCF, it * 4 + (2 * pp + 1), it * 6 + (u + 3))
                    pe.wait_ge(fx.v_lo, it * 4 + (2 * pp + 2))
                    attention(fx, (f_steps, f_chunks, f_ends), fq_hi, fq_lo, fk_hi, fk_lo, fv, (fp0, fp1),
                              (fph0, fph1), (fpl0, fpl1), it * (2 * NST) + pp * NST,
                              it * (2 * NCF) + pp * NCF, it * (2 * NGR) + pp * NGR)
            pe.wait_ge(fx.o_lo, NPAIR)
            with pe.Fori(0, KT // 2) as j:
                for c in range(2):
                    tile(j * 2 + (U_FOUT + c), j * 2 + (U_FOUT + c), (U_FOUT + c) % 2, a_hi, a_lo)
            norm(n1, True)
            pe.wait_ge(n1.lo, KT)

            def up(u, t):
                for c in range(4):
                    tile(u + c, t + c, (U_FFN + c) % 2, b_hi, b_lo)

            def down(u, t, group_parity, seen):
                pe.wait_ge(up_lo, seen)
                for q in range(2):
                    quarter_tiles(u + q, t + 4 * q, (U_FFN + q) % 2, a_hi, a_lo, (2 * group_parity, 2 * group_parity + 1))

            up(U_FFN, T_FFN)
            with pe.Fori(0, (NGRP - 1) // 2) as it:
                for g in range(2):
                    u, t = U_FFN + 4 + 6 * g, T_FFN + 4 + 12 * g
                    up(it * 12 + u, it * 24 + t)
                    down(it * 12 + (u + 4), it * 24 + (t + 4), g, it * 8 + 4 * (g + 1))
            down(U_PLE - 2, T_PLE - 8, (NGRP - 1) % 2, 4 * NGRP)
            pe.wait_ge(ple_lo, PLE_KT)
            for q in range(2):
                quarter_tiles(U_PLE + q, T_PLE + 4 * q, (U_PLE + q) % 2, p_hi, p_lo, range(PLE_KT))
            norm(n2, True)
            pe.wait_ge(n2.lo, KT)
            for j in range(KT):
                tile(U_GATE + j, T_GATE + j, (U_GATE + j) % 2, a_hi, a_lo)

        @block.scalar
        def _(act):
            settle = settler(act)

            act.dma_start(cst[:], cols).then_inc(cols_in, 16)
            for j in range(KT):
                act.dma_start(z[:, j, :], xT[j, :, :]).then_inc(n0.x_in, 16)

            def norm(ns, mean, hi, bias):
                for j in range(KT):
                    if mean:
                        act.wait_ge(ns.centred, j + 1)
                    elif j == 0:
                        act.wait_ge(ns.x_in, 16 * KT)
                    if j >= 2:
                        act.wait_ge(ns.sq_used, j - 1)
                    nc.scalar.activation(sq[j % 2][:], z[:, j, :], ACT.Square).then_inc(ns.sq, 1)
                act.wait_ge(ns.sq_used, KT)
                act.wait_ge(cols_in, 16)
                act.wait_ge(const_made, 13)
                nc.scalar.activation(nrm[:], score[1][:], ACT.Sqrt, bias=eps_ln[:] if mean else eps_rms[:]).then_inc(ns.std, 1)
                for j in range(KT):
                    act.wait_ge(ns.y, j + 1)
                    if bias is not None:
                        nc.scalar.activation(z[:, j, :], z[:, j, :], ACT.Identity, bias=col(bias + j)).then_inc(ns.yb, 1)
                        act.wait_ge(ns.yb, j + 1)
                    nc.scalar.activation(hi[:, j, :], z[:, j, :], ACT.Copy).then_inc(ns.hi, 1)

            def copy_tile(dst, t):
                for h in range(2):
                    act.wait_ge(tile_done[h], t + 1)
                    nc.scalar.activation(dst[:, hs(h)], bank[h][:], ACT.Copy).then_inc(tile_out[h], 1)

            def v_hi(at, v, n):
                for h in range(2):
                    act.wait_ge(at.v_flip, n + (h + 1))
                    nc.scalar.activation(v[:, 4 * h:4 * h + 4, :, 0:DH],
                                         flip[:].rearrange("p (b h d) -> p b h d", h=2, d=DH), ACT.Copy).then_inc(at.v_hi, 1)

            def attention(at, plan, prob, pt_hi, fold, st, ch, gr, pair):
                steps, chunks, ends = plan

                def expo(s):
                    hh, qb, k0, w = steps[s]
                    act.wait_ge(at.flipped, ch + (ends[s - 2] if s >= 2 else 0))
                    act.wait_ge(at.neg_max, st + (s + 1))
                    src = score[s % 2] if at is sw else prob[s % 2]
                    nc.scalar.activation(prob[s % 2][:, 0:w], src[:, 0:w], ACT.Exp, bias=neg_max[:, s % 2:s % 2 + 1],
                                         scale=SCALE if at is sw else 1.0,
                                         accum_out=row_sum[:, s % 2:s % 2 + 1]).then_inc(at.exp, 1)
                    if at is sw:
                        settle()
                        nc.scalar.activation(sink_exp[:, s % 2:s % 2 + 1], neg_max[:, s % 2:s % 2 + 1], ACT.Exp,
                                             bias=col(pair * 2 + (C_SINK + hh))).then_inc(at.sink, 1)

                def normalise(s):
                    w = steps[s][3]
                    act.wait_ge(at.inv, st + (s + 1))
                    nc.scalar.activation(prob[s % 2][:, 0:w], prob[s % 2][:, 0:w], ACT.Copy,
                                         scale=row_inv[:, s % 2:s % 2 + 1]).then_inc(at.prob, 1)

                def high(n):
                    s, c, w, first, last = chunks[n]
                    if n >= 2:
                        act.wait_ge(at.pv, ch + (n - 1))
                    act.wait_ge(at.flipped, ch + (n + 1))
                    nc.scalar.activation(pt_hi[n % 2][:, 0:w], flip[:, 0:w], ACT.Copy).then_inc(at.hi, 1)

                expo(0)
                normalise(0)
                for s in range(NST):
                    mine = range(ends[s - 1] if s else 0, ends[s])
                    if s + 1 < NST:
                        expo(s + 1)
                    high(mine[0])
                    if s + 1 < NST:
                        normalise(s + 1)
                    for n in mine[1:]:
                        high(n)
                    if s % 4 == 3:
                        g = s // 4
                        act.wait_ge(at.o, gr + g)
                        act.wait_ge(at.pv, ch + ends[s])
                        nc.scalar.activation(fold[0:DH, :], pv[DH:P, :], ACT.Copy).then_inc(at.fold, 1)

            def head_norm(at, n, dst_hi):
                for h in range(2):
                    act.wait_ge(at.q_ms, n * 2 + (h + 1))
                    nc.scalar.activation(s_sq[:, hs(h)], score[0][:, hs(h)], ACT.Sqrt, bias=eps_rms[:]).then_inc(at.q_std, 1)
                act.wait_ge(at.q_n, n + 1)
                nc.scalar.activation(dst_hi[:], s_raw[:], ACT.Copy).then_inc(at.q_hi, 1)

            def raw_and_square(at, t, n):
                for h in range(2):
                    act.wait_ge(tile_done[h], t + 1)
                    nc.scalar.activation(s_raw[:, hs(h)], bank[h][:], ACT.Copy).then_inc(tile_out[h], 1)
                for h in range(2):
                    act.wait_ge(tile_out[h], t + 1)
                    nc.scalar.activation(s_sq[:, hs(h)], s_raw[:, hs(h)], ACT.Square).then_inc(at.q_sq, 1)

            norm(n0, False, a_hi, None)
            with act.Fori(0, KT) as i:
                act.wait_ge(conv_o, i * 2)
                copy_tile(cv_v, i * 4)
                for h in range(2):
                    act.wait_ge(tile_done[h], i * 4 + 4)
                    nc.scalar.activation(cv_g[:, hs(h)], bank[h][:], ACT.Silu).then_inc(tile_out[h], 1)
                for h in range(2):
                    act.wait_ge(conv_o, i * 2 + (h + 1))
                    settle()
                    nc.scalar.activation(b_hi[:, i, hs(h)], cv_o[:, hs(h)], ACT.Copy).then_inc(conv_hi, 1)
            act.wait_ge(conv_lo, 2 * KT)
            with act.Fori(0, KT) as j:
                act.wait_ge(mix_done, j * 2)
                copy_tile(mix_y, j * 2 + U_MIX)
                for h in range(2):
                    act.wait_ge(tile_done[h], j * 2 + (U_MIX + 2))
                    settle()
                    nc.scalar.activation(mix_g[:, hs(h)], bank[h][:], ACT.Sigmoid,
                                         bias=col(j + C_GATEB)).then_inc(tile_out[h], 1)
                act.wait_ge(mix_done, j * 2 + 2)
                act.dma_start(t_scr[j, :, :], mix_t[:]).then_inc(t_stored, 16)
            act.wait_ge(t_stored, 16 * KT)
            for kv in range(2):
                u0 = U_SWA + kv * SWA_KV
                if kv:
                    act.wait_ge(sw.o_lo, 4 * kv)
                raw_and_square(sw, u0, 5 * kv)
                copy_tile(s_o, u0 + 1)
                head_norm(sw, 5 * kv, sk_hi)
                v_hi(sw, sv, 2 * kv)
                with act.Fori(0, 2) as it:
                    for pp in range(2):
                        u = u0 + 2 + 3 * pp
                        n = 5 * kv + 1 + pp
                        pair = 4 * kv + pp
                        act.wait_ge(sw.q_lo, it * 2 + n)
                        raw_and_square(sw, it * 6 + u, it * 2 + n)
                        act.wait_ge(sw.og, it * 2 + pair)
                        for h in range(2):
                            act.wait_ge(tile_done[h], it * 6 + (u + 2))
                            nc.scalar.activation(s_z[:, hs(h)], bank[h][:], ACT.Silu).then_inc(tile_out[h], 1)
                        head_norm(sw, it * 2 + n, sq_hi)
                        act.wait_ge(sw.g_out, it * 32 + pair * 16)
                        for h in range(2):
                            act.wait_ge(tile_done[h], it * 6 + (u + 3))
                            settle()
                            nc.scalar.activation(s_g[:, hs(h)], bank[h][:], ACT.Sigmoid,
                                                 bias=col(it * 2 + (C_GATEB + KT + pair))).then_inc(tile_out[h], 1)
                        for h in range(2):
                            act.wait_ge(tile_out[h], it * 6 + (u + 3))
                        act.dma_start(g_scr[it * 2 + pair, :, :], s_g[:]).then_inc(sw.g_out, 16)
                        attention(sw, (s_steps, s_chunks, s_ends), (sp0, sp1), (sph0, sph1), s_fold,
                                  it * (2 * NST) + pair * NST, it * (2 * NCS) + pair * NCS,
                                  it * (2 * NGR) + pair * NGR, it * 2 + pair)
                        act.wait_ge(sw.og, it * 2 + (pair + 1))
                        settle()
                        nc.scalar.activation(b_hi[:, it * 2 + pair, :], s_o[:], ACT.Copy).then_inc(sw.o_hi, 1)
            act.wait_ge(sw.g_out, 16 * NPAIR)
            act.wait_ge(sw.o_lo, NPAIR)
            m_t, m_g = (m_t0, m_t1), (m_g0, m_g1)
            for s in range(2):
                act.dma_start(m_t[s][:], t_scr[s, :, :]).then_inc(mt_in[s], 16)
                act.dma_start(m_g[s][:], g_scr[s, :, :]).then_inc(mg_in[s], 16)

            def merged_hi(j):
                for h in range(2):
                    act.wait_ge(m_sum, j * 2 + (h + 1))
                    settle()
                    nc.scalar.activation(a_hi[:, j, hs(h)], m_m[:, hs(h)], ACT.Copy).then_inc(m_hi, 1)

            with act.Fori(0, KT // 2 - 1) as it:
                for c in range(2):
                    merged_hi(it * 2 + c)
                    act.dma_start(m_t[c][:], t_scr[it * 2 + (2 + c), :, :]).then_inc(mt_in[c], 16)
                    act.dma_start(m_g[c][:], g_scr[it * 2 + (2 + c), :, :]).then_inc(mg_in[c], 16)
            for j in (KT - 2, KT - 1):
                merged_hi(j)
            x_ins = (x_in0, x_in1)
            for s in range(2):
                act.dma_start(x_ins[s][:], xT[s, :, :]).then_inc(x_in[s], 16)

            def layer_hi(j):
                for h in range(2):
                    act.wait_ge(tile_out[h], j + (U_OUT + 1))
                    settle()
                    nc.scalar.activation(b_hi[:, j, hs(h)], x_sum[:, hs(h)], ACT.Copy).then_inc(x_hi, 1)

            with act.Fori(0, KT // 2 - 1) as it:
                for c in range(2):
                    layer_hi(it * 2 + c)
                    act.dma_start(x_ins[c][:], xT[it * 2 + (2 + c), :, :]).then_inc(x_in[c], 16)
            for j in (KT - 2, KT - 1):
                layer_hi(j)
            act.wait_ge(x_lo, 2 * KT)
            for h in range(2):
                act.wait_ge(tile_done[h], U_F + 1)
                nc.scalar.activation(fp0[0:16, hs(h)], bank[h][0:16, :], ACT.Identity,
                                     bias=cst[0:16, C_BF:C_BF + 1]).then_inc(tile_out[h], 1)
            for h in range(2):
                act.wait_ge(tile_out[h], U_F + 1)
            nc.scalar.activation(fp1[0:16, :], fp0[0:16, :], ACT.Abs).then_inc(f_step, 1)
            act.wait_ge(f_step, 1)
            nc.scalar.activation(fp1[0:16, :], fp1[0:16, :], ACT.Exp, scale=-1.0).then_inc(f_step, 1)
            act.wait_ge(f_step, 2)
            nc.scalar.activation(fp1[0:16, :], fp1[0:16, :], ACT.Ln, bias=1.0).then_inc(f_step, 1)
            act.wait_ge(f_step, 6)
            act.dma_start(c_scr, fp1[0:16, :]).then_inc(c_stored, 16)
            act.wait_ge(c_stored, 16)
            with act.Fori(0, NPAIR // 2) as it:
                for pp in range(2):
                    u = U_FOX + 3 * pp
                    act.wait_ge(fx.max, it * (2 * NST) + pp * NST)
                    for hh, dst in enumerate((fc0, fc1)):
                        act.dma_start(dst[:], c_scr[bass.ds(it * 4 + (2 * pp + hh), 1), :].partition_broadcast(P)).then_inc(fx.c_in, 16)
                    for c, dst in enumerate((fq_hi, fk_hi)):
                        for h in range(2):
                            act.wait_ge(tile_done[h], it * 6 + (u + c + 1))
                            nc.scalar.activation(dst[:, hs(h)], bank[h][:], ACT.Copy).then_inc(fx.q_hi, 1)
                    act.wait_ge(fx.o_lo, it * 2 + pp)
                    copy_tile(f_o, it * 6 + (u + 2))
                    v_hi(fx, fv, it * 4 + 2 * pp)
                    attention(fx, (f_steps, f_chunks, f_ends), (fp0, fp1), (fph0, fph1), f_fold,
                              it * (2 * NST) + pp * NST, it * (2 * NCF) + pp * NCF, it * (2 * NGR) + pp * NGR, None)
                    act.wait_ge(fx.o, it * (2 * NGR) + (pp + 1) * NGR)
                    settle()
                    nc.scalar.activation(a_hi[:, it * 2 + pp, :], f_o[:], ACT.Copy).then_inc(fx.o_hi, 1)
            norm(n1, True, b_hi, C_LN1B)
            act.wait_ge(n1.lo, KT)
            for j in range(KT):
                nc.scalar.activation(z[:, j, :], z[:, j, :], ACT.Copy, scale=ALPHA).then_inc(z_alpha, 1)

            def up(t, n, parity):
                for c in range(2):
                    act.wait_ge(up_prod, (n + c) * 2)
                    copy_tile(up_u, t + 2 * c)
                    for h in range(2):
                        act.wait_ge(tile_done[h], t + (2 * c + 2))
                        nc.scalar.activation(up_g[:, 2 + h * HALF:2 + (h + 1) * HALF], bank[h][:],
                                             ACT.Copy).then_inc(tile_out[h], 1)
                    act.wait_ge(up_conv, (n + c) * 3 + 3)
                    nc.scalar.activation(up_y[:], up_y[:], ACT.Gelu).then_inc(up_gelu, 1)
                    for h in range(2):
                        act.wait_ge(up_prod, (n + c) * 2 + (h + 1))
                        nc.scalar.activation(a_hi[:, 2 * parity + c, hs(h)], up_o[:, hs(h)], ACT.Copy).then_inc(up_hi, 1)

            act.wait_ge(ffn_pad, 1)
            up(T_FFN, 0, 0)
            with act.Fori(0, (NGRP - 1) // 2) as it:
                for g in range(2):
                    up(it * 24 + (T_FFN + 4 + 12 * g), it * 4 + (2 * g + 2), (g + 1) % 2)
            act.wait_ge(up_lo, 2 * FT)
            for k in range(PLE_KT):
                act.dma_start(p_raw[:, k, :], pT[k, :, :]).then_inc(p_in, 16)
            act.wait_ge(p_in, 16 * PLE_KT)
            for k in range(PLE_KT):
                nc.scalar.activation(p_hi[:, k, :], p_raw[:, k, :], ACT.Copy).then_inc(ple_hi, 1)
            for m in range(KT):
                copy_tile(ple[:, m, :], T_PLE + m)
            norm(n2, True, a_hi, C_LN2B)
            for j in range(KT):
                for h in range(2):
                    if j:
                        act.wait_ge(g_done, 2 * j - 1 + h)
                    act.wait_ge(tile_done[h], T_GATE + j + 1)
                    nc.scalar.activation(g_sig[:, hs(h)], bank[h][:], ACT.Sigmoid, bias=col(C_PLEB + j)).then_inc(tile_out[h], 1)
                act.wait_ge(g_sum, 2 * j + 2)
                act.dma_start(out[j, :, :], g_out[:]).then_inc(out_stored, 16)
            act.wait_ge(out_stored, 16 * KT)

        @block.vector
        def _(dve):
            v = nc.vector

            settle = settler(dve)

            def norm(ns, mean, hi, lo, gain):
                if mean:
                    dve.wait_ge(ns.mean, 2)
                    for j in range(KT):
                        v.tensor_tensor(z[:, j, :], z[:, j, :], score[0][:], ALU.subtract).then_inc(ns.centred, 1)
                dve.wait_ge(ns.std, 1)
                v.reciprocal(nrm[:], nrm[:]).then_inc(ns.rstd, 1)
                dve.wait_ge(ns.rstd, 1)

                def scaled(j):
                    if mean:
                        dve.wait_ge(ns.sq, j + 1)
                    v.scalar_tensor_tensor(z[:, j, :], z[:, j, :], col(gain + j), nrm[:], ALU.mult, ALU.mult).then_inc(ns.y, 1)

                scaled(0)
                for j in range(KT):
                    if j + 1 < KT:
                        scaled(j + 1)
                    dve.wait_ge(ns.hi, j + 1)
                    v.tensor_tensor(lo[:, j, :], z[:, j, :], hi[:, j, :].bitcast(F32), ALU.subtract).then_inc(ns.lo, 1)

            def v_lo(at, dst, n):
                for h in range(2):
                    dve.wait_ge(at.v_hi, n + (h + 1))
                    v.tensor_tensor(dst[:, 4 * h:4 * h + 4, :, DH:P], flip[:].rearrange("p (b h d) -> p b h d", h=2, d=DH),
                                    dst[:, 4 * h:4 * h + 4, :, 0:DH].bitcast(F32), ALU.subtract).then_inc(at.v_lo, 1)

            def attention(at, plan, prob, pt_hi, pt_lo, fold, o, bias, st, ch, gr, pair):
                steps, chunks, ends = plan

                def maxima(s):
                    hh, qb, k0, w = steps[s]
                    one = slice(s % 2, s % 2 + 1)
                    if at is sw:
                        dve.wait_ge(at.scored, st + (s + 1))
                        v.reduce_max(mx[:, one], score[s % 2][:, 0:w], AX).then_inc(at.max, 1)
                        dve.wait_ge(at.max, st + (s + 1))
                        v.tensor_scalar(neg_max[:, one], mx[:, one], -SCALE, neg_sink[:, bass.ds(pair * 2 + hh, 1)],
                                        ALU.mult, ALU.min).then_inc(at.neg_max, 1)
                    else:
                        dve.wait_ge(at.flipped, ch + (ends[s - 2] if s >= 2 else 0))
                        dve.wait_ge(at.scored, st + (s + 1))
                        settle()
                        v.tensor_tensor_reduce(out=prob[s % 2][:, 0:w], in0=score[s % 2][:, 0:w], in1=bias[hh][:, 0:w],
                                               scale=SCALE, scalar=-3.0e38, op0=ALU.subtract, op1=ALU.max,
                                               accum_out=mx[:, one]).then_inc(at.max, 1)
                        dve.wait_ge(at.max, st + (s + 1))
                        v.tensor_scalar(neg_max[:, one], mx[:, one], -1.0, None, ALU.mult).then_inc(at.neg_max, 1)

                def inverse(s):
                    one = slice(s % 2, s % 2 + 1)
                    if at is sw:
                        dve.wait_ge(at.sink, st + (s + 1))
                        v.tensor_tensor(row_sum[:, one], row_sum[:, one], sink_exp[:, one], ALU.add).then_inc(at.total, 1)
                        dve.wait_ge(at.total, st + (s + 1))
                    else:
                        dve.wait_ge(at.exp, st + (s + 1))
                    v.reciprocal(row_inv[:, one], row_sum[:, one]).then_inc(at.inv, 1)

                def low(n):
                    s, c, w, first, last = chunks[n]
                    dve.wait_ge(at.hi, ch + (n + 1))
                    v.tensor_tensor(pt_lo[n % 2][:, 0:w], flip[:, 0:w], pt_hi[n % 2][:, 0:w].bitcast(F32),
                                    ALU.subtract).then_inc(at.lo, 1)

                maxima(0)
                inverse(0)
                for s in range(NST):
                    mine = range(ends[s - 1] if s else 0, ends[s])
                    if s + 1 < NST:
                        maxima(s + 1)
                    low(mine[0])
                    if s + 1 < NST:
                        inverse(s + 1)
                    for n in mine[1:]:
                        low(n)
                    if s % 4 == 3:
                        g = s // 4
                        hh = g // 2
                        dve.wait_ge(at.fold, gr + (g + 1))
                        v.tensor_tensor(o[hh * DH:(hh + 1) * DH, hs(g % 2)], pv[0:DH, :], fold[0:DH, :],
                                        ALU.add).then_inc(at.o, 1)

            def head_norm(at, n, gain, hi, lo):
                for h in range(2):
                    dve.wait_ge(at.q_std, n * 2 + (h + 1))
                    v.reciprocal(s_sq[:, hs(h)], s_sq[:, hs(h)]).then_inc(at.q_rstd, 1)
                dve.wait_ge(at.q_rstd, n * 2 + 2)
                v.scalar_tensor_tensor(s_raw[:], s_raw[:], col(gain), s_sq[:], ALU.mult, ALU.mult).then_inc(at.q_n, 1)
                dve.wait_ge(at.q_hi, n + 1)
                v.tensor_tensor(lo[:], s_raw[:], hi[:].bitcast(F32), ALU.subtract).then_inc(at.q_lo, 1)

            dve.wait_ge(cols_in, 16)
            v.tensor_scalar(neg_sink[:], cst[:, C_SINK:C_SINK + 2 * NPAIR], -1.0, None, ALU.mult).then_inc(conv_step, 1)
            norm(n0, False, a_hi, a_lo, C_NORM)
            dve.wait_ge(n0.lo, KT)
            v.memset(cv_u[:, 0:2], 0.0).then_inc(conv_step, 1)
            with dve.Fori(0, KT) as i:
                for h in range(2):
                    dve.wait_ge(tile_out[h], i * 4 + 1)
                    dve.wait_ge(tile_done[h], i * 4 + 2)
                    v.tensor_tensor(cv_u[:, 2 + h * HALF:2 + (h + 1) * HALF], bank[h][:], cv_v[:, hs(h)],
                                    ALU.mult).then_inc(tile_out[h], 1)
                for h in range(2):
                    dve.wait_ge(tile_out[h], i * 4 + 2)
                v.tensor_scalar(cv_y[:], cv_u[:, 0:S], col(i * 3 + C_CONV), None, ALU.mult).then_inc(conv_step, 1)
                for k in (1, 2):
                    dve.wait_ge(conv_step, i * 3 + (2 + k))
                    v.scalar_tensor_tensor(cv_y[:], cv_u[:, k:k + S], col(i * 3 + (C_CONV + k)), cv_y[:], ALU.mult,
                                           ALU.add).then_inc(conv_step, 1)
                dve.wait_ge(conv_step, i * 3 + 5)
                for h in range(2):
                    dve.wait_ge(tile_done[h], i * 4 + 3)
                    v.tensor_tensor(cv_y[:, hs(h)], bank[h][:], cv_y[:, hs(h)], ALU.mult).then_inc(tile_out[h], 1)
                for h in range(2):
                    dve.wait_ge(tile_out[h], i * 4 + 4)
                    v.tensor_tensor(cv_o[:, hs(h)], cv_y[:, hs(h)], cv_g[:, hs(h)], ALU.mult).then_inc(conv_o, 1)
                for h in range(2):
                    dve.wait_ge(conv_hi, i * 2 + (h + 1))
                    v.tensor_tensor(b_lo[:, i, hs(h)], cv_o[:, hs(h)], b_hi[:, i, hs(h)].bitcast(F32),
                                    ALU.subtract).then_inc(conv_lo, 1)
            with dve.Fori(0, KT) as j:
                dve.wait_ge(t_stored, j * 16)
                for h in range(2):
                    dve.wait_ge(tile_out[h], j * 2 + (U_MIX + 2))
                    v.tensor_tensor(mix_t[:, hs(h)], mix_y[:, hs(h)], mix_g[:, hs(h)], ALU.mult).then_inc(mix_done, 1)
            for kv in range(2):
                head_norm(sw, 5 * kv, C_KG, sk_hi, sk_lo)
                v_lo(sw, sv, 2 * kv)
                with dve.Fori(0, 2) as it:
                    for pp in range(2):
                        u = U_SWA + kv * SWA_KV + 2 + 3 * pp
                        n = 5 * kv + 1 + pp
                        pair = 4 * kv + pp
                        head_norm(sw, it * 2 + n, C_QG, sq_hi, sq_lo)
                        attention(sw, (s_steps, s_chunks, s_ends), (sp0, sp1), (sph0, sph1), (spl0, spl1), s_fold, s_o,
                                  None, it * (2 * NST) + pair * NST, it * (2 * NCS) + pair * NCS,
                                  it * (2 * NGR) + pair * NGR, it * 2 + pair)
                        dve.wait_ge(sw.o, it * (2 * NGR) + (pair + 1) * NGR)
                        for h in range(2):
                            dve.wait_ge(tile_out[h], it * 6 + (u + 2))
                        v.tensor_tensor(s_o[:], s_o[:], s_z[:], ALU.mult).then_inc(sw.og, 1)
                        dve.wait_ge(sw.o_hi, it * 2 + (pair + 1))
                        v.tensor_tensor(b_lo[:, it * 2 + pair, :], s_o[:], b_hi[:, it * 2 + pair, :].bitcast(F32),
                                        ALU.subtract).then_inc(sw.o_lo, 1)
            m_t, m_g = (m_t0, m_t1), (m_g0, m_g1)
            with dve.Fori(0, KT // 2) as it:
                for c in range(2):
                    dve.wait_ge(mg_in[c], it * 16 + 16)
                    dve.wait_ge(mt_in[c], it * 16 + 16)
                    dve.wait_ge(m_lo, it * 4 + 2 * c)
                    for h in range(2):
                        dve.wait_ge(tile_done[h], it * 2 + (U_AOUT + c + 1))
                        v.tensor_tensor(m_m[:, hs(h)], bank[h][:], m_g[c][:, hs(h)], ALU.mult).then_inc(tile_out[h], 1)
                    for h in range(2):
                        dve.wait_ge(tile_out[h], it * 2 + (U_AOUT + c + 1))
                        v.tensor_tensor(m_m[:, hs(h)], m_m[:, hs(h)], m_t[c][:, hs(h)], ALU.add).then_inc(m_sum, 1)
                    for h in range(2):
                        dve.wait_ge(m_hi, it * 4 + (2 * c + h + 1))
                        v.tensor_tensor(a_lo[:, it * 2 + c, hs(h)], m_m[:, hs(h)], a_hi[:, it * 2 + c, hs(h)].bitcast(F32),
                                        ALU.subtract).then_inc(m_lo, 1)
            x_ins = (x_in0, x_in1)
            with dve.Fori(0, KT // 2) as it:
                for c in range(2):
                    dve.wait_ge(x_in[c], it * 16 + 16)
                    dve.wait_ge(x_lo, it * 4 + 2 * c)
                    for h in range(2):
                        dve.wait_ge(tile_done[h], it * 2 + (U_OUT + c + 1))
                        v.tensor_tensor(x_sum[:, hs(h)], bank[h][:], x_ins[c][:, hs(h)], ALU.add).then_inc(tile_out[h], 1)
                    for h in range(2):
                        dve.wait_ge(x_hi, it * 4 + (2 * c + h + 1))
                        v.tensor_tensor(b_lo[:, it * 2 + c, hs(h)], x_sum[:, hs(h)], b_hi[:, it * 2 + c, hs(h)].bitcast(F32),
                                        ALU.subtract).then_inc(x_lo, 1)
            dve.wait_ge(f_step, 3)
            v.tensor_scalar(fp0[0:16, :], fp0[0:16, :], 0.0, None, ALU.min).then_inc(f_step, 1)
            dve.wait_ge(f_step, 4)
            v.tensor_tensor_scan(fp0[0:16, :], fp0[0:16, :], fp1[0:16, :], 0.0, ALU.add, ALU.subtract).then_inc(f_step, 1)
            dve.wait_ge(f_step, 5)
            v.tensor_scalar(fp1[0:16, :], fp0[0:16, :], 1.0 / SCALE, None, ALU.mult).then_inc(f_step, 1)
            dve.wait_ge(c_stored, 16)
            with dve.Fori(0, NPAIR // 2) as it:
                for pp in range(2):
                    u = U_FOX + 3 * pp
                    for c, (hi, lo) in enumerate(((fq_hi, fq_lo), (fk_hi, fk_lo))):
                        for h in range(2):
                            dve.wait_ge(fx.q_hi, it * 8 + (4 * pp + 2 * c + h + 1))
                            v.tensor_tensor(lo[:, hs(h)], bank[h][:], hi[:, hs(h)].bitcast(F32),
                                            ALU.subtract).then_inc(tile_out[h], 1)
                    for h in range(2):
                        dve.wait_ge(tile_out[h], it * 6 + (u + 2))
                    v_lo(fx, fv, it * 4 + 2 * pp)
                    dve.wait_ge(fx.c_in, it * 64 + (32 * pp + 32))
                    attention(fx, (f_steps, f_chunks, f_ends), (fp0, fp1), (fph0, fph1), (fpl0, fpl1), f_fold, f_o,
                              (fc0, fc1), it * (2 * NST) + pp * NST, it * (2 * NCF) + pp * NCF,
                              it * (2 * NGR) + pp * NGR, None)
                    dve.wait_ge(fx.o_hi, it * 2 + (pp + 1))
                    v.tensor_tensor(a_lo[:, it * 2 + pp, :], f_o[:], a_hi[:, it * 2 + pp, :].bitcast(F32),
                                    ALU.subtract).then_inc(fx.o_lo, 1)
            dve.wait_ge(fx.o_lo, NPAIR)
            v.memset(acc[:], 0.0).then_inc(z_part, 1)

            with dve.Fori(0, KT) as j:
                for h in range(2):
                    dve.wait_ge(tile_done[h], j + (U_FOUT + 1))
                    v.scalar_tensor_tensor(z[:, j, hs(h)], b_hi[:, j, hs(h)].bitcast(F32), ALPHA, bank[h][:], ALU.mult,
                                           ALU.add).then_inc(tile_out[h], 1)
                for h in range(2):
                    dve.wait_ge(tile_out[h], j + (U_FOUT + 1))
                    v.scalar_tensor_tensor(z[:, j, hs(h)], b_lo[:, j, hs(h)].bitcast(F32), ALPHA, z[:, j, hs(h)], ALU.mult,
                                           ALU.add).then_inc(z_part, 1)
                for h in range(2):
                    dve.wait_ge(z_part, j * 2 + (h + 2))
                    v.tensor_tensor(acc[:, hs(h)], acc[:, hs(h)], z[:, j, hs(h)], ALU.add).then_inc(n1.acc, 1)
                dve.wait_ge(n1.acc, j * 2 + 2)
            norm(n1, True, b_hi, b_lo, C_LN1G)

            def up(t, n, parity):
                for c in range(2):
                    f = n + c
                    for h in range(2):
                        dve.wait_ge(tile_out[h], t + (2 * c + 2))
                    v.tensor_scalar(up_y[:], up_g[:, 0:S], col(f * 3 + C_FCW), col(f + C_FCB), ALU.mult,
                                    ALU.add).then_inc(up_conv, 1)
                    for k in (1, 2):
                        dve.wait_ge(up_conv, f * 3 + k)
                        v.scalar_tensor_tensor(up_y[:], up_g[:, k:k + S], col(f * 3 + (C_FCW + k)), up_y[:], ALU.mult,
                                               ALU.add).then_inc(up_conv, 1)
                    dve.wait_ge(up_gelu, f + 1)
                    for h in range(2):
                        v.tensor_tensor(up_o[:, hs(h)], up_y[:, hs(h)], up_u[:, hs(h)], ALU.mult).then_inc(up_prod, 1)
                    for h in range(2):
                        dve.wait_ge(up_hi, f * 2 + (h + 1))
                        v.tensor_tensor(a_lo[:, 2 * parity + c, hs(h)], up_o[:, hs(h)],
                                        a_hi[:, 2 * parity + c, hs(h)].bitcast(F32), ALU.subtract).then_inc(up_lo, 1)

            def down(t, sums=None):
                for m in range(KT):
                    for h in range(2):
                        dve.wait_ge(tile_done[h], t + (m + 1))
                        v.tensor_tensor(z[:, m, hs(h)], z[:, m, hs(h)], bank[h][:], ALU.add).then_inc(tile_out[h], 1)
                    if sums is not None:
                        for h in range(2):
                            dve.wait_ge(tile_out[h], t + (m + 1))
                            if m:
                                dve.wait_ge(sums, 2 * m)
                                v.tensor_tensor(acc[:, hs(h)], acc[:, hs(h)], z[:, m, hs(h)], ALU.add).then_inc(sums, 1)
                            else:
                                v.tensor_copy(acc[:, hs(h)], z[:, m, hs(h)]).then_inc(sums, 1)

            dve.wait_ge(n1.lo, KT)
            v.memset(up_g[:, 0:2], 0.0).then_inc(ffn_pad, 1)
            up(T_FFN, 0, 0)
            dve.wait_ge(z_alpha, KT)
            with dve.Fori(0, (NGRP - 1) // 2) as it:
                for g in range(2):
                    t = T_FFN + 4 + 12 * g
                    up(it * 24 + t, it * 4 + (2 * g + 2), (g + 1) % 2)
                    down(it * 24 + (t + 4))
            dve.wait_ge(up_lo, 2 * FT)
            down(T_PLE - KT, n2.acc)
            for k in range(PLE_KT):
                dve.wait_ge(ple_hi, k + 1)
                v.tensor_tensor(p_lo[:, k, :], p_raw[:, k, :], p_hi[:, k, :].bitcast(F32), ALU.subtract).then_inc(ple_lo, 1)
            norm(n2, True, a_hi, a_lo, C_LN2G)
            for j in range(KT):
                if j:
                    dve.wait_ge(out_stored, 16 * j)
                for h in range(2):
                    dve.wait_ge(tile_out[h], T_GATE + j + 1)
                    v.tensor_tensor(g_out[:, hs(h)], ple[:, j, hs(h)], g_sig[:, hs(h)], ALU.mult).then_inc(g_done, 1)
                for h in range(2):
                    dve.wait_ge(g_done, 2 * j + h + 1)
                    v.tensor_tensor(g_out[:, hs(h)], g_out[:, hs(h)], z[:, j, hs(h)], ALU.add).then_inc(g_sum, 1)


def lay_out(a):
    a = {k: np.asarray(v) for k, v in a.items()}

    def units(w):
        n = w.shape[1] // P
        return w.reshape(KT, P, n, P).transpose(2, 1, 0, 3).reshape(n, P, KT * P)

    def quarters(w):
        return w.reshape(2, P, 2, 4, P).transpose(2, 1, 3, 0, 4).reshape(2, P, KT * P)

    order = [h for p in range(NPAIR) for h in (8 * (p // 4) + p % 4, 8 * (p // 4) + 4 + p % 4)]
    by_pair = np.concatenate([np.arange(h * DH, (h + 1) * DH) for h in order])

    w_in, conv_out, attn_out, w_out = (a[k][0] for k in ("w_in", "w_conv_out", "w_attn_out", "w_out"))
    kv = P * 2
    at = np.cumsum([0, D, D, D, D, D, kv, kv, D, D, D])
    v_c, b_c, c_c, z_c, q, k, v, z_a, g_a, g_b = (w_in[:, at[i]:at[i + 1]] for i in range(10))
    v_c, b_c, c_c, z_c, g_a, g_b, k, v = (units(w) for w in (v_c, b_c, c_c, z_c, g_a, g_b, k, v))
    q, z_a = units(q[:, by_pair]), units(z_a[:, by_pair])
    conv_out, attn_out, w_out = units(conv_out), units(attn_out[by_pair]), units(w_out)
    seq = []
    for i in range(KT):
        seq += [v_c[i], c_c[i], b_c[i], z_c[i]]
    for i in range(KT):
        seq += [conv_out[i], g_a[i]]
    for t in range(2):
        seq += [k[t], v[t]]
        for p in range(4 * t, 4 * t + 4):
            seq += [q[p], z_a[p], g_b[p]]
    seq += [*attn_out, *w_out]
    w2 = a["attn_w_in_2"][0]
    seq += [*units(np.pad(w2[:, 3 * D:], ((0, 0), (0, P - 2 * NPAIR))))]
    fq, fk, fv = (units(w2[:, i * D:(i + 1) * D]) for i in range(3))
    for p in range(NPAIR):
        seq += [fq[p], fk[p], fv[p]]
    seq += [*units(a["attn_w_out_2"][0])]
    w_up, w_down = a["ffn_w_up_2"][0], a["ffn_w_down_2"][0]
    u, g = units(w_up[:, :FFN]), units(w_up[:, FFN:])
    down = [quarters(w_down[n * 2 * P:(n + 1) * 2 * P]) for n in range(NGRP)]
    for n in range(NGRP):
        seq += [u[2 * n], g[2 * n], u[2 * n + 1], g[2 * n + 1]]
        if n:
            seq += [*down[n - 1]]
    seq += [*down[-1], *quarters(a["ple_w_proj_2"][0]), *units(a["ple_w_gate_2"][0])]
    weights = np.stack(seq)
    assert weights.shape[0] == U_END

    def columns(vec):
        return vec.reshape(-1, P).T

    def taps(w):
        return w.reshape(3, -1, P).transpose(2, 1, 0).reshape(P, -1)

    cols = np.concatenate([
        columns(a["norm_g"][0]), taps(a["conv_w"][0]), columns(np.tile(a["q_norm_g"][0], 2)),
        columns(np.tile(a["k_norm_g"][0], 2)), columns(a["gate_b"][0]), taps(a["ffn_conv_w_2"][0]),
        columns(a["ffn_conv_b_2"][0]), columns(a["ln_mix_g_2"][0]), columns(a["ln_mix_b_2"][0]),
        columns(a["ln_ffn_g_2"][0]), columns(a["ln_ffn_b_2"][0]), columns(a["ple_b_gate_2"][0]),
        columns(np.pad(a["attn_b_f_2"][0], (0, P - 2 * NPAIR))), np.tile(a["sinks"][0][order], (P, 1))], axis=1)
    assert cols.shape == (P, N_COLS)

    def feature_major(x):
        return np.ascontiguousarray(x.T.reshape(-1, P, S))

    return {"in_x": feature_major(a["x"][0]), "in_w": weights, "in_cols": np.ascontiguousarray(cols),
            "in_p": feature_major(a["p_2"][0, 0])}


def kernel(**inputs):
    import concourse.bacc as _bacc
    from concourse import mybir as _mybir
    from concourse.bass_utils import run_bass_kernel_spmd as _run

    arrays = lay_out(inputs)
    nc = _bacc.Bacc("TRN2", target_bir_lowering=False, num_devices=1)
    f32 = _mybir.dt.float32
    ins = {k: nc.dram_tensor(k, a.shape, f32, kind="ExternalInput").ap() for k, a in arrays.items()}
    out = nc.dram_tensor("out_y", (KT, P, S), f32, kind="ExternalOutput").ap()
    t_scr = nc.dram_tensor("t_scr", (KT, P, S), f32, kind="Internal").ap()
    g_scr = nc.dram_tensor("g_scr", (KT, P, S), f32, kind="Internal").ap()
    c_scr = nc.dram_tensor("c_scr", (2 * NPAIR, S), f32, kind="Internal").ap()
    build(nc, ins["in_x"], ins["in_w"], ins["in_cols"], ins["in_p"], out, t_scr, g_scr, c_scr)
    r = _run(nc, [arrays], core_ids=[0])
    return np.ascontiguousarray(r.results[0]["out_y"].reshape(D, S).T).reshape(1, S, D)
```

```python
from contextlib import ExitStack

import numpy as np
import concourse.bass as bass
import concourse.mybir as mybir

F32 = mybir.dt.float32
F32R = mybir.dt.float32r
ALU = mybir.AluOpType
ACT = mybir.ActivationFunctionType
AX = mybir.AxisListType.X

P = 128
D = 1024
S = 1024
KT = D // P
HALF = 512
DH = 64
NPAIR = 8
NB = S // P
FFN = 2816
FT = FFN // P
NGRP = FT // 2
PLE_KT = 2
NEG = -1e30
SCALE = DH ** -0.5
ALPHA = 2.0 ** 0.25
RMS_EPS, LN_EPS = 1e-6, 1e-5

U_CONV = 0
U_MIX = U_CONV + 4 * KT
U_SWA = U_MIX + 2 * KT
U_PAIR = U_SWA + 5
U_AOUT = U_PAIR + 3 * NPAIR - 1
U_OUT = U_AOUT + KT
U_F = U_OUT + KT
U_FOX = U_F + 1
U_FOUT = U_FOX + 3 * NPAIR
U_FFN = U_FOUT + KT
U_PLE = U_FFN + 6 * NGRP
U_GATE = U_PLE + 2
U_END = U_GATE + KT
T_FFN = U_FFN
T_PLE = T_FFN + 12 * NGRP
T_GATE = T_PLE + KT
T_END = T_GATE + KT
O_PLE = T_FFN + 4 * NGRP
O_GATE = O_PLE + KT

C_NORM = 0
C_CONV = C_NORM + KT
C_QG = C_CONV + 3 * KT
C_KG = C_QG + 1
C_GATEB = C_KG + 1
C_FCW = C_GATEB + 2 * KT
C_FCB = C_FCW + 3 * FT
C_LN1G = C_FCB + FT
C_LN1B = C_LN1G + KT
C_LN2G = C_LN1B + KT
C_LN2B = C_LN2G + KT
C_PLEB = C_LN2B + KT
C_BF = C_PLEB + KT
C_SINK = C_BF + 1
N_COLS = C_SINK + 2 * NPAIR


class NormSemaphores:

    def __init__(self, sem, n):
        self.x_in = sem(n + "_x_in")
        self.acc = sem(n + "_acc")
        self.mean = sem(n + "_mean")
        self.centred = sem(n + "_centred")
        self.sq = sem(n + "_sq")
        self.sq_used = sem(n + "_sq_used")
        self.std = sem(n + "_std")
        self.rstd = sem(n + "_rstd")
        self.y = sem(n + "_y")
        self.yb = sem(n + "_yb")
        self.hi = sem(n + "_hi")
        self.lo = sem(n + "_lo")


class AttentionSemaphores:

    def __init__(self, sem, n):
        self.q_sq = sem(n + "_q_sq")
        self.q_ms = sem(n + "_q_ms")
        self.q_std = sem(n + "_q_std")
        self.q_rstd = sem(n + "_q_rstd")
        self.q_n = sem(n + "_q_n")
        self.q_hi = sem(n + "_q_hi")
        self.q_lo = sem(n + "_q_lo")
        self.v_flip = sem(n + "_v_flip")
        self.v_hi = sem(n + "_v_hi")
        self.v_lo = sem(n + "_v_lo")
        self.scored = sem(n + "_scored")
        self.max = sem(n + "_max")
        self.neg_max = sem(n + "_neg_max")
        self.exp = sem(n + "_exp")
        self.sink = sem(n + "_sink")
        self.total = sem(n + "_total")
        self.inv = sem(n + "_inv")
        self.prob = sem(n + "_prob")
        self.flipped = sem(n + "_flipped")
        self.hi = sem(n + "_hi")
        self.lo = sem(n + "_lo")
        self.pv = sem(n + "_pv")
        self.fold = sem(n + "_fold")
        self.o = sem(n + "_o")
        self.og = sem(n + "_og")
        self.o_hi = sem(n + "_o_hi")
        self.o_lo = sem(n + "_o_lo")
        self.g_out = sem(n + "_g_out")


STEPS = [(hh, qb) for hh in range(2) for qb in range(NB)]
NST = len(STEPS)
CHUNKS = [(s, b, min(4, qb + 1 - b)) for s, (hh, qb) in enumerate(STEPS) for b in range(0, qb + 1, 4)]
NCH = len(CHUNKS)
CHUNKS_OF = [[n for n, c in enumerate(CHUNKS) if c[0] == s] for s in range(NST)]
WSTEPS = [(hh, g) for hh in range(2) for g in range(2)]
NW = len(WSTEPS)


def build(nc, xT, weights, cols, pT, out, t_scr, g_scr, c_scr):
    ctx = ExitStack()
    with ctx:
        top = [0]
        base = -(-nc.sbuf_base // 32) * 32

        def fixed(name, shape, dt):
            n = int(np.prod(shape[1:])) * 4
            t = nc.alloc_sbuf_tensor_at(name, [P, *shape[1:]], dt, offset=base + top[0])
            top[0] += -(-n // 32) * 32
            return t

        total = 207 * 1024 + 512

        raw = [fixed(f"raw{b}", [P, HALF], F32) for b in range(2)]
        whi = [fixed(f"whi{s}", [P, KT, P], F32R) for s in range(2)]
        wlo = [fixed(f"wlo{s}", [P, KT, P], F32R) for s in range(2)]
        ident = fixed("ident", [P, P], F32)
        ident_r = fixed("ident_r", [P, P], F32R)
        mask_r = fixed("mask_r", [P, 3 * P], F32R)
        head_mean = fixed("head_mean", [P, P], F32)
        feat_mean = fixed("feat_mean", [P, P], F32)
        cst = fixed("cst", [P, N_COLS], F32)
        eps_rms = fixed("eps_rms", [P, 1], F32)
        eps_ln = fixed("eps_ln", [P, 1], F32)
        neg_sink = fixed("neg_sink", [P, 2 * NPAIR], F32)
        mx = fixed("mx", [P, 8], F32)
        neg_max = fixed("neg_max", [P, 8], F32)
        row_sum = fixed("row_sum", [P, 8], F32)
        sink_exp = fixed("sink_exp", [P, 8], F32)
        row_inv = fixed("row_inv", [P, 8], F32)
        a_hi_at = top[0]
        a_hi = fixed("a_hi", [P, KT, S], F32R)
        a_lo_at = top[0]
        a_lo = fixed("a_lo", [P, KT, S], F32R)
        b_hi_at = top[0]
        b_hi = fixed("b_hi", [P, KT, S], F32R)
        b_lo_at = top[0]
        b_lo = fixed("b_lo", [P, KT, S], F32R)
        over_at = top[0]

        def overlay(at, *specs):
            top[0] = at
            made = [fixed(*x) for x in specs]
            assert top[0] <= total, (top[0], total)
            return made

        z, sq0, sq1, nrm, acc = overlay(over_at, ("z", [P, KT, S], F32), ("sq0", [P, S], F32), ("sq1", [P, S], F32),
                                        ("nrm", [P, S], F32), ("acc", [P, S], F32))
        sq = [sq0, sq1]
        (mask_f,) = overlay(b_hi_at, ("mask_f", [P, 3 * P], F32))
        cv_v, cv_u, cv_y, cv_g, cv_o = overlay(over_at, ("cv_v", [P, S], F32), ("cv_u", [P, S + 2], F32),
                                               ("cv_y", [P, S], F32), ("cv_g", [P, S], F32), ("cv_o", [P, S], F32))
        mix_y, mix_g, mix_t = overlay(over_at, ("mix_y", [P, S], F32), ("mix_g", [P, S], F32), ("mix_t", [P, S], F32))
        sk_hi0, sk_hi1, sk_lo0, sk_lo1, sv0, sv1 = overlay(
            b_lo_at, *((f"sk_{x}{t}", [P, S], F32R) for x in ("hi", "lo") for t in range(2)),
            ("sv0", [P, NB, 2, P], F32R), ("sv1", [P, NB, 2, P], F32R))
        sk_hi, sk_lo, sv = (sk_hi0, sk_hi1), (sk_lo0, sk_lo1), (sv0, sv1)
        (s_o,) = overlay(b_hi_at, ("s_o", [P, KT, S], F32))
        (sq_hi0, sq_hi1, sq_lo0, sq_lo1, sp0, sp1, sph0, sph1, spl0, spl1, s_z, s_g, s_raw, s_sq, s_fold) = overlay(
            over_at, *((f"sq_{x}{t}", [P, S], F32R) for x in ("hi", "lo") for t in range(2)),
            ("sp0", [P, S], F32), ("sp1", [P, S], F32),
            ("sph0", [P, HALF], F32R), ("sph1", [P, HALF], F32R), ("spl0", [P, HALF], F32R), ("spl1", [P, HALF], F32R),
            ("s_z", [P, S], F32), ("s_g", [P, S], F32), ("s_raw", [P, S], F32), ("s_sq", [P, S], F32),
            ("s_fold", [P, HALF], F32))
        sq_hi, sq_lo, sp = (sq_hi0, sq_hi1), (sq_lo0, sq_lo1), (sp0, sp1)
        sp_hi, sp_lo = (sph0, sph1), (spl0, spl1)
        m_t0, m_t1, m_g0, m_g1, m_m = overlay(over_at, ("m_t0", [P, S], F32), ("m_t1", [P, S], F32),
                                              ("m_g0", [P, S], F32), ("m_g1", [P, S], F32), ("m_m", [P, S], F32))
        x_in0, x_in1, x_sum = overlay(over_at + 20 * 1024, ("x_in0", [P, S], F32), ("x_in1", [P, S], F32),
                                      ("x_sum", [P, S], F32))
        fq_hi0, fq_lo0, fk_hi0, fk_lo0, fq_hi1, fq_lo1, fk_hi1, fk_lo1 = overlay(
            a_lo_at, *((f"f{x}_{part}{t}", [P, S], F32R) for t in range(2) for x in ("q", "k") for part in ("hi", "lo")))
        f_hi, f_lo = ((fq_hi0, fk_hi0), (fq_hi1, fk_hi1)), ((fq_lo0, fk_lo0), (fq_lo1, fk_lo1))
        (f_o,) = overlay(a_hi_at, ("f_o", [P, KT, S], F32))
        fv, fp0, fp1, fp2, fp_hi, fp_lo, fc0, fc1, f_fold, f_raw = overlay(
            over_at, ("fv", [P, NB, 2, P], F32R), ("fp0", [P, S], F32), ("fp1", [P, S], F32),
            ("fp2", [P, S], F32), ("fp_hi", [P, NB, 2, P], F32R), ("fp_lo", [P, NB, 2, P], F32R), ("fc0", [P, S], F32), ("fc1", [P, S], F32),
            ("f_fold", [P, HALF], F32), ("f_raw", [P, S], F32))
        fp, fc = (fp0, fp1, fp2), (fc0, fc1)
        _, up_u, up_g, up_y, up_o = overlay(over_at, ("z_again", [P, KT, S], F32), ("up_u", [P, S], F32),
                                            ("up_g", [P, S + 2], F32), ("up_y", [P, S], F32), ("up_o", [P, S], F32))
        (ple,) = overlay(b_hi_at, ("ple", [P, KT, S], F32))
        p_raw, p_hi, p_lo, g_sig, g_out = overlay(
            b_lo_at, ("p_raw", [P, PLE_KT, S], F32), ("p_hi", [P, PLE_KT, S], F32R), ("p_lo", [P, PLE_KT, S], F32R),
            ("g_sig", [P, S], F32), ("g_out", [P, S], F32))

        def psum(name, n):
            return ctx.enter_context(nc.psum_tensor(name, [P, n], F32))

        bank = [psum(f"bank{h}", HALF) for h in range(2)]
        score = [psum(f"score{s}", S) for s in range(2)]
        flip = psum("flip", HALF)
        pv = psum("pv", HALF)
        down_bank = [[score[h][:, m * HALF:(m + 1) * HALF] for m in range(2)] for h in range(2)]
        flips = (flip, bank[1])

        def sem(name):
            return ctx.enter_context(nc.semaphore(name))

        cols_in = sem("cols_in")
        const_made = sem("const_made")
        raw_in = [sem(f"raw_in{b}") for b in range(2)]
        w_hi = sem("w_hi")
        w_lo = sem("w_lo")
        tile_done = [sem(f"tile_done{h}") for h in range(2)]
        tile_out = [sem(f"tile_out{h}") for h in range(2)]

        n0, n1, n2 = NormSemaphores(sem, "n0"), NormSemaphores(sem, "n1"), NormSemaphores(sem, "n2")
        sw, fx = AttentionSemaphores(sem, "sw"), AttentionSemaphores(sem, "fx")
        conv_step = sem("conv_step")
        conv_o = sem("conv_o")
        conv_hi = sem("conv_hi")
        conv_lo = sem("conv_lo")
        mix_done = sem("mix_done")
        t_stored = sem("t_stored")
        mt_in = [sem(f"mt_in{s}") for s in range(2)]
        mg_in = [sem(f"mg_in{s}") for s in range(2)]
        m_sum = sem("m_sum")
        m_hi = sem("m_hi")
        m_lo = sem("m_lo")
        x_in = [sem(f"x_in_{s}") for s in range(2)]
        x_hi = sem("x_hi")
        x_lo = sem("x_lo")
        f_step = sem("f_step")
        c_stored = sem("c_stored")
        c_in = [sem(f"c_in{h}") for h in range(2)]
        z_part = sem("z_part")
        ffn_pad = sem("ffn_pad")
        up_conv = sem("up_conv")
        up_gelu = sem("up_gelu")
        up_prod = sem("up_prod")
        up_hi = sem("up_hi")
        up_lo = sem("up_lo")
        down_out = [sem(f"down_out{h}") for h in range(2)]
        z_alpha = sem("z_alpha")
        p_in = sem("p_in")
        ple_hi = sem("ple_hi")
        ple_lo = sem("ple_lo")
        g_done = sem("g_done")
        g_sum = sem("g_sum")
        out_stored = sem("out_stored")

        passed = sem("passed")

        def settler(engine):
            def settle():
                engine.sem_inc(passed, 1)
            return settle

        block = ctx.enter_context(nc.Block())

        def hs(h):
            return slice(h * HALF, (h + 1) * HALF)

        def col(c):
            return cst[:, bass.ds(c, 1)] if not isinstance(c, int) else cst[:, c:c + 1]

        @block.sync
        def _(sp):
            for b in range(2):
                sp.dma_start(raw[b][:], weights[0, :, hs(b)]).then_inc(raw_in[b], 16)
            with sp.Fori(1, U_END) as u:
                for b in range(2):
                    sp.wait_ge(w_lo, u * 2 + (b - 1))
                    sp.dma_start(raw[b][:], weights[u, :, hs(b)]).then_inc(raw_in[b], 16)

        @block.gpsimd
        def _(pool):
            nc.gpsimd.memset(ident[:], 0.0).then_inc(const_made, 1)
            nc.gpsimd.memset(mask_f[:], 0.0).then_inc(const_made, 1)
            nc.gpsimd.memset(head_mean[:], 0.0).then_inc(const_made, 1)
            nc.gpsimd.memset(feat_mean[:], 1.0 / D).then_inc(const_made, 1)
            pool.wait_ge(const_made, 4)
            nc.gpsimd.memset(mask_f[:, 2 * P:3 * P], NEG).then_inc(const_made, 1)
            nc.gpsimd.affine_select(out=ident[:], in_=ident[:], compare_op=ALU.not_equal, fill=1.0, base=0,
                                    pattern=[[-1, P]], channel_multiplier=1).then_inc(const_made, 1)
            nc.gpsimd.affine_select(out=mask_f[:, 0:P], in_=mask_f[:, 0:P], compare_op=ALU.is_gt, fill=NEG, base=0,
                                    pattern=[[1, P]], channel_multiplier=-1).then_inc(const_made, 1)
            nc.gpsimd.affine_select(out=mask_f[:, P:2 * P], in_=mask_f[:, P:2 * P], compare_op=ALU.is_ge, fill=NEG,
                                    base=0, pattern=[[-1, P]], channel_multiplier=1).then_inc(const_made, 1)
            pool.wait_ge(const_made, 8)
            for h in range(2):
                nc.gpsimd.memset(head_mean[h * DH:(h + 1) * DH, h * DH:(h + 1) * DH], 1.0 / DH).then_inc(const_made, 1)
            pool.wait_ge(const_made, 10)
            nc.gpsimd.tensor_scalar(ident_r[:], ident[:], 1.0, 1.0, ALU.mult, ALU.mult).then_inc(const_made, 1)
            nc.gpsimd.tensor_scalar(mask_r[:], mask_f[:], 1.0, 1.0, ALU.mult, ALU.mult).then_inc(const_made, 1)
            nc.gpsimd.memset(eps_rms[:], RMS_EPS).then_inc(const_made, 1)
            nc.gpsimd.memset(eps_ln[:], LN_EPS).then_inc(const_made, 1)

            settle = settler(pool)

            def split(u, slot, freed):
                for b in range(2):
                    if freed is not None and b == 0:
                        pool.wait_ge(tile_done[1], freed)
                    pool.wait_ge(raw_in[b], u * 16 + 16)
                    settle()
                    hi, lo = whi[slot][:, 4 * b:4 * b + 4, :], wlo[slot][:, 4 * b:4 * b + 4, :]
                    src = raw[b][:].rearrange("p (k c) -> p k c", c=P)
                    nc.gpsimd.tensor_scalar(hi, src, 1.0, 1.0, ALU.mult, ALU.mult).then_inc(w_hi, 1)
                    pool.wait_ge(w_hi, u * 2 + (b + 1))
                    nc.gpsimd.tensor_tensor(lo, src, hi.bitcast(F32), ALU.subtract).then_inc(w_lo, 1)

            split(0, 0, None)
            split(1, 1, None)
            assert (U_FFN + 4 - 2) % 2 == 1
            with pool.Fori(0, (U_FFN + 4 - 3) // 2) as it:
                for c in range(2):
                    split(it * 2 + (2 + c), c, it * 2 + (1 + c))
            u = U_FFN + 3
            split(u, u % 2, u - 1)
            freed = (-1, 0, 1, 2, 3, 4)
            with pool.Fori(0, NGRP - 1) as it:
                for c in range(6):
                    split(it * 6 + (U_FFN + 4 + c), (U_FFN + c) % 2, it * 12 + (T_FFN + 4 + freed[c]))
            t = T_FFN + 4 + 12 * (NGRP - 1)
            for c, freed in enumerate((t - 4, t, t + 4, t + 8)):
                u = U_FFN + 4 + 6 * (NGRP - 1) + c
                split(u, u % 2, freed)
            for c in range(KT):
                u = U_GATE + c
                split(u, u % 2, (T_PLE + 4, T_PLE + 8)[c] if c < 2 else T_GATE + c - 1)

        @block.tensor
        def _(pe):
            def product(psum_ap, w, hi, lo, kts, wk, h):
                n = len(kts)
                for i, (kt, k) in enumerate(zip(kts, wk)):
                    for j, (ws, a) in enumerate(((whi, hi), (whi, lo), (wlo, hi))):
                        last = nc.tensor.matmul(psum_ap, ws[w][:, k, :], a[:, kt, hs(h)],
                                                start=(i == 0 and j == 0), stop=(i == n - 1 and j == 2))
                return last

            def tile(u, before, slot, hi, lo):
                pe.wait_ge(w_lo, u * 2 + 2)
                for h in range(2):
                    pe.wait_ge(tile_out[h], before)
                    product(bank[h][:], slot, hi, lo, range(KT), range(KT), h).then_inc(tile_done[h], 1)

            def quarter_tiles(u, before, slot, hi, lo, kts):
                pe.wait_ge(w_lo, u * 2 + 2)
                for m in range(4):
                    for h in range(2):
                        pe.wait_ge(tile_out[h], before + m)
                        product(bank[h][:], slot, hi, lo, kts, (2 * m, 2 * m + 1), h).then_inc(tile_done[h], 1)

            def down_tiles(u, group, q, slot, kts):
                pe.wait_ge(w_lo, u * 2 + 2)
                for m in range(4 * q, 4 * q + 4):
                    for h in range(2):
                        pe.wait_ge(down_out[h], group * KT + max(m - 1, 0))
                        product(down_bank[h][m % 2], slot, a_hi, a_lo, kts, (2 * (m % 4), 2 * (m % 4) + 1),
                                h).then_inc(tile_done[h], 1)

            def norm(ns, mean):
                if mean:
                    for h in range(2):
                        if h == 0:
                            pe.wait_ge(ns.acc, 2 * KT)
                        nc.tensor.matmul(score[0][:, hs(h)], feat_mean[:], acc[:, hs(h)],
                                         start=True, stop=True).then_inc(ns.mean, 1)
                for j in range(KT):
                    pe.wait_ge(ns.sq, j + 1)
                    for h in range(2):
                        last = nc.tensor.matmul(score[1][:, hs(h)], feat_mean[:], sq[j % 2][:, hs(h)],
                                                start=(j == 0), stop=(j == KT - 1))
                    last.then_inc(ns.sq_used, 1)

            def mean_square(n, h, dst):
                pe.wait_ge(sw.q_sq, n * 2 + (h + 1))
                nc.tensor.matmul(dst, head_mean[:], s_sq[:, hs(h)], start=True, stop=True).then_inc(sw.q_ms, 1)

            def flip_v(at, src, h, n, ready):
                pe.wait_ge(tile_out[h], ready)
                for b in range(4):
                    last = nc.tensor.transpose(flips[h][:, b * P:(b + 1) * P],
                                               src[:, (4 * h + b) * P:(4 * h + b + 1) * P], ident[:])
                last.then_inc(at.v_flip, 1)

            def part(u, t, slot, h, k, hi, lo):
                if k == 0:
                    if h == 0:
                        pe.wait_ge(w_lo, u * 2 + 2)
                        pe.wait_ge(tile_out[0], t)
                        pe.wait_ge(tile_out[1], t)
                    else:
                        pe.wait_ge(tile_out[0], t + 1)
                for j, (ws, a) in enumerate(((whi, hi), (whi, lo), (wlo, hi))):
                    last = nc.tensor.matmul(bank[0][:], ws[slot][:, k, :], a[:, k, hs(h)],
                                            start=(k == 0 and j == 0), stop=(k == KT - 1 and j == 2))
                if k == KT - 1:
                    last.then_inc(tile_done[h], 1)

            def window_pair(it, pp):
                last_pair = isinstance(it, int) and it * 2 + pp == NPAIR - 1
                st = it * (2 * NW) + pp * NW
                u0 = U_PAIR + 3 * pp
                n = it * 2 + (pp + 3)
                q_hi, q_lo, k_hi, k_lo, v = sq_hi[pp], sq_lo[pp], sk_hi[pp], sk_lo[pp], sv[pp]

                def fill(c, h):
                    if last_pair and c == 0:
                        return
                    back = 1 if last_pair else 0
                    u = it * 6 + (u0 + c - back)
                    if c == 1 and h == 0 and not last_pair:
                        pe.wait_ge(sw.q_std, n * 2 + 2)
                    for k in range(KT):
                        part(u, u, (u0 + c - back) % 2, h, k, a_hi, a_lo)

                def scores(s):
                    hh, g = WSTEPS[s]
                    rows = slice(hh * DH, (hh + 1) * DH)
                    pe.wait_ge(sw.exp, st * 4 + 4 * max(s - 1, 0))
                    for j in range(4):
                        qb = 4 * g + j
                        q = slice(qb * P, (qb + 1) * P)
                        c = j * 2 * P
                        if qb == 0:
                            nc.tensor.matmul(score[s % 2][:, 0:P], ident_r[:], mask_r[:, 2 * P:3 * P], start=True, stop=True)
                            ks, dst, mask = slice(0, P), score[s % 2][:, P:2 * P], mask_r[:, P:2 * P]
                        else:
                            ks, dst = slice((qb - 1) * P, (qb + 1) * P), score[s % 2][:, c:c + 2 * P]
                            mask = mask_r[:, 0:2 * P]
                        nc.tensor.matmul(dst, q_hi[rows, q], k_hi[rows, ks], start=True, stop=False)
                        nc.tensor.matmul(dst, q_hi[rows, q], k_lo[rows, ks], start=False, stop=False)
                        nc.tensor.matmul(dst, ident_r[:], mask, start=False, stop=False)
                        mm = nc.tensor.matmul(dst, q_lo[rows, q], k_hi[rows, ks], start=False, stop=True)
                    mm.then_inc(sw.scored, 1)

                def flip_p(s):
                    for c in range(2):
                        if c == 0:
                            pe.wait_ge(sw.prob, st + (s + 1))
                        pe.wait_ge(sw.lo, st * 2 + (2 * s + c - 1) if s or c else st * 2)
                        for b in range(4):
                            mm = nc.tensor.transpose(flips[c][:, b * P:(b + 1) * P],
                                                     sp[s % 2][:, (4 * c + b) * P:(4 * c + b + 1) * P], ident[:])
                        mm.then_inc(sw.flipped, 1)

                def values(s):
                    hh, g = WSTEPS[s]
                    pe.wait_ge(sw.o, st + s)
                    for c in range(2):
                        pe.wait_ge(sw.lo, st * 2 + (2 * s + c + 1))
                        for b in range(4):
                            j, i = (4 * c + b) // 2, b % 2
                            blk = 4 * g + j - 1 + i
                            if blk < 0:
                                continue
                            for pt in (sp_hi, sp_lo):
                                mm = nc.tensor.matmul(pv[:, j * P:(j + 1) * P], v[:, blk, hh, :],
                                                      pt[c][:, b * P:(b + 1) * P],
                                                      start=((i == 0 or blk == 0) and pt is sp_hi),
                                                      stop=(i == 1 and pt is sp_lo))
                        mm.then_inc(sw.pv, 1)

                pe.wait_ge(sw.q_lo, it * 2 + (pp + 3))
                scores(0)
                scores(1)
                fill(0, 0)
                flip_p(0)
                fill(0, 1)
                scores(2)
                values(0)
                flip_p(1)
                if not last_pair:
                    pe.wait_ge(tile_out[1], it * 6 + (u0 + 1))
                    mean_square(n, 0, bank[0][:])
                scores(3)
                if not last_pair:
                    pe.wait_ge(sw.q_std, n * 2 + 1)
                    mean_square(n, 1, bank[0][:])
                values(1)
                fill(1, 0)
                flip_p(2)
                fill(1, 1)
                values(2)
                fill(2, 0)
                flip_p(3)
                fill(2, 1)
                values(3)

            def forget_part(it, pp, i):
                u = U_FOX + 3 * pp + i // 16
                part(it * 6 + u, it * 6 + u, u % 2, i // 8 % 2, i % 8, b_hi, b_lo)

            def forget_pair(it, pp, fills):
                st, ch, gr = it * (2 * NST) + pp * NST, it * (2 * NCH) + pp * NCH, it * 8 + 4 * pp
                (q_hi, k_hi), (q_lo, k_lo) = f_hi[pp], f_lo[pp]

                def scores(s):
                    hh, qb = STEPS[s]
                    rows = slice(hh * DH, (hh + 1) * DH)
                    q = slice(qb * P, (qb + 1) * P)
                    w = (qb + 1) * P
                    pe.wait_ge(fx.max, st + max(s - 1, 0))
                    for c in range(0, w, HALF):
                        n = min(HALF, w - c)
                        ks = slice(c, c + n)
                        dst = score[s % 2][:, ks]
                        nc.tensor.matmul(dst, q_hi[rows, q], k_hi[rows, ks], start=True, stop=False)
                        nc.tensor.matmul(dst, q_hi[rows, q], k_lo[rows, ks], start=False, stop=False)
                        if c + n == w:
                            nc.tensor.matmul(score[s % 2][:, w - P:w], ident_r[:], mask_r[:, P:2 * P], start=False, stop=False)
                        mm = nc.tensor.matmul(dst, q_lo[rows, q], k_hi[rows, ks], start=False, stop=True)
                    mm.then_inc(fx.scored, 1)

                def flip_p(s):
                    for i, n in enumerate(CHUNKS_OF[s]):
                        blk, nb = CHUNKS[n][1:]
                        if i == 0:
                            pe.wait_ge(fx.prob, st + (s + 1))
                        if n < 2:
                            pe.wait_ge(fx.v_lo, it * 4 + (2 * pp + n + 1))
                        else:
                            pe.wait_ge(fx.lo, ch + (n - 1))
                        for b in range(nb):
                            mm = nc.tensor.transpose(flips[n % 2][:, b * P:(b + 1) * P],
                                                     fp[s % 3][:, (blk + b) * P:(blk + b + 1) * P], ident[:])
                        mm.then_inc(fx.flipped, 1)

                def values(s):
                    hh, qb = STEPS[s]
                    c = (qb - 1) % 4 * P
                    pe.wait_ge(fx.lo, ch + (CHUNKS_OF[s][-1] + 1))
                    if c == 0:
                        pe.wait_ge(fx.o, gr + s // 4)
                    for i, blk in enumerate([0, qb, *range(1, qb)]):
                        for pt in (fp_hi, fp_lo):
                            cols = slice(P if blk == qb else 0, 2 * P)
                            mm = nc.tensor.matmul(pv[:, c + cols.start:c + 2 * P], fv[:, blk, hh, :],
                                                  pt[:, blk, 1 if blk == qb else 0:2, :],
                                                  start=(i == 0 and pt is fp_hi),
                                                  stop=(pt is fp_lo and i == qb))
                    mm.then_inc(fx.pv, 1)

                for h in range(2):
                    pe.wait_ge(tile_out[h], it * 6 + (U_FOX + 3 * pp + 2))
                scores(0)
                scores(1)
                for i in range(40, 48):
                    forget_part(it, pp, i)
                for h in range(2):
                    pe.wait_ge(fx.lo, ch)
                    flip_v(fx, f_raw, h, it * 4 + (2 * pp + h), it * 6 + (U_FOX + 3 * pp + 3))
                scores(2)
                for s in range(NST):
                    flip_p(s)
                    if s + 3 < NST:
                        scores(s + 3)
                    if fills and s < 15:
                        for i in range(8 * (s // 3) + (0, 3, 6)[s % 3], 8 * (s // 3) + (3, 6, 8)[s % 3]):
                            forget_part(it if pp == 0 else it + 1, 1 - pp, i)
                    if s % 2:
                        values(s)

            pe.wait_ge(const_made, 14)
            norm(n0, False)
            pe.wait_ge(n0.lo, KT)
            with pe.Fori(0, KT) as i:
                for c in range(4):
                    tile(i * 4 + c, i * 4 + c, c % 2, a_hi, a_lo)
            pe.wait_ge(conv_lo, 2 * KT)
            with pe.Fori(0, KT) as j:
                for c, (hi, lo) in enumerate(((b_hi, b_lo), (a_hi, a_lo))):
                    tile(j * 2 + (U_MIX + c), j * 2 + (U_MIX + c), c, hi, lo)
            for t in range(2):
                for c in range(2):
                    u = U_SWA + 2 * t + c
                    tile(u, u, u % 2, a_hi, a_lo)
                for h in range(2):
                    mean_square(t, h, score[0][:, hs(h)])
                for h in range(2):
                    pe.wait_ge(sw.lo, 0)
                    if t:
                        pe.wait_ge(sw.v_lo, h + 1)
                    else:
                        pe.wait_ge(tile_out[1], U_SWA + 2)
                    flip_v(sw, s_z, h, 2 * t + h, U_SWA + 2 * t + 2)
                pe.wait_ge(sw.v_lo, 2 * t + 2)
            u = U_SWA + 4
            tile(u, u, u % 2, a_hi, a_lo)
            for h in range(2):
                mean_square(2, h, score[0][:, hs(h)])
            with pe.Fori(0, NPAIR // 2 - 1) as it:
                for pp in range(2):
                    window_pair(it, pp)
            for pp in range(2):
                window_pair(NPAIR // 2 - 1, pp)
            pe.wait_ge(tile_out[1], U_AOUT)
            pe.wait_ge(sw.o_lo, NPAIR)
            with pe.Fori(0, KT // 2) as j:
                for c in range(2):
                    tile(j * 2 + (U_AOUT + c), j * 2 + (U_AOUT + c), (U_AOUT + c) % 2, b_lo, b_hi)
            pe.wait_ge(m_lo, 2 * KT)
            with pe.Fori(0, KT // 2) as j:
                for c in range(2):
                    tile(j * 2 + (U_OUT + c), j * 2 + (U_OUT + c), (U_OUT + c) % 2, a_hi, a_lo)
            pe.wait_ge(x_lo, 2 * KT)
            tile(U_F, U_F, U_F % 2, b_hi, b_lo)
            for i in range(40):
                forget_part(0, 0, i)
            with pe.Fori(0, NPAIR // 2 - 1) as it:
                for pp in range(2):
                    forget_pair(it, pp, True)
            for pp in range(2):
                forget_pair(NPAIR // 2 - 1, pp, pp == 0)
            pe.wait_ge(tile_out[1], U_FOUT)
            pe.wait_ge(fx.o_lo, NPAIR)
            with pe.Fori(0, KT // 2) as j:
                for c in range(2):
                    tile(j * 2 + (U_FOUT + c), j * 2 + (U_FOUT + c), (U_FOUT + c) % 2, a_lo, a_hi)
            norm(n1, True)
            pe.wait_ge(n1.lo, KT)

            def up(u, before):
                for c in range(4):
                    tile(u + c, before + c, (U_FFN + c) % 2, b_hi, b_lo)

            def down(u, group, parity, seen):
                pe.wait_ge(up_lo, seen)
                for q in range(2):
                    down_tiles(u + q, group, q, (U_FFN + q) % 2, (2 * parity, 2 * parity + 1))

            up(U_FFN, T_FFN)
            with pe.Fori(0, (NGRP - 1) // 2) as it:
                for g in range(2):
                    u = U_FFN + 4 + 6 * g
                    up(it * 12 + u, it * 8 + (T_FFN + 4 + 4 * g))
                    down(it * 12 + (u + 4), it * 2 + g, g, it * 8 + 4 * (g + 1))
            down(U_PLE - 2, NGRP - 1, (NGRP - 1) % 2, 4 * NGRP)
            pe.wait_ge(ple_lo, PLE_KT)
            for q in range(2):
                quarter_tiles(U_PLE + q, O_PLE + 4 * q, (U_PLE + q) % 2, p_hi, p_lo, range(PLE_KT))
            norm(n2, True)
            pe.wait_ge(n2.lo, KT)
            for j in range(KT):
                tile(U_GATE + j, O_GATE + j, (U_GATE + j) % 2, a_hi, a_lo)

        @block.scalar
        def _(act):
            settle = settler(act)

            act.dma_start(cst[:], cols).then_inc(cols_in, 16)
            for j in range(KT):
                act.dma_start(z[:, j, :], xT[j, :, :]).then_inc(n0.x_in, 16)

            def norm(ns, mean, hi, bias):
                for j in range(KT):
                    if mean:
                        act.wait_ge(ns.centred, j + 1)
                    elif j == 0:
                        act.wait_ge(ns.x_in, 16 * KT)
                    if j >= 2:
                        act.wait_ge(ns.sq_used, j - 1)
                    nc.scalar.activation(sq[j % 2][:], z[:, j, :], ACT.Square).then_inc(ns.sq, 1)
                act.wait_ge(ns.sq_used, KT)
                act.wait_ge(cols_in, 16)
                act.wait_ge(const_made, 14)
                nc.scalar.activation(nrm[:], score[1][:], ACT.Ln, bias=eps_ln[:] if mean else eps_rms[:]).then_inc(ns.std, 1)
                act.wait_ge(ns.std, 1)
                nc.scalar.activation(nrm[:], nrm[:], ACT.Exp, scale=-0.5).then_inc(ns.rstd, 1)
                for j in range(KT):
                    act.wait_ge(ns.y, j + 1)
                    if bias is not None:
                        nc.scalar.activation(z[:, j, :], z[:, j, :], ACT.Identity, bias=col(bias + j)).then_inc(ns.yb, 1)
                        act.wait_ge(ns.yb, j + 1)
                    nc.scalar.activation(hi[:, j, :], z[:, j, :], ACT.Copy).then_inc(ns.hi, 1)

            def copy_tile(dst, t):
                for h in range(2):
                    act.wait_ge(tile_done[h], t + 1)
                    nc.scalar.activation(dst[:, hs(h)], bank[h][:], ACT.Copy).then_inc(tile_out[h], 1)

            def v_hi(at, v, h, n):
                act.wait_ge(at.v_flip, n + 1)
                nc.scalar.activation(v[:, 4 * h:4 * h + 4, :, 0:DH],
                                     flips[h][:].rearrange("p (b h d) -> p b h d", h=2, d=DH), ACT.Copy).then_inc(at.v_hi, 1)

            def raw_and_square(bank_of, t, n, h):
                act.wait_ge(tile_done[h], t + 1)
                nc.scalar.activation(s_raw[:, hs(h)], bank_of[:], ACT.Copy).then_inc(tile_out[h], 1)
                act.wait_ge(tile_out[h], t + 1)
                nc.scalar.activation(s_sq[:, hs(h)], s_raw[:, hs(h)], ACT.Square).then_inc(sw.q_sq, 1)

            def root(src, n, h):
                act.wait_ge(sw.q_ms, n * 2 + (h + 1))
                nc.scalar.activation(s_sq[:, hs(h)], src, ACT.Ln, bias=eps_rms[:]).then_inc(sw.q_std, 1)
                act.wait_ge(sw.q_std, n * 2 + (h + 1))
                settle()
                nc.scalar.activation(s_sq[:, hs(h)], s_sq[:, hs(h)], ACT.Exp, scale=-0.5).then_inc(sw.q_rstd, 1)

            def normed_hi(dst, n):
                act.wait_ge(sw.q_n, n + 1)
                nc.scalar.activation(dst[:], s_raw[:], ACT.Copy).then_inc(sw.q_hi, 1)

            def window_pair(it, pp):
                last_pair = isinstance(it, int) and it * 2 + pp == NPAIR - 1
                st = it * (2 * NW) + pp * NW
                pair = it * 2 + pp
                u0 = U_PAIR + 3 * pp - (1 if last_pair else 0)
                n = it * 2 + (pp + 3)

                def expo(s):
                    hh, g = WSTEPS[s]
                    act.wait_ge(sw.flipped, st * 2 + max(2 * s - 2, 0))
                    act.wait_ge(sw.neg_max, st + (s + 1))
                    for j in range(4):
                        cols = slice(j * 2 * P, (j + 1) * 2 * P)
                        one = slice(4 * (s % 2) + j, 4 * (s % 2) + j + 1)
                        nc.scalar.activation(sp[s % 2][:, cols], score[s % 2][:, cols], ACT.Exp, bias=neg_max[:, one],
                                             scale=SCALE, accum_out=row_sum[:, one]).then_inc(sw.exp, 1)
                    four = slice(4 * (s % 2), 4 * (s % 2) + 4)
                    settle()
                    nc.scalar.activation(sink_exp[:, four], neg_max[:, four], ACT.Exp,
                                         bias=col(it * 4 + (2 * pp + hh + C_SINK))).then_inc(sw.sink, 1)

                def high(s):
                    for c in range(2):
                        act.wait_ge(sw.pv, st * 2 + max(2 * s + c - 1, 0))
                        act.wait_ge(sw.flipped, st * 2 + (2 * s + c + 1))
                        nc.scalar.activation(sp_hi[c][:], flips[c][:], ACT.Copy).then_inc(sw.hi, 1)

                def fold(s):
                    act.wait_ge(sw.o, st + s)
                    act.wait_ge(sw.pv, st * 2 + (2 * s + 2))
                    nc.scalar.activation(s_fold[0:DH, :], pv[DH:P, :], ACT.Copy).then_inc(sw.fold, 1)

                def query(h):
                    if not last_pair:
                        raw_and_square(bank[0], it * 6 + u0, n, h)

                def gate_a(h):
                    act.wait_ge(tile_done[h], it * 6 + (u0 + 2))
                    nc.scalar.activation(s_z[:, hs(h)], bank[0][:], ACT.Silu).then_inc(tile_out[h], 1)

                def gate_b(h):
                    act.wait_ge(tile_done[h], it * 6 + (u0 + 3))
                    settle()
                    nc.scalar.activation(s_g[:, hs(h)], bank[0][:], ACT.Sigmoid,
                                         bias=col(pair + (C_GATEB + KT))).then_inc(tile_out[h], 1)

                expo(0)
                query(0)
                expo(1)
                high(0)
                query(1)
                fold(0)
                if not last_pair:
                    root(bank[0][:], n, 0)
                expo(2)
                high(1)
                if not last_pair:
                    root(bank[0][:], n, 1)
                fold(1)
                expo(3)
                act.wait_ge(sw.og, it * 2 + pp)
                gate_a(0)
                high(2)
                if not last_pair:
                    normed_hi(sq_hi[1 - pp], n)
                gate_a(1)
                fold(2)
                act.wait_ge(sw.g_out, it * 32 + 16 * pp)
                gate_b(0)
                high(3)
                gate_b(1)
                for h in range(2):
                    act.wait_ge(tile_out[h], it * 6 + (u0 + 3))
                act.dma_start(g_scr[pair, :, :], s_g[:]).then_inc(sw.g_out, 16)
                fold(3)

            def forget_out(it, pp, i):
                c, h = i // 2, i % 2
                act.wait_ge(tile_done[h], it * 6 + (U_FOX + 3 * pp + c + 1))
                if c < 2:
                    nc.scalar.activation(f_hi[pp][c][:, hs(h)], bank[0][:], ACT.Copy).then_inc(fx.q_hi, 1)
                else:
                    nc.scalar.activation(f_raw[:, hs(h)], bank[0][:], ACT.Copy).then_inc(tile_out[h], 1)

            def sums_in(it, pp, hh):
                row = bass.ds(it * 4 + (2 * pp + hh), 1)
                act.dma_start(fc[hh][:], c_scr[row, :].partition_broadcast(P)).then_inc(c_in[hh], 16)

            def forget_pair(it, pp, fills):
                st, ch, gr = it * (2 * NST) + pp * NST, it * (2 * NCH) + pp * NCH, it * 8 + 4 * pp
                following = (it, 1) if pp == 0 else (it + 1, 0)

                def expo(s):
                    w = (STEPS[s][1] + 1) * P
                    one = slice(s % 4, s % 4 + 1)
                    act.wait_ge(fx.neg_max, st + (s + 1))
                    nc.scalar.activation(fp[s % 3][:, 0:w], fp[s % 3][:, 0:w], ACT.Exp, bias=neg_max[:, one],
                                         accum_out=row_sum[:, one]).then_inc(fx.exp, 1)

                def normalise(s):
                    w = (STEPS[s][1] + 1) * P
                    act.wait_ge(fx.inv, st + (s + 1))
                    nc.scalar.activation(fp[s % 3][:, 0:w], fp[s % 3][:, 0:w], ACT.Copy,
                                         scale=row_inv[:, s % 4:s % 4 + 1]).then_inc(fx.prob, 1)

                def high(n):
                    s, blk, nb = CHUNKS[n]
                    if s % 2 == 0:
                        act.wait_ge(fx.pv, it * 16 + (8 * pp + s // 2))
                    act.wait_ge(fx.flipped, ch + (n + 1))
                    nc.scalar.activation(fp_hi[:, blk:blk + nb, s % 2, :],
                                         flips[n % 2][:, 0:nb * P].rearrange("p (b c) -> p b c", c=P),
                                         ACT.Copy).then_inc(fx.hi, 1)

                expo(0)
                normalise(0)
                expo(1)
                forget_out(it, pp, 5)
                act.wait_ge(fx.pv, it * 16 + 8 * pp)
                for h in range(2):
                    v_hi(fx, fv, h, it * 4 + (2 * pp + h))
                for s in range(NST):
                    if fills and s and s % 3 == 0:
                        forget_out(*following, s // 3 - 1)
                    if s + 1 < NST:
                        normalise(s + 1)
                    for n in CHUNKS_OF[s]:
                        high(n)
                    if s + 2 < NST:
                        expo(s + 2)
                    if s % 4 == 3:
                        act.wait_ge(fx.o, gr + s // 4)
                        act.wait_ge(fx.pv, it * 16 + (8 * pp + (s + 1) // 2))
                        nc.scalar.activation(f_fold[0:DH, :], pv[DH:P, :], ACT.Copy).then_inc(fx.fold, 1)
                    if fills and s in (9, 15):
                        act.wait_ge(fx.max, st + (8 if s == 9 else 16))
                        sums_in(*following, s // 15)

            norm(n0, False, a_hi, None)
            with act.Fori(0, KT) as i:
                act.wait_ge(conv_o, i * 2)
                copy_tile(cv_v, i * 4)
                for h in range(2):
                    act.wait_ge(tile_done[h], i * 4 + 4)
                    nc.scalar.activation(cv_g[:, hs(h)], bank[h][:], ACT.Silu).then_inc(tile_out[h], 1)
                for h in range(2):
                    act.wait_ge(conv_o, i * 2 + (h + 1))
                    settle()
                    nc.scalar.activation(b_hi[:, i, hs(h)], cv_o[:, hs(h)], ACT.Copy).then_inc(conv_hi, 1)
            act.wait_ge(conv_lo, 2 * KT)
            with act.Fori(0, KT) as j:
                act.wait_ge(mix_done, j * 2)
                copy_tile(mix_y, j * 2 + U_MIX)
                for h in range(2):
                    act.wait_ge(tile_done[h], j * 2 + (U_MIX + 2))
                    settle()
                    nc.scalar.activation(mix_g[:, hs(h)], bank[h][:], ACT.Sigmoid,
                                         bias=col(j + C_GATEB)).then_inc(tile_out[h], 1)
                act.wait_ge(mix_done, j * 2 + 2)
                act.dma_start(t_scr[j, :, :], mix_t[:]).then_inc(t_stored, 16)
            act.wait_ge(t_stored, 16 * KT)
            for t in range(2):
                if t:
                    act.wait_ge(sw.q_lo, t)
                for h in range(2):
                    raw_and_square(bank[h], U_SWA + 2 * t, t, h)
                if t:
                    act.wait_ge(sw.v_flip, 2 * t)
                copy_tile(s_z, U_SWA + 2 * t + 1)
                for h in range(2):
                    root(score[0][:, hs(h)], t, h)
                normed_hi(sk_hi[t], t)
                for h in range(2):
                    v_hi(sw, sv[t], h, 2 * t + h)
            act.wait_ge(sw.q_lo, 2)
            for h in range(2):
                raw_and_square(bank[h], U_SWA + 4, 2, h)
            for h in range(2):
                root(score[0][:, hs(h)], 2, h)
            normed_hi(sq_hi[0], 2)
            with act.Fori(0, NPAIR // 2 - 1) as it:
                for pp in range(2):
                    act.wait_ge(sw.q_lo, it * 2 + (pp + 3))
                    window_pair(it, pp)
            for pp in range(2):
                act.wait_ge(sw.q_lo, NPAIR + 1 + pp)
                window_pair(NPAIR // 2 - 1, pp)
            for j in range(NPAIR):
                act.wait_ge(sw.og, NPAIR)
                nc.scalar.activation(b_lo[:, j, :], s_o[:, j, :], ACT.Copy).then_inc(sw.o_hi, 1)
            act.wait_ge(sw.g_out, 16 * NPAIR)
            act.wait_ge(sw.o_lo, NPAIR)
            m_t, m_g = (m_t0, m_t1), (m_g0, m_g1)
            for s in range(2):
                act.dma_start(m_t[s][:], t_scr[s, :, :]).then_inc(mt_in[s], 16)
                act.dma_start(m_g[s][:], g_scr[s, :, :]).then_inc(mg_in[s], 16)

            def merged_hi(j):
                for h in range(2):
                    act.wait_ge(m_sum, j * 2 + (h + 1))
                    settle()
                    nc.scalar.activation(a_hi[:, j, hs(h)], m_m[:, hs(h)], ACT.Copy).then_inc(m_hi, 1)

            with act.Fori(0, KT // 2 - 1) as it:
                for c in range(2):
                    merged_hi(it * 2 + c)
                    act.dma_start(m_t[c][:], t_scr[it * 2 + (2 + c), :, :]).then_inc(mt_in[c], 16)
                    act.dma_start(m_g[c][:], g_scr[it * 2 + (2 + c), :, :]).then_inc(mg_in[c], 16)
            for j in (KT - 2, KT - 1):
                merged_hi(j)
            x_ins = (x_in0, x_in1)
            for s in range(2):
                act.dma_start(x_ins[s][:], xT[s, :, :]).then_inc(x_in[s], 16)

            def layer_hi(j):
                for h in range(2):
                    act.wait_ge(tile_out[h], j + (U_OUT + 1))
                    settle()
                    nc.scalar.activation(b_hi[:, j, hs(h)], x_sum[:, hs(h)], ACT.Copy).then_inc(x_hi, 1)

            with act.Fori(0, KT // 2 - 1) as it:
                for c in range(2):
                    layer_hi(it * 2 + c)
                    act.dma_start(x_ins[c][:], xT[it * 2 + (2 + c), :, :]).then_inc(x_in[c], 16)
            for j in (KT - 2, KT - 1):
                layer_hi(j)
            act.wait_ge(x_lo, 2 * KT)
            for h in range(2):
                act.wait_ge(tile_done[h], U_F + 1)
                nc.scalar.activation(fp0[0:16, hs(h)], bank[h][0:16, :], ACT.Identity,
                                     bias=cst[0:16, C_BF:C_BF + 1]).then_inc(tile_out[h], 1)
            for h in range(2):
                act.wait_ge(tile_out[h], U_F + 1)
            nc.scalar.activation(fp1[0:16, :], fp0[0:16, :], ACT.Abs).then_inc(f_step, 1)
            act.wait_ge(f_step, 1)
            nc.scalar.activation(fp1[0:16, :], fp1[0:16, :], ACT.Exp, scale=-1.0).then_inc(f_step, 1)
            act.wait_ge(f_step, 2)
            nc.scalar.activation(fp1[0:16, :], fp1[0:16, :], ACT.Ln, bias=1.0).then_inc(f_step, 1)
            act.wait_ge(f_step, 6)
            act.dma_start(c_scr, fp1[0:16, :]).then_inc(c_stored, 16)
            act.wait_ge(c_stored, 16)
            for hh in range(2):
                sums_in(0, 0, hh)
            for i in range(5):
                forget_out(0, 0, i)
            with act.Fori(0, NPAIR // 2 - 1) as it:
                for pp in range(2):
                    forget_pair(it, pp, True)
            for pp in range(2):
                forget_pair(NPAIR // 2 - 1, pp, pp == 0)
            act.wait_ge(fx.o, 4 * NPAIR)
            for j in range(NPAIR):
                nc.scalar.activation(a_lo[:, j, :], f_o[:, j, :], ACT.Copy).then_inc(fx.o_hi, 1)
            norm(n1, True, b_hi, C_LN1B)
            act.wait_ge(n1.lo, KT)
            for j in range(KT):
                nc.scalar.activation(z[:, j, :], z[:, j, :], ACT.Copy, scale=ALPHA).then_inc(z_alpha, 1)

            def up(t, n, parity):
                for c in range(2):
                    act.wait_ge(up_prod, (n + c) * 2)
                    copy_tile(up_u, t + 2 * c)
                    for h in range(2):
                        act.wait_ge(tile_done[h], t + (2 * c + 2))
                        nc.scalar.activation(up_g[:, 2 + h * HALF:2 + (h + 1) * HALF], bank[h][:],
                                             ACT.Copy).then_inc(tile_out[h], 1)
                    act.wait_ge(up_conv, (n + c) * 3 + 3)
                    nc.scalar.activation(up_y[:], up_y[:], ACT.Gelu).then_inc(up_gelu, 1)
                    for h in range(2):
                        act.wait_ge(up_prod, (n + c) * 2 + (h + 1))
                        nc.scalar.activation(a_hi[:, 2 * parity + c, hs(h)], up_o[:, hs(h)], ACT.Copy).then_inc(up_hi, 1)

            act.wait_ge(ffn_pad, 1)
            up(T_FFN, 0, 0)
            with act.Fori(0, (NGRP - 1) // 2) as it:
                for g in range(2):
                    up(it * 24 + (T_FFN + 4 + 12 * g), it * 4 + (2 * g + 2), (g + 1) % 2)
            act.wait_ge(up_lo, 2 * FT)
            for k in range(PLE_KT):
                act.dma_start(p_raw[:, k, :], pT[k, :, :]).then_inc(p_in, 16)
            act.wait_ge(p_in, 16 * PLE_KT)
            for k in range(PLE_KT):
                nc.scalar.activation(p_hi[:, k, :], p_raw[:, k, :], ACT.Copy).then_inc(ple_hi, 1)
            for m in range(KT):
                copy_tile(ple[:, m, :], T_PLE + m)
            norm(n2, True, a_hi, C_LN2B)
            for j in range(KT):
                for h in range(2):
                    if j:
                        act.wait_ge(g_done, 2 * j - 1 + h)
                    act.wait_ge(tile_done[h], T_GATE + j + 1)
                    nc.scalar.activation(g_sig[:, hs(h)], bank[h][:], ACT.Sigmoid, bias=col(C_PLEB + j)).then_inc(tile_out[h], 1)
                act.wait_ge(g_sum, 2 * j + 2)
                act.dma_start(out[j, :, :], g_out[:]).then_inc(out_stored, 16)
            act.wait_ge(out_stored, 16 * KT)

        @block.vector
        def _(dve):
            v = nc.vector

            settle = settler(dve)

            def norm(ns, mean, hi, lo, gain):
                if mean:
                    dve.wait_ge(ns.mean, 2)
                    for j in range(KT):
                        v.tensor_tensor(z[:, j, :], z[:, j, :], score[0][:], ALU.subtract).then_inc(ns.centred, 1)
                dve.wait_ge(ns.rstd, 1)

                def scaled(j):
                    if mean:
                        dve.wait_ge(ns.sq, j + 1)
                    v.scalar_tensor_tensor(z[:, j, :], z[:, j, :], col(gain + j), nrm[:], ALU.mult, ALU.mult).then_inc(ns.y, 1)

                scaled(0)
                for j in range(KT):
                    if j + 1 < KT:
                        scaled(j + 1)
                    dve.wait_ge(ns.hi, j + 1)
                    v.tensor_tensor(lo[:, j, :], z[:, j, :], hi[:, j, :].bitcast(F32), ALU.subtract).then_inc(ns.lo, 1)

            def v_lo(at, dst, h, n):
                dve.wait_ge(at.v_hi, n + 1)
                v.tensor_tensor(dst[:, 4 * h:4 * h + 4, :, DH:P], flips[h][:].rearrange("p (b h d) -> p b h d", h=2, d=DH),
                                dst[:, 4 * h:4 * h + 4, :, 0:DH].bitcast(F32), ALU.subtract).then_inc(at.v_lo, 1)

            def normed(n, gain):
                dve.wait_ge(sw.q_rstd, n * 2 + 2)
                v.scalar_tensor_tensor(s_raw[:], s_raw[:], col(gain), s_sq[:], ALU.mult, ALU.mult).then_inc(sw.q_n, 1)

            def normed_lo(n, hi, lo):
                dve.wait_ge(sw.q_hi, n + 1)
                v.tensor_tensor(lo[:], s_raw[:], hi[:].bitcast(F32), ALU.subtract).then_inc(sw.q_lo, 1)

            def window_pair(it, pp):
                last_pair = isinstance(it, int) and it * 2 + pp == NPAIR - 1
                st = it * (2 * NW) + pp * NW
                pair = it * 2 + pp
                u0 = U_PAIR + 3 * pp - (1 if last_pair else 0)
                n = it * 2 + (pp + 3)

                def maxima(s):
                    hh, g = WSTEPS[s]
                    four = slice(4 * (s % 2), 4 * (s % 2) + 4)
                    dve.wait_ge(sw.scored, st + (s + 1))
                    v.reduce_max(mx[:, four], score[s % 2][:].rearrange("p (j k) -> p j k", j=4), AX).then_inc(sw.max, 1)
                    dve.wait_ge(sw.max, st + (s + 1))
                    v.tensor_scalar(neg_max[:, four], mx[:, four], -SCALE, neg_sink[:, bass.ds(it * 4 + (2 * pp + hh), 1)],
                                    ALU.mult, ALU.min).then_inc(sw.neg_max, 1)

                def normalise(s):
                    four = slice(4 * (s % 2), 4 * (s % 2) + 4)
                    dve.wait_ge(sw.sink, st + (s + 1))
                    dve.wait_ge(sw.exp, st * 4 + (4 * s + 4))
                    v.tensor_tensor(row_sum[:, four], row_sum[:, four], sink_exp[:, four], ALU.add).then_inc(sw.total, 1)
                    dve.wait_ge(sw.total, st + (s + 1))
                    v.reciprocal(row_inv[:, four], row_sum[:, four]).then_inc(sw.inv, 1)
                    dve.wait_ge(sw.inv, st + (s + 1))
                    p4 = sp[s % 2][:].rearrange("p (j k) -> p j k", j=4)
                    v.tensor_tensor(p4, p4, row_inv[:, four].unsqueeze(2).to_broadcast([P, 4, 2 * P]),
                                    ALU.mult).then_inc(sw.prob, 1)

                def low(s):
                    for c in range(2):
                        dve.wait_ge(sw.hi, st * 2 + (2 * s + c + 1))
                        v.tensor_tensor(sp_lo[c][:], flips[c][:], sp_hi[c][:].bitcast(F32), ALU.subtract).then_inc(sw.lo, 1)

                def add(s):
                    hh, g = WSTEPS[s]
                    dve.wait_ge(sw.fold, st + (s + 1))
                    v.tensor_tensor(s_o[hh * DH:(hh + 1) * DH, pair, hs(g)], pv[0:DH, :], s_fold[0:DH, :],
                                    ALU.add).then_inc(sw.o, 1)

                maxima(0)
                normalise(0)
                maxima(1)
                low(0)
                normalise(1)
                add(0)
                maxima(2)
                low(1)
                normalise(2)
                add(1)
                maxima(3)
                if not last_pair:
                    normed(n, C_QG)
                low(2)
                normalise(3)
                if not last_pair:
                    normed_lo(n, sq_hi[1 - pp], sq_lo[1 - pp])
                add(2)
                low(3)
                add(3)
                dve.wait_ge(sw.o, st + NW)
                for h in range(2):
                    dve.wait_ge(tile_out[h], it * 6 + (u0 + 2))
                v.tensor_tensor(s_o[:, pair, :], s_o[:, pair, :], s_z[:], ALU.mult).then_inc(sw.og, 1)

            def forget_out(it, pp, i):
                c, h = i // 2, i % 2
                if c < 2:
                    dve.wait_ge(fx.q_hi, it * 8 + (4 * pp + i + 1))
                    v.tensor_tensor(f_lo[pp][c][:, hs(h)], bank[0][:], f_hi[pp][c][:, hs(h)].bitcast(F32),
                                    ALU.subtract).then_inc(tile_out[h], 1)

            def forget_pair(it, pp, fills):
                st, ch, gr = it * (2 * NST) + pp * NST, it * (2 * NCH) + pp * NCH, it * 8 + 4 * pp
                following = (it, 1) if pp == 0 else (it + 1, 0)

                def maxima(s):
                    hh, qb = STEPS[s]
                    w = (qb + 1) * P
                    one = slice(s % 4, s % 4 + 1)
                    if qb == 0:
                        dve.wait_ge(c_in[hh], it * 32 + (16 * pp + 16))
                    dve.wait_ge(fx.flipped, ch + (CHUNKS_OF[s - 3][-1] + 1 if s >= 3 else 0))
                    dve.wait_ge(fx.scored, st + (s + 1))
                    settle()
                    v.tensor_tensor_reduce(out=fp[s % 3][:, 0:w], in0=score[s % 2][:, 0:w], in1=fc[hh][:, 0:w],
                                           scale=SCALE, scalar=-3.0e38, op0=ALU.subtract, op1=ALU.max,
                                           accum_out=mx[:, one]).then_inc(fx.max, 1)
                    dve.wait_ge(fx.max, st + (s + 1))
                    v.tensor_scalar(neg_max[:, one], mx[:, one], -1.0, None, ALU.mult).then_inc(fx.neg_max, 1)

                def inverse(s):
                    one = slice(s % 4, s % 4 + 1)
                    dve.wait_ge(fx.exp, st + (s + 1))
                    v.reciprocal(row_inv[:, one], row_sum[:, one]).then_inc(fx.inv, 1)

                def low(n):
                    s, blk, nb = CHUNKS[n]
                    dve.wait_ge(fx.hi, ch + (n + 1))
                    v.tensor_tensor(fp_lo[:, blk:blk + nb, s % 2, :],
                                    flips[n % 2][:, 0:nb * P].rearrange("p (b c) -> p b c", c=P),
                                    fp_hi[:, blk:blk + nb, s % 2, :].bitcast(F32), ALU.subtract).then_inc(fx.lo, 1)

                maxima(0)
                inverse(0)
                maxima(1)
                inverse(1)
                for h in range(2):
                    v_lo(fx, fv, h, it * 4 + (2 * pp + h))
                for s in range(NST):
                    if fills and s and s % 3 == 0:
                        forget_out(*following, s // 3 - 1)
                    if s + 2 < NST:
                        maxima(s + 2)
                    for n in CHUNKS_OF[s]:
                        low(n)
                    if s + 2 < NST:
                        inverse(s + 2)
                    if s % 4 == 3:
                        hh, qb = STEPS[s]
                        dve.wait_ge(fx.fold, gr + (s // 4 + 1))
                        v.tensor_tensor(f_o[hh * DH:(hh + 1) * DH, it * 2 + pp, hs(qb // 4)], pv[0:DH, :],
                                        f_fold[0:DH, :], ALU.add).then_inc(fx.o, 1)

            dve.wait_ge(cols_in, 16)
            v.tensor_scalar(neg_sink[:], cst[:, C_SINK:C_SINK + 2 * NPAIR], -1.0, None, ALU.mult).then_inc(conv_step, 1)
            norm(n0, False, a_hi, a_lo, C_NORM)
            dve.wait_ge(n0.lo, KT)
            v.memset(cv_u[:, 0:2], 0.0).then_inc(conv_step, 1)
            with dve.Fori(0, KT) as i:
                for h in range(2):
                    dve.wait_ge(tile_out[h], i * 4 + 1)
                    dve.wait_ge(tile_done[h], i * 4 + 2)
                    v.tensor_tensor(cv_u[:, 2 + h * HALF:2 + (h + 1) * HALF], bank[h][:], cv_v[:, hs(h)],
                                    ALU.mult).then_inc(tile_out[h], 1)
                for h in range(2):
                    dve.wait_ge(tile_out[h], i * 4 + 2)
                v.tensor_scalar(cv_y[:], cv_u[:, 0:S], col(i * 3 + C_CONV), None, ALU.mult).then_inc(conv_step, 1)
                for k in (1, 2):
                    dve.wait_ge(conv_step, i * 3 + (2 + k))
                    v.scalar_tensor_tensor(cv_y[:], cv_u[:, k:k + S], col(i * 3 + (C_CONV + k)), cv_y[:], ALU.mult,
                                           ALU.add).then_inc(conv_step, 1)
                dve.wait_ge(conv_step, i * 3 + 5)
                for h in range(2):
                    dve.wait_ge(tile_done[h], i * 4 + 3)
                    v.tensor_tensor(cv_y[:, hs(h)], bank[h][:], cv_y[:, hs(h)], ALU.mult).then_inc(tile_out[h], 1)
                for h in range(2):
                    dve.wait_ge(tile_out[h], i * 4 + 4)
                    v.tensor_tensor(cv_o[:, hs(h)], cv_y[:, hs(h)], cv_g[:, hs(h)], ALU.mult).then_inc(conv_o, 1)
                for h in range(2):
                    dve.wait_ge(conv_hi, i * 2 + (h + 1))
                    v.tensor_tensor(b_lo[:, i, hs(h)], cv_o[:, hs(h)], b_hi[:, i, hs(h)].bitcast(F32),
                                    ALU.subtract).then_inc(conv_lo, 1)
            with dve.Fori(0, KT) as j:
                dve.wait_ge(t_stored, j * 16)
                for h in range(2):
                    dve.wait_ge(tile_out[h], j * 2 + (U_MIX + 2))
                    v.tensor_tensor(mix_t[:, hs(h)], mix_y[:, hs(h)], mix_g[:, hs(h)], ALU.mult).then_inc(mix_done, 1)
            for t in range(2):
                normed(t, C_KG)
                normed_lo(t, sk_hi[t], sk_lo[t])
                for h in range(2):
                    v_lo(sw, sv[t], h, 2 * t + h)
            normed(2, C_QG)
            normed_lo(2, sq_hi[0], sq_lo[0])
            with dve.Fori(0, NPAIR // 2 - 1) as it:
                for pp in range(2):
                    window_pair(it, pp)
            for pp in range(2):
                window_pair(NPAIR // 2 - 1, pp)
            for j in range(NPAIR):
                dve.wait_ge(sw.o_hi, j + 1)
                v.tensor_tensor(b_hi[:, j, :], s_o[:, j, :], b_lo[:, j, :].bitcast(F32), ALU.subtract).then_inc(sw.o_lo, 1)
            m_t, m_g = (m_t0, m_t1), (m_g0, m_g1)
            with dve.Fori(0, KT // 2) as it:
                for c in range(2):
                    dve.wait_ge(mg_in[c], it * 16 + 16)
                    dve.wait_ge(mt_in[c], it * 16 + 16)
                    dve.wait_ge(m_lo, it * 4 + 2 * c)
                    for h in range(2):
                        dve.wait_ge(tile_done[h], it * 2 + (U_AOUT + c + 1))
                        v.tensor_tensor(m_m[:, hs(h)], bank[h][:], m_g[c][:, hs(h)], ALU.mult).then_inc(tile_out[h], 1)
                    for h in range(2):
                        dve.wait_ge(tile_out[h], it * 2 + (U_AOUT + c + 1))
                        v.tensor_tensor(m_m[:, hs(h)], m_m[:, hs(h)], m_t[c][:, hs(h)], ALU.add).then_inc(m_sum, 1)
                    for h in range(2):
                        dve.wait_ge(m_hi, it * 4 + (2 * c + h + 1))
                        v.tensor_tensor(a_lo[:, it * 2 + c, hs(h)], m_m[:, hs(h)], a_hi[:, it * 2 + c, hs(h)].bitcast(F32),
                                        ALU.subtract).then_inc(m_lo, 1)
            x_ins = (x_in0, x_in1)
            with dve.Fori(0, KT // 2) as it:
                for c in range(2):
                    dve.wait_ge(x_in[c], it * 16 + 16)
                    dve.wait_ge(x_lo, it * 4 + 2 * c)
                    for h in range(2):
                        dve.wait_ge(tile_done[h], it * 2 + (U_OUT + c + 1))
                        v.tensor_tensor(x_sum[:, hs(h)], bank[h][:], x_ins[c][:, hs(h)], ALU.add).then_inc(tile_out[h], 1)
                    for h in range(2):
                        dve.wait_ge(x_hi, it * 4 + (2 * c + h + 1))
                        v.tensor_tensor(b_lo[:, it * 2 + c, hs(h)], x_sum[:, hs(h)], b_hi[:, it * 2 + c, hs(h)].bitcast(F32),
                                        ALU.subtract).then_inc(x_lo, 1)
            dve.wait_ge(f_step, 3)
            v.tensor_scalar(fp0[0:16, :], fp0[0:16, :], 0.0, None, ALU.min).then_inc(f_step, 1)
            dve.wait_ge(f_step, 4)
            v.tensor_tensor_scan(fp0[0:16, :], fp0[0:16, :], fp1[0:16, :], 0.0, ALU.add, ALU.subtract).then_inc(f_step, 1)
            dve.wait_ge(f_step, 5)
            v.tensor_scalar(fp1[0:16, :], fp0[0:16, :], 1.0 / SCALE, None, ALU.mult).then_inc(f_step, 1)
            dve.wait_ge(c_stored, 16)
            for i in range(5):
                forget_out(0, 0, i)
            with dve.Fori(0, NPAIR // 2 - 1) as it:
                for pp in range(2):
                    forget_pair(it, pp, True)
            for pp in range(2):
                forget_pair(NPAIR // 2 - 1, pp, pp == 0)
            for j in range(NPAIR):
                dve.wait_ge(fx.o_hi, j + 1)
                v.tensor_tensor(a_hi[:, j, :], f_o[:, j, :], a_lo[:, j, :].bitcast(F32), ALU.subtract).then_inc(fx.o_lo, 1)
            dve.wait_ge(fx.o_lo, NPAIR)
            v.memset(acc[:], 0.0).then_inc(z_part, 1)

            with dve.Fori(0, KT) as j:
                for h in range(2):
                    dve.wait_ge(tile_done[h], j + (U_FOUT + 1))
                    v.scalar_tensor_tensor(z[:, j, hs(h)], b_hi[:, j, hs(h)].bitcast(F32), ALPHA, bank[h][:], ALU.mult,
                                           ALU.add).then_inc(tile_out[h], 1)
                for h in range(2):
                    dve.wait_ge(tile_out[h], j + (U_FOUT + 1))
                    v.scalar_tensor_tensor(z[:, j, hs(h)], b_lo[:, j, hs(h)].bitcast(F32), ALPHA, z[:, j, hs(h)], ALU.mult,
                                           ALU.add).then_inc(z_part, 1)
                for h in range(2):
                    dve.wait_ge(z_part, j * 2 + (h + 2))
                    v.tensor_tensor(acc[:, hs(h)], acc[:, hs(h)], z[:, j, hs(h)], ALU.add).then_inc(n1.acc, 1)
                dve.wait_ge(n1.acc, j * 2 + 2)
            norm(n1, True, b_hi, b_lo, C_LN1G)

            def convolved(before, n, c):
                f = n + c
                for h in range(2):
                    dve.wait_ge(tile_out[h], before + (2 * c + 2))
                v.tensor_scalar(up_y[:], up_g[:, 0:S], col(f * 3 + C_FCW), col(f + C_FCB), ALU.mult,
                                ALU.add).then_inc(up_conv, 1)
                for k in (1, 2):
                    dve.wait_ge(up_conv, f * 3 + k)
                    v.scalar_tensor_tensor(up_y[:], up_g[:, k:k + S], col(f * 3 + (C_FCW + k)), up_y[:], ALU.mult,
                                           ALU.add).then_inc(up_conv, 1)

            def gated(n, c, parity):
                f = n + c
                dve.wait_ge(up_gelu, f + 1)
                for h in range(2):
                    v.tensor_tensor(up_o[:, hs(h)], up_y[:, hs(h)], up_u[:, hs(h)], ALU.mult).then_inc(up_prod, 1)
                for h in range(2):
                    dve.wait_ge(up_hi, f * 2 + (h + 1))
                    v.tensor_tensor(a_lo[:, 2 * parity + c, hs(h)], up_o[:, hs(h)],
                                    a_hi[:, 2 * parity + c, hs(h)].bitcast(F32), ALU.subtract).then_inc(up_lo, 1)

            def down(t, m):
                for h in range(2):
                    dve.wait_ge(tile_done[h], t + (m + 1))
                    v.tensor_tensor(z[:, m, hs(h)], z[:, m, hs(h)], down_bank[h][m % 2], ALU.add).then_inc(down_out[h], 1)

            dve.wait_ge(n1.lo, KT)
            v.memset(up_g[:, 0:2], 0.0).then_inc(ffn_pad, 1)
            for c in range(2):
                convolved(T_FFN, 0, c)
                gated(0, c, 0)
            dve.wait_ge(z_alpha, KT)
            with dve.Fori(0, (NGRP - 1) // 2) as it:
                for g in range(2):
                    n = it * 4 + (2 * g + 2)
                    before = it * 8 + (T_FFN + 4 + 4 * g)
                    t = it * 24 + (T_FFN + 8 + 12 * g)
                    convolved(before, n, 0)
                    gated(n, 0, (g + 1) % 2)
                    convolved(before, n, 1)
                    for m in range(2):
                        down(t, m)
                    gated(n, 1, (g + 1) % 2)
                    for m in range(2, KT):
                        down(t, m)
            dve.wait_ge(up_lo, 2 * FT)
            for m in range(KT):
                down(T_PLE - KT, m)
                for h in range(2):
                    dve.wait_ge(down_out[h], (NGRP - 1) * KT + m + 1)
                    if m:
                        dve.wait_ge(n2.acc, 2 * m)
                        v.tensor_tensor(acc[:, hs(h)], acc[:, hs(h)], z[:, m, hs(h)], ALU.add).then_inc(n2.acc, 1)
                    else:
                        v.tensor_copy(acc[:, hs(h)], z[:, m, hs(h)]).then_inc(n2.acc, 1)
            for k in range(PLE_KT):
                dve.wait_ge(ple_hi, k + 1)
                v.tensor_tensor(p_lo[:, k, :], p_raw[:, k, :], p_hi[:, k, :].bitcast(F32), ALU.subtract).then_inc(ple_lo, 1)
            norm(n2, True, a_hi, a_lo, C_LN2G)
            for j in range(KT):
                if j:
                    dve.wait_ge(out_stored, 16 * j)
                for h in range(2):
                    dve.wait_ge(tile_out[h], O_GATE + j + 1)
                    v.tensor_tensor(g_out[:, hs(h)], ple[:, j, hs(h)], g_sig[:, hs(h)], ALU.mult).then_inc(g_done, 1)
                for h in range(2):
                    dve.wait_ge(g_done, 2 * j + h + 1)
                    v.tensor_tensor(g_out[:, hs(h)], g_out[:, hs(h)], z[:, j, hs(h)], ALU.add).then_inc(g_sum, 1)


def lay_out(a):
    a = {k: np.asarray(v) for k, v in a.items()}

    def units(w):
        n = w.shape[1] // P
        return w.reshape(KT, P, n, P).transpose(2, 1, 0, 3).reshape(n, P, KT * P)

    def quarters(w):
        return w.reshape(2, P, 2, 4, P).transpose(2, 1, 3, 0, 4).reshape(2, P, KT * P)

    order = [h for p in range(NPAIR) for h in (8 * (p % 2) + p // 2, 8 * (p % 2) + 4 + p // 2)]
    by_pair = np.concatenate([np.arange(h * DH, (h + 1) * DH) for h in order])

    w_in, conv_out, attn_out, w_out = (a[k][0] for k in ("w_in", "w_conv_out", "w_attn_out", "w_out"))
    kv = P * 2
    at = np.cumsum([0, D, D, D, D, D, kv, kv, D, D, D])
    v_c, b_c, c_c, z_c, q, k, v, z_a, g_a, g_b = (w_in[:, at[i]:at[i + 1]] for i in range(10))
    v_c, b_c, c_c, z_c, g_a, g_b, k, v = (units(w) for w in (v_c, b_c, c_c, z_c, g_a, g_b, k, v))
    q, z_a = units(q[:, by_pair]), units(z_a[:, by_pair])
    conv_out, attn_out, w_out = units(conv_out), units(attn_out[by_pair]), units(w_out)
    seq = []
    for i in range(KT):
        seq += [v_c[i], c_c[i], b_c[i], z_c[i]]
    for i in range(KT):
        seq += [conv_out[i], g_a[i]]
    seq += [k[0], v[0], k[1], v[1], q[0]]
    for p in range(NPAIR):
        seq += ([q[p + 1]] if p + 1 < NPAIR else []) + [z_a[p], g_b[p]]
    seq += [*attn_out, *w_out]
    w2 = a["attn_w_in_2"][0]
    seq += [*units(np.pad(w2[:, 3 * D:], ((0, 0), (0, P - 2 * NPAIR))))]
    fq, fk, fv = (units(w2[:, i * D:(i + 1) * D]) for i in range(3))
    for p in range(NPAIR):
        seq += [fq[p], fk[p], fv[p]]
    seq += [*units(a["attn_w_out_2"][0])]
    w_up, w_down = a["ffn_w_up_2"][0], a["ffn_w_down_2"][0]
    u, g = units(w_up[:, :FFN]), units(w_up[:, FFN:])
    down = [quarters(w_down[n * 2 * P:(n + 1) * 2 * P]) for n in range(NGRP)]
    for n in range(NGRP):
        seq += [u[2 * n], g[2 * n], u[2 * n + 1], g[2 * n + 1]]
        if n:
            seq += [*down[n - 1]]
    seq += [*down[-1], *quarters(a["ple_w_proj_2"][0]), *units(a["ple_w_gate_2"][0])]
    weights = np.stack(seq)
    assert weights.shape[0] == U_END

    def columns(vec):
        return vec.reshape(-1, P).T

    def taps(w):
        return w.reshape(3, -1, P).transpose(2, 1, 0).reshape(P, -1)

    cols = np.concatenate([
        columns(a["norm_g"][0]), taps(a["conv_w"][0]), columns(np.tile(a["q_norm_g"][0], 2)),
        columns(np.tile(a["k_norm_g"][0], 2)), columns(a["gate_b"][0]), taps(a["ffn_conv_w_2"][0]),
        columns(a["ffn_conv_b_2"][0]), columns(a["ln_mix_g_2"][0]), columns(a["ln_mix_b_2"][0]),
        columns(a["ln_ffn_g_2"][0]), columns(a["ln_ffn_b_2"][0]), columns(a["ple_b_gate_2"][0]),
        columns(np.pad(a["attn_b_f_2"][0], (0, P - 2 * NPAIR))), np.tile(a["sinks"][0][order], (P, 1))], axis=1)
    assert cols.shape == (P, N_COLS)

    def feature_major(x):
        return np.ascontiguousarray(x.T.reshape(-1, P, S))

    return {"in_x": feature_major(a["x"][0]), "in_w": weights, "in_cols": np.ascontiguousarray(cols),
            "in_p": feature_major(a["p_2"][0, 0])}


def kernel(**inputs):
    import concourse.bacc as _bacc
    from concourse import mybir as _mybir
    from concourse.bass_utils import run_bass_kernel_spmd as _run

    arrays = lay_out(inputs)
    nc = _bacc.Bacc("TRN2", target_bir_lowering=False, num_devices=1)
    f32 = _mybir.dt.float32
    ins = {k: nc.dram_tensor(k, a.shape, f32, kind="ExternalInput").ap() for k, a in arrays.items()}
    out = nc.dram_tensor("out_y", (KT, P, S), f32, kind="ExternalOutput").ap()
    t_scr = nc.dram_tensor("t_scr", (KT, P, S), f32, kind="Internal").ap()
    g_scr = nc.dram_tensor("g_scr", (KT, P, S), f32, kind="Internal").ap()
    c_scr = nc.dram_tensor("c_scr", (2 * NPAIR, S), f32, kind="Internal").ap()
    build(nc, ins["in_x"], ins["in_w"], ins["in_cols"], ins["in_p"], out, t_scr, g_scr, c_scr)
    r = _run(nc, [arrays], core_ids=[0])
    return np.ascontiguousarray(r.results[0]["out_y"].reshape(D, S).T).reshape(1, S, D)
```

```python
from contextlib import ExitStack

import numpy as np
import concourse.bass as bass
import concourse.mybir as mybir

F32 = mybir.dt.float32
F32R = mybir.dt.float32r
ALU = mybir.AluOpType
ACT = mybir.ActivationFunctionType
AX = mybir.AxisListType.X

P = 128
D = 1024
S = 1024
KT = D // P
HALF = 512
DH = 64
NPAIR = 8
NB = S // P
FFN = 2816
FT = FFN // P
NGRP = FT // 2
PLE_KT = 2
NEG = -1e30
SCALE = DH ** -0.5
ALPHA = 2.0 ** 0.25
RMS_EPS, LN_EPS = 1e-6, 1e-5

U_CONV = 0
U_MIX = U_CONV + 4 * KT
U_SWA = U_MIX + 2 * KT
U_PAIR = U_SWA + 5
U_AOUT = U_PAIR + 3 * NPAIR - 1
U_OUT = U_AOUT + KT
U_F = U_OUT + KT
U_FOX = U_F + 1
U_FOUT = U_FOX + 3 * NPAIR
U_FFN = U_FOUT + 2 * KT
U_PLE = U_FFN + 6 * NGRP
U_GATE = U_PLE + 2
U_END = U_GATE + KT
T_FOUT = U_FOUT
T_FFN = T_FOUT + KT
T_PLE = T_FFN + 12 * NGRP
T_GATE = T_PLE + KT
T_END = T_GATE + KT
O_PLE = T_FFN + 4 * NGRP
O_GATE = O_PLE + KT

C_NORM = 0
C_CONV = C_NORM + KT
C_QG = C_CONV + 3 * KT
C_KG = C_QG + 1
C_GATEB = C_KG + 1
C_FCW = C_GATEB + 2 * KT
C_FCB = C_FCW + 3 * FT
C_LN1G = C_FCB + FT
C_LN1B = C_LN1G + KT
C_LN2G = C_LN1B + KT
C_LN2B = C_LN2G + KT
C_PLEB = C_LN2B + KT
C_BF = C_PLEB + KT
C_SINK = C_BF + 1
N_COLS = C_SINK + 2 * NPAIR


class NormSemaphores:

    def __init__(self, sem, n):
        self.acc = sem(n + "_acc")
        self.mean = sem(n + "_mean")
        self.centred = sem(n + "_centred")
        self.sq = sem(n + "_sq")
        self.sq_used = sem(n + "_sq_used")
        self.std = sem(n + "_std")
        self.rstd = sem(n + "_rstd")
        self.y = sem(n + "_y")
        self.hi = sem(n + "_hi")
        self.lo = sem(n + "_lo")


class AttentionSemaphores:

    def __init__(self, sem, n):
        self.q_sq = sem(n + "_q_sq")
        self.q_ms = sem(n + "_q_ms")
        self.q_std = sem(n + "_q_std")
        self.q_rstd = sem(n + "_q_rstd")
        self.q_n = sem(n + "_q_n")
        self.q_hi = sem(n + "_q_hi")
        self.q_lo = sem(n + "_q_lo")
        self.k_twice = sem(n + "_k_twice")
        self.z_tanh = sem(n + "_z_tanh")
        self.v_flip = sem(n + "_v_flip")
        self.v_hi = sem(n + "_v_hi")
        self.v_lo = sem(n + "_v_lo")
        self.scored = sem(n + "_scored")
        self.max = sem(n + "_max")
        self.neg_max = sem(n + "_neg_max")
        self.exp = sem(n + "_exp")
        self.sink = sem(n + "_sink")
        self.total = sem(n + "_total")
        self.inv = sem(n + "_inv")
        self.prob = sem(n + "_prob")
        self.flipped = sem(n + "_flipped")
        self.hi = sem(n + "_hi")
        self.lo = sem(n + "_lo")
        self.pv = sem(n + "_pv")
        self.fold = sem(n + "_fold")
        self.o = sem(n + "_o")
        self.og = sem(n + "_og")
        self.o_hi = sem(n + "_o_hi")
        self.o_lo = sem(n + "_o_lo")
        self.g_out = sem(n + "_g_out")


STEPS = [(hh, qb) for hh in range(2) for qb in range(NB)]
NST = len(STEPS)
CHUNKS = [(s, b, min(4, qb + 1 - b)) for s, (hh, qb) in enumerate(STEPS) for b in range(0, qb + 1, 4)]
NCH = len(CHUNKS)
CHUNKS_OF = [[n for n, c in enumerate(CHUNKS) if c[0] == s] for s in range(NST)]
FILL = (2,) * 8 + (4, 4) + (2,) * 4 + (4, 4)
PARTS = [range(sum(FILL[:s]), sum(FILL[:s + 1])) for s in range(NST)]
LEAVES = {s + 1: PARTS[s][-1] // 8 for s in range(NST) if PARTS[s][-1] % 8 == 7}
WSTEPS = [(hh, g) for hh in range(2) for g in range(2)]
NW = len(WSTEPS)


def build(nc, xT, weights, cols, pT, out, t_scr, g_scr, c_scr):
    ctx = ExitStack()
    with ctx:
        top = [0]
        base = -(-nc.sbuf_base // 32) * 32

        def fixed(name, shape, dt):
            n = int(np.prod(shape[1:])) * 4
            t = nc.alloc_sbuf_tensor_at(name, [P, *shape[1:]], dt, offset=base + top[0])
            top[0] += -(-n // 32) * 32
            return t

        total = 207 * 1024 + 512

        raw = [fixed(f"raw{b}", [P, HALF], F32) for b in range(2)]
        whi = [fixed(f"whi{s}", [P, KT, P], F32R) for s in range(2)]
        wlo = [fixed(f"wlo{s}", [P, KT, P], F32R) for s in range(2)]
        ident = fixed("ident", [P, P], F32)
        ident_r = fixed("ident_r", [P, P], F32R)
        mask_r = fixed("mask_r", [P, 3 * P], F32R)
        head_mean = fixed("head_mean", [P, P], F32)
        feat_mean = fixed("feat_mean", [P, P], F32)
        cst = fixed("cst", [P, N_COLS], F32)
        eps_rms = fixed("eps_rms", [P, 1], F32)
        eps_ln = fixed("eps_ln", [P, 1], F32)
        shift = fixed("shift", [P, KT], F32)
        half_gate = fixed("half_gate", [P, KT], F32)
        neg_sink = fixed("neg_sink", [P, 2 * NPAIR], F32)
        mx = fixed("mx", [P, 8], F32)
        neg_max = fixed("neg_max", [P, 8], F32)
        row_sum = fixed("row_sum", [P, 8], F32)
        sink_exp = fixed("sink_exp", [P, 8], F32)
        row_inv = fixed("row_inv", [P, 8], F32)
        a_hi_at = top[0]
        a_hi = fixed("a_hi", [P, KT, S], F32R)
        a_lo_at = top[0]
        a_lo = fixed("a_lo", [P, KT, S], F32R)
        b_hi_at = top[0]
        b_hi = fixed("b_hi", [P, KT, S], F32R)
        b_lo_at = top[0]
        b_lo = fixed("b_lo", [P, KT, S], F32R)
        over_at = top[0]

        def overlay(at, *specs):
            top[0] = at
            made = [fixed(*x) for x in specs]
            assert top[0] <= total, (top[0], total)
            return made

        z, sq0, sq1, nrm, acc = overlay(over_at, ("z", [P, KT, S], F32), ("sq0", [P, HALF], F32), ("sq1", [P, HALF], F32),
                                        ("nrm", [P, S], F32), ("acc", [P, S], F32))
        sq = [sq0, sq1]
        (mask_f,) = overlay(b_hi_at, ("mask_f", [P, 3 * P], F32))
        cv_v, cv_u, cv_y, cv_g, cv_o = overlay(over_at, ("cv_v", [P, S], F32), ("cv_u", [P, S + 2], F32),
                                               ("cv_y", [P, S], F32), ("cv_g", [P, S], F32), ("cv_o", [P, S], F32))
        mix_y, mix_g, mix_t = overlay(over_at, ("mix_y", [P, S], F32), ("mix_g", [P, S], F32), ("mix_t", [P, S], F32))
        def psum(name, n):
            return ctx.enter_context(nc.psum_tensor(name, [P, n], F32))

        bank = [psum(f"bank{h}", HALF) for h in range(2)]
        score = [psum(f"score{s}", S) for s in range(2)]
        flip = psum("flip", HALF)
        pv = psum("pv", HALF)
        down_bank = [[score[h][:, m * HALF:(m + 1) * HALF] for m in range(2)] for h in range(2)]
        flips = (flip, bank[1])

        head_rows = (slice(0, DH), slice(DH, P))
        sk00, sk01, sv0, sk10, sk11, sv1 = overlay(
            b_lo_at, *((f"{n}{t}", shape, F32R) for t in range(2) for n, shape in (
                ("sk0", [P, S]), ("sk1", [P, S]), ("sv", [P, NB, 2, P]))))
        s_k, sv = ((sk00, sk01), (sk10, sk11)), (sv0, sv1)
        (s_o,) = overlay(b_hi_at, ("s_o", [P, KT, S], F32))
        (sq0_parts, sq1_parts, sk_lo0, sk_lo1, sp0, sp1, sp_hi, sp_lo, s_z, s_g, s_raw, s_sq, s_fold) = overlay(
            over_at, *((x, [P, S], F32R) for x in ("sq0_parts", "sq1_parts", "sk_lo0", "sk_lo1")),
            ("sp0", [P, S], F32), ("sp1", [P, S], F32),
            ("sp_hi", [P, S], F32R), ("sp_lo", [P, S], F32R),
            ("s_z", [P, S], F32), ("s_g", [P, S], F32), ("s_raw", [P, S], F32), ("s_sq", [P, S], F32),
            ("s_fold", [P, HALF], F32))
        early = [s_o[:, j, :] for j in range(KT)]
        v_flips = [[score[1][:, h * HALF:(h + 1) * HALF] for h in range(2)], [flip[:], bank[1][:]]]
        s_q, sk_lo, sp = (sq0_parts, sq1_parts), (sk_lo0, sk_lo1), (sp0, sp1)
        m_t0, m_t1, m_g0, m_g1, m_m = overlay(over_at, ("m_t0", [P, S], F32), ("m_t1", [P, S], F32),
                                              ("m_g0", [P, S], F32), ("m_g1", [P, S], F32), ("m_m", [P, S], F32))
        x_in0, x_in1, x_sum = overlay(over_at + 20 * 1024, ("x_in0", [P, S], F32), ("x_in1", [P, S], F32),
                                      ("x_sum", [P, S], F32))
        fq1_even, fk1_even, fk_lo_even, fq0, fk0, fq1_odd, fk1_odd, fk_lo_odd = overlay(
            a_lo_at, *((x, [P, S], F32R) for x in ("fq1_even", "fk1_even", "fk_lo_even", "fq0", "fk0",
                                                   "fq1_odd", "fk1_odd", "fk_lo_odd")))
        f_q, f_k = ((fq0, fq1_even), (fq0, fq1_odd)), ((fk0, fk1_even), (fk0, fk1_odd))
        f_klo = (fk_lo_even, fk_lo_odd)
        (f_o,) = overlay(a_hi_at, ("f_o", [P, KT, S], F32))
        fv, fp0, fp1, fp2, fp_hi, fp_lo, fc0, fc1, f_fold, f_raw = overlay(
            over_at, ("fv", [P, NB, 2, P], F32R), ("fp0", [P, S], F32), ("fp1", [P, S], F32),
            ("fp2", [P, S], F32), ("fp_hi", [P, NB, 2, P], F32R), ("fp_lo", [P, NB, 2, P], F32R), ("fc0", [P, S], F32), ("fc1", [P, S], F32),
            ("f_fold", [P, HALF], F32), ("f_raw", [P, S], F32))
        fp, fc = (fp0, fp1, fp2), (fc0, fc1)
        *_, up_y, up_o, up_u, up_g = overlay(
            over_at, ("z_again", [P, KT, S], F32), ("sq_again", [P, 2 * HALF], F32), ("up_y", [P, S], F32),
            ("up_o", [P, S], F32), ("up_u", [P, S], F32), ("up_g", [P, S + 2], F32))
        (ple,) = overlay(b_hi_at, ("ple", [P, KT, S], F32))
        p_raw, p_hi, p_lo, g_sig, g_out = overlay(
            b_lo_at, ("p_raw", [P, PLE_KT, S], F32), ("p_hi", [P, PLE_KT, S], F32R), ("p_lo", [P, PLE_KT, S], F32R),
            ("g_sig", [P, S], F32), ("g_out", [P, S], F32))

        def sem(name):
            return ctx.enter_context(nc.semaphore(name))

        cols_in = sem("cols_in")
        mean_made = sem("mean_made")
        const_made = sem("const_made")
        raw_in = [sem(f"raw_in{b}") for b in range(2)]
        w_hi = sem("w_hi")
        w_lo = sem("w_lo")
        tile_done = [sem(f"tile_done{h}") for h in range(2)]
        tile_out = [sem(f"tile_out{h}") for h in range(2)]

        n0, n1, n2 = NormSemaphores(sem, "n0"), NormSemaphores(sem, "n1"), NormSemaphores(sem, "n2")
        sw, fx = AttentionSemaphores(sem, "sw"), AttentionSemaphores(sem, "fx")
        conv_step = sem("conv_step")
        conv_o = sem("conv_o")
        conv_hi = sem("conv_hi")
        conv_lo = sem("conv_lo")
        mix_done = sem("mix_done")
        t_stored = sem("t_stored")
        mt_in = [sem(f"mt_in{s}") for s in range(2)]
        mg_in = [sem(f"mg_in{s}") for s in range(2)]
        m_sum = sem("m_sum")
        m_hi = sem("m_hi")
        m_lo = sem("m_lo")
        x_in = [sem(f"x_in_{s}") for s in range(2)]
        x_hi = sem("x_hi")
        x_lo = sem("x_lo")
        f_step = sem("f_step")
        c_stored = sem("c_stored")
        c_in = [sem(f"c_in{h}") for h in range(2)]
        z_part = sem("z_part")
        ffn_pad = sem("ffn_pad")
        up_conv = sem("up_conv")
        up_gelu = sem("up_gelu")
        up_prod = sem("up_prod")
        up_hi = sem("up_hi")
        up_lo = sem("up_lo")
        down_out = [sem(f"down_out{h}") for h in range(2)]
        z_alpha = sem("z_alpha")
        xT_in = [[sem(f"xT_in{h}_{j}") for j in range(KT)] for h in range(2)]
        shift_made = sem("shift_made")
        half_made = sem("half_made")
        p_in = sem("p_in")
        ple_hi = sem("ple_hi")
        ple_lo = sem("ple_lo")
        g_done = sem("g_done")
        g_sum = sem("g_sum")
        out_stored = sem("out_stored")

        passed = sem("passed")

        def settler(engine):
            def settle():
                engine.sem_inc(passed, 1)
            return settle

        block = ctx.enter_context(nc.Block())

        def hs(h):
            return slice(h * HALF, (h + 1) * HALF)

        def col(c):
            return cst[:, bass.ds(c, 1)] if not isinstance(c, int) else cst[:, c:c + 1]

        @block.sync
        def _(sp):
            for j in range(KT):
                sp.dma_start(z[:, j, hs(0)], xT[j, :, hs(0)]).then_inc(xT_in[0][j], 16)
            for b in range(2):
                sp.dma_start(raw[b][:], weights[0, :, hs(b)]).then_inc(raw_in[b], 16)
            for j in range(KT):
                sp.dma_start(z[:, j, hs(1)], xT[j, :, hs(1)]).then_inc(xT_in[1][j], 16)
            with sp.Fori(1, U_END) as u:
                for b in range(2):
                    sp.wait_ge(w_lo, u * 2 + (b - 1))
                    sp.dma_start(raw[b][:], weights[u, :, hs(b)]).then_inc(raw_in[b], 16)

        @block.gpsimd
        def _(pool):
            nc.gpsimd.memset(feat_mean[:], 1.0 / D).then_inc(mean_made, 1)
            nc.gpsimd.memset(eps_rms[:], RMS_EPS).then_inc(mean_made, 1)
            nc.gpsimd.memset(eps_ln[:], LN_EPS).then_inc(mean_made, 1)
            nc.gpsimd.memset(ident[:], 0.0).then_inc(const_made, 1)
            nc.gpsimd.memset(mask_f[:], 0.0).then_inc(const_made, 1)
            nc.gpsimd.memset(head_mean[:], 0.0).then_inc(const_made, 1)
            pool.wait_ge(const_made, 3)
            nc.gpsimd.memset(mask_f[:, 2 * P:3 * P], NEG).then_inc(const_made, 1)
            nc.gpsimd.affine_select(out=ident[:], in_=ident[:], compare_op=ALU.not_equal, fill=1.0, base=0,
                                    pattern=[[-1, P]], channel_multiplier=1).then_inc(const_made, 1)
            nc.gpsimd.affine_select(out=mask_f[:, 0:P], in_=mask_f[:, 0:P], compare_op=ALU.is_gt, fill=NEG, base=0,
                                    pattern=[[1, P]], channel_multiplier=-1).then_inc(const_made, 1)
            nc.gpsimd.affine_select(out=mask_f[:, P:2 * P], in_=mask_f[:, P:2 * P], compare_op=ALU.is_ge, fill=NEG,
                                    base=0, pattern=[[-1, P]], channel_multiplier=1).then_inc(const_made, 1)
            pool.wait_ge(const_made, 7)
            for h in range(2):
                nc.gpsimd.memset(head_mean[h * DH:(h + 1) * DH, h * DH:(h + 1) * DH], 1.0 / DH).then_inc(const_made, 1)
            pool.wait_ge(const_made, 9)
            nc.gpsimd.tensor_scalar(ident_r[:], ident[:], 1.0, 1.0, ALU.mult, ALU.mult).then_inc(const_made, 1)
            nc.gpsimd.tensor_scalar(mask_r[:], mask_f[:], 1.0, 1.0, ALU.mult, ALU.mult).then_inc(const_made, 1)

            settle = settler(pool)

            def split(u, slot, done, freed):
                for b in range(2):
                    if done is not None and b == 0:
                        pool.wait_ge(done, freed)
                    pool.wait_ge(raw_in[b], u * 16 + 16)
                    settle()
                    hi, lo = whi[slot][:, 4 * b:4 * b + 4, :], wlo[slot][:, 4 * b:4 * b + 4, :]
                    src = raw[b][:].rearrange("p (k c) -> p k c", c=P)
                    nc.gpsimd.tensor_scalar(hi, src, 1.0, 1.0, ALU.mult, ALU.mult).then_inc(w_hi, 1)
                    pool.wait_ge(w_hi, u * 2 + (b + 1))
                    nc.gpsimd.tensor_tensor(lo, src, hi.bitcast(F32), ALU.subtract).then_inc(w_lo, 1)

            split(0, 0, None, 0)
            split(1, 1, None, 0)
            assert (U_FOUT + 2 - 2) % 2 == 1
            with pool.Fori(0, (U_FOUT - 1) // 2) as it:
                for c in range(2):
                    split(it * 2 + (2 + c), c, tile_done[1], it * 2 + (1 + c))
            split(U_FOUT + 1, (U_FOUT + 1) % 2, tile_done[1], U_FOUT)
            with pool.Fori(0, KT) as it:
                for c in range(2):
                    u = U_FOUT + 2 + c
                    split(it * 2 + u, u % 2, tile_done[c], it + (T_FOUT + 1))
            for c in range(2):
                u = U_FFN + 2 + c
                split(u, u % 2, tile_done[1], T_FFN + 1 + c)
            u = U_FFN + 4
            split(u, u % 2, tile_done[1], T_FFN + 3)
            freed = (0, 1, 2, 3, 4, 8)
            with pool.Fori(0, NGRP - 1) as it:
                for c in range(6):
                    split(it * 6 + (U_FFN + 5 + c), (U_FFN + 5 + c) % 2, tile_done[1], it * 12 + (T_FFN + 4 + freed[c]))
            t = T_FFN + 4 + 12 * (NGRP - 1)
            for c, freed in enumerate((t, t + 4, t + 8)):
                u = U_PLE - 1 + c
                split(u, u % 2, tile_done[1], freed)
            for c in range(KT):
                u = U_GATE + c
                split(u, u % 2, tile_done[1], (T_PLE + 4, T_PLE + 8)[c] if c < 2 else T_GATE + c - 1)

        @block.tensor
        def _(pe):
            def product(psum_ap, w, hi, lo, kts, wk, h, first=True, final=True):
                n = len(kts)
                for i, (kt, k) in enumerate(zip(kts, wk)):
                    for j, (ws, a) in enumerate(((whi, hi), (whi, lo), (wlo, hi))):
                        last = nc.tensor.matmul(psum_ap, ws[w][:, k, :], a[:, kt, hs(h)],
                                                start=(first and i == 0 and j == 0), stop=(final and i == n - 1 and j == 2))
                return last

            def tile(u, before, slot, hi, lo):
                pe.wait_ge(w_lo, u * 2 + 2)
                for h in range(2):
                    pe.wait_ge(tile_out[h], before)
                    product(bank[h][:], slot, hi, lo, range(KT), range(KT), h).then_inc(tile_done[h], 1)

            def down_tiles(u, group, q, slot, kts):
                pe.wait_ge(w_lo, u * 2 + 2)
                for m in range(4 * q, 4 * q + 4):
                    for h in range(2):
                        pe.wait_ge(down_out[h], group * KT + max(m - 1, 0))
                        product(down_bank[h][m % 2], slot, a_hi, a_lo, kts, (2 * (m % 4), 2 * (m % 4) + 1),
                                h).then_inc(tile_done[h], 1)

            def mean(ns, h):
                pe.wait_ge(ns.acc, h * KT + KT)
                nc.tensor.matmul(score[0][:, hs(h)], feat_mean[:], acc[:, hs(h)], start=True, stop=True).then_inc(ns.mean, 1)

            def squares(ns, h, tiles):
                for j in tiles:
                    i = h * KT + j
                    pe.wait_ge(ns.sq, i + 1)
                    nc.tensor.matmul(score[1][:, hs(h)], feat_mean[:], sq[i % 2][:], start=(j == 0),
                                     stop=(j == KT - 1)).then_inc(ns.sq_used, 1)

            def half(u, before, slot, hi, lo, h, ready, per_k=1, per_half=KT):
                pe.wait_ge(w_lo, u * 2 + 2)
                pe.wait_ge(tile_out[h], before)
                for k in range(KT):
                    pe.wait_ge(ready, h * per_half + k * per_k + 1)
                    last = product(bank[h][:], slot, hi, lo, [k], [k], h, k == 0, k == KT - 1)
                last.then_inc(tile_done[h], 1)

            def mean_square(n, h, dst, square):
                pe.wait_ge(sw.q_sq, n * 2 + (h + 1))
                nc.tensor.matmul(dst, head_mean[:], square[:, hs(h)], start=True, stop=True).then_inc(sw.q_ms, 1)

            def flip_v(at, dst, src, h, ready):
                pe.wait_ge(tile_out[h], ready)
                for b in range(4):
                    last = nc.tensor.transpose(dst[:, b * P:(b + 1) * P],
                                               src[:, (4 * h + b) * P:(4 * h + b + 1) * P], ident[:])
                last.then_inc(at.v_flip, 1)

            def part(u, t, slot, h, k, hi, lo, b=0, two_banks=False):
                if k == 0:
                    if b:
                        pe.wait_ge(tile_out[1], t)
                    elif h == 0:
                        pe.wait_ge(w_lo, u * 2 + 2)
                        pe.wait_ge(tile_out[0], t)
                        if not two_banks:
                            pe.wait_ge(tile_out[1], t)
                    else:
                        pe.wait_ge(tile_out[0], t + 1)
                for j, (ws, a) in enumerate(((whi, hi), (whi, lo), (wlo, hi))):
                    last = nc.tensor.matmul(bank[b][:], ws[slot][:, k, :], a[:, k, hs(h)],
                                            start=(k == 0 and j == 0), stop=(k == KT - 1 and j == 2))
                if k == KT - 1:
                    last.then_inc(tile_done[h], 1)

            def window_pair(it, pp):
                last_pair = isinstance(it, int) and it * 2 + pp == NPAIR - 1
                st = it * (2 * NW) + pp * NW
                u0 = U_PAIR + 3 * pp
                n = it * 2 + (pp + 3)
                v = sv[pp]

                def fill(c, h):
                    if last_pair and c == 0:
                        return
                    back = 1 if last_pair else 0
                    u = it * 6 + (u0 + c - back)
                    if c == 1 and h == 0 and not last_pair:
                        pe.wait_ge(sw.q_std, n * 2 + 2)
                    for k in range(KT):
                        part(u, u, (u0 + c - back) % 2, h, k, a_hi, a_lo)

                def scores(s):
                    hh, g = WSTEPS[s]
                    rows = head_rows[hh]
                    pe.wait_ge(sw.exp, st * 4 + 4 * max(s - 1, 0))
                    for j in range(4):
                        qb = 4 * g + j
                        q = slice(qb * P, (qb + 1) * P)
                        c = j * 2 * P
                        if qb == 0:
                            nc.tensor.matmul(score[s % 2][:, 0:P], ident_r[:], mask_r[:, 2 * P:3 * P], start=True, stop=True)
                            ks, dst, mask = slice(0, P), score[s % 2][:, P:2 * P], mask_r[:, P:2 * P]
                        else:
                            ks, dst = slice((qb - 1) * P, (qb + 1) * P), score[s % 2][:, c:c + 2 * P]
                            mask = mask_r[:, 0:2 * P]
                        nc.tensor.matmul(dst, s_q[hh][:, q], s_k[pp][hh][:, ks], start=True, stop=False)
                        nc.tensor.matmul(dst, ident_r[:], mask, start=False, stop=False)
                        mm = nc.tensor.matmul(dst, s_q[hh][rows, q], sk_lo[pp][rows, ks], start=False, stop=True)
                    mm.then_inc(sw.scored, 1)

                def flip_p(s):
                    for c in range(2):
                        if c == 0:
                            pe.wait_ge(sw.prob, st + (s + 1))
                        pe.wait_ge(sw.lo, st * 2 + (2 * s + c - 1) if s or c else st * 2)
                        for b in range(4):
                            mm = nc.tensor.transpose(flips[c][:, b * P:(b + 1) * P],
                                                     sp[s % 2][:, (4 * c + b) * P:(4 * c + b + 1) * P], ident[:])
                        mm.then_inc(sw.flipped, 1)

                def values(s):
                    hh, g = WSTEPS[s]
                    pe.wait_ge(sw.o, st + s)
                    for i, (j, n, own) in enumerate(((0, 2, 1), (2, 2, 1), (1, 2, 1), (0, 1, 0), (3, 1, 1))):
                        blk = 4 * g + j - 1 + own
                        if i in (0, 1):
                            pe.wait_ge(sw.lo, st * 2 + (2 * s + i + 1))
                        if blk < 0:
                            continue
                        b = 2 * j + own
                        for pt in (sp_hi, sp_lo):
                            mm = nc.tensor.matmul(pv[:, j * P:(j + n) * P], v[:, blk, hh, :], pt[:, b * P:(b + n) * P],
                                                  start=(i == 0 and pt is sp_hi), stop=(i == 4 and pt is sp_lo))
                    mm.then_inc(sw.pv, 1)

                pe.wait_ge(sw.q_lo, it * 4 + (2 * pp + 6))
                pe.wait_ge(sw.k_twice, 2 * pp + 2)
                scores(0)
                pe.wait_ge(sw.v_lo, 4)
                scores(1)
                fill(0, 0)
                if last_pair:
                    fill(1, 0)
                flip_p(0)
                fill(0, 1)
                scores(2)
                values(0)
                flip_p(1)
                if not last_pair:
                    pe.wait_ge(tile_out[1], it * 6 + (u0 + 1))
                    mean_square(n, 0, bank[0][:], s_sq)
                scores(3)
                if not last_pair:
                    pe.wait_ge(sw.q_std, n * 2 + 1)
                    mean_square(n, 1, bank[0][:], s_sq)
                values(1)
                if not last_pair:
                    fill(1, 0)
                flip_p(2)
                fill(1, 1)
                values(2)
                fill(2, 0)
                flip_p(3)
                fill(2, 1)
                values(3)

            def forget_part(it, pp, i, two_banks=False):
                u = U_FOX + 3 * pp + i // 16
                part(it * 6 + u, it * 6 + u, u % 2, i // 8 % 2, i % 8, b_hi, b_lo,
                     i // 8 % 2 if two_banks else 0, two_banks)

            def forget_pair(it, pp, fills):
                st, ch, gr = it * (2 * NST) + pp * NST, it * (2 * NCH) + pp * NCH, it * 8 + 4 * pp

                def scores(s):
                    hh, qb = STEPS[s]
                    rows = head_rows[hh]
                    q = slice(qb * P, (qb + 1) * P)
                    w = (qb + 1) * P
                    pe.wait_ge(fx.max, st + max(s - 1, 0))
                    for c in range(0, w, HALF):
                        n = min(HALF, w - c)
                        ks = slice(c, c + n)
                        dst = score[s % 2][:, ks]
                        nc.tensor.matmul(dst, f_q[pp][hh][:, q], f_k[pp][hh][:, ks], start=True, stop=False)
                        if c + n == w:
                            nc.tensor.matmul(score[s % 2][:, w - P:w], ident_r[:], mask_r[:, P:2 * P], start=False, stop=False)
                        mm = nc.tensor.matmul(dst, f_q[pp][hh][rows, q], f_klo[pp][rows, ks], start=False, stop=True)
                    mm.then_inc(fx.scored, 1)

                def flip_p(s):
                    for i, n in enumerate(CHUNKS_OF[s]):
                        blk, nb = CHUNKS[n][1:]
                        if i == 0:
                            pe.wait_ge(fx.prob, st + (s + 1))
                        if n < 2:
                            pe.wait_ge(fx.v_lo, it * 4 + (2 * pp + n + 1))
                        else:
                            pe.wait_ge(fx.lo, ch + (n - 1))
                        for b in range(nb):
                            mm = nc.tensor.transpose(flips[n % 2][:, b * P:(b + 1) * P],
                                                     fp[s % 3][:, (blk + b) * P:(blk + b + 1) * P], ident[:])
                        mm.then_inc(fx.flipped, 1)

                def values(s):
                    hh, qb = STEPS[s]
                    c = (qb - 1) % 4 * P
                    pe.wait_ge(fx.lo, ch + (CHUNKS_OF[s][-1] + 1))
                    if c == 0:
                        pe.wait_ge(fx.o, gr + s // 4)
                    for i, blk in enumerate([0, qb, *range(1, qb)]):
                        for pt in (fp_hi, fp_lo):
                            cols = slice(P if blk == qb else 0, 2 * P)
                            mm = nc.tensor.matmul(pv[:, c + cols.start:c + 2 * P], fv[:, blk, hh, :],
                                                  pt[:, blk, 1 if blk == qb else 0:2, :],
                                                  start=(i == 0 and pt is fp_hi),
                                                  stop=(pt is fp_lo and i == qb))
                    mm.then_inc(fx.pv, 1)

                for h in range(2):
                    pe.wait_ge(tile_out[h], it * 6 + (U_FOX + 3 * pp + 2))
                pe.wait_ge(fx.q_lo, it * 8 + (4 * pp + 4))
                pe.wait_ge(fx.k_twice, it * 8 + (4 * pp + 4))
                scores(0)
                scores(1)
                for i in range(40, 48):
                    forget_part(it, pp, i)
                for h in range(2):
                    pe.wait_ge(fx.lo, ch)
                    flip_v(fx, flips[h], f_raw, h, it * 6 + (U_FOX + 3 * pp + 3))
                scores(2)
                for s in range(NST):
                    flip_p(s)
                    if s and s % 2 == 0:
                        values(s - 1)
                    if s + 3 < NST:
                        scores(s + 3)
                    if fills:
                        for i in PARTS[s]:
                            forget_part(it if pp == 0 else it + 1, 1 - pp, i)
                values(NST - 1)

            pe.wait_ge(mean_made, 3)
            for h in range(2):
                squares(n0, h, range(KT))
            for h in range(2):
                for c in range(2):
                    half(c, c, c, a_hi, a_lo, h, n0.lo)
            for c in (2, 3):
                tile(c, c, c % 2, a_hi, a_lo)
            with pe.Fori(1, KT) as i:
                for c in range(4):
                    tile(i * 4 + c, i * 4 + c, c % 2, a_hi, a_lo)
            with pe.Fori(0, KT) as j:
                for c, (hi, lo) in enumerate(((a_hi, a_lo), (b_hi, b_lo))):
                    if c == 1:
                        pe.wait_ge(conv_lo, 2 * KT)
                    tile(j * 2 + (U_MIX + c), j * 2 + (U_MIX + c), c, hi, lo)
            pe.wait_ge(const_made, 11)
            for c in range(5):
                u = U_SWA + c
                tile(u, u, u % 2, a_hi, a_lo)
                if 1 <= c <= 3:
                    for h in range(2):
                        if c > 1:
                            pe.wait_ge(sw.q_std, 2 * (c - 1))
                        mean_square(c - 1, h, score[0][:, hs(h)], early[2 * c - 1])
            for t in range(2):
                for h in range(2):
                    flip_v(sw, v_flips[t][h], early[6 + t], h, U_SWA + 4 + t)
            with pe.Fori(0, NPAIR // 2 - 1) as it:
                for pp in range(2):
                    window_pair(it, pp)
            for pp in range(2):
                window_pair(NPAIR // 2 - 1, pp)
            pe.wait_ge(tile_out[1], U_AOUT)
            for h in range(2):
                half(U_AOUT, U_AOUT, U_AOUT % 2, b_lo, b_hi, h, sw.o_lo, 1, 0)
            tile(U_AOUT + 1, U_AOUT + 1, (U_AOUT + 1) % 2, b_lo, b_hi)
            with pe.Fori(1, KT // 2) as j:
                for c in range(2):
                    tile(j * 2 + (U_AOUT + c), j * 2 + (U_AOUT + c), (U_AOUT + c) % 2, b_lo, b_hi)
            for h in range(2):
                half(U_OUT, U_OUT, U_OUT % 2, a_hi, a_lo, h, m_lo, 2, 1)
            tile(U_OUT + 1, U_OUT + 1, (U_OUT + 1) % 2, a_hi, a_lo)
            with pe.Fori(1, KT // 2) as j:
                for c in range(2):
                    tile(j * 2 + (U_OUT + c), j * 2 + (U_OUT + c), (U_OUT + c) % 2, a_hi, a_lo)
            for h in range(2):
                half(U_F, U_F, U_F % 2, b_hi, b_lo, h, x_lo, 2, 1)
            for i in range(40):
                forget_part(0, 0, i, True)
            with pe.Fori(0, NPAIR // 2 - 1) as it:
                for pp in range(2):
                    forget_pair(it, pp, True)
            for pp in range(2):
                forget_pair(NPAIR // 2 - 1, pp, pp == 0)
            pe.wait_ge(tile_out[1], U_FOUT)
            def out_half(j, i, c, h):
                pe.wait_ge(w_lo, (i + U_FOUT) * 2 + 2)
                pe.wait_ge(tile_out[c], j + (T_FOUT + h * KT // 2))
                product(bank[c][:], (U_FOUT + c) % 2, a_lo, a_hi, range(KT), range(KT), h).then_inc(tile_done[c], 1)

            half(U_FOUT, T_FOUT, U_FOUT % 2, a_lo, a_hi, 0, fx.o_lo)
            out_half(0, 1, 1, 0)
            with pe.Fori(1, KT // 2) as it:
                for c in range(2):
                    out_half(it, it * 2 + c, c, 0)
            for j in range(KT):
                out_half(j // 2, KT + j, j % 2, 1)
                if j == 0:
                    mean(n1, 0)
                elif j <= 4:
                    squares(n1, 0, (2 * j - 2, 2 * j - 1))
            mean(n1, 1)
            def up(u, before):
                for c in range(4):
                    tile(u + c, before + c, (U_FFN + c) % 2, b_hi, b_lo)

            def down(u, group, parity, seen):
                pe.wait_ge(up_lo, seen)
                for q in range(2):
                    down_tiles(u + q, group, q, (U_FFN + q) % 2, (2 * parity, 2 * parity + 1))

            half(U_FFN, T_FFN, U_FFN % 2, b_hi, b_lo, 0, n1.lo)
            squares(n1, 1, range(KT))
            half(U_FFN + 1, T_FFN + 1, (U_FFN + 1) % 2, b_hi, b_lo, 0, n1.lo)
            for c in range(2):
                half(U_FFN + c, T_FFN + c, (U_FFN + c) % 2, b_hi, b_lo, 1, n1.lo)
            for c in (2, 3):
                tile(U_FFN + c, T_FFN + c, (U_FFN + c) % 2, b_hi, b_lo)
            with pe.Fori(0, (NGRP - 1) // 2) as it:
                for g in range(2):
                    u = U_FFN + 4 + 6 * g
                    up(it * 12 + u, it * 8 + (T_FFN + 4 + 4 * g))
                    down(it * 12 + (u + 4), it * 2 + g, g, it * 8 + 4 * (g + 1))
            pe.wait_ge(up_lo, 4 * NGRP)
            pe.wait_ge(w_lo, U_PLE * 2)
            kts = (2 * ((NGRP - 1) % 2), 2 * ((NGRP - 1) % 2) + 1)
            for h in range(2):
                for m in range(KT):
                    pe.wait_ge(down_out[h], (NGRP - 1) * KT + max(m - 1, 0))
                    product(down_bank[h][m % 2], (U_PLE - 2 + m // 4) % 2, a_hi, a_lo, kts, (2 * (m % 4), 2 * (m % 4) + 1),
                            h).then_inc(tile_done[h], 1)
                    if h == 1 and m == 1:
                        mean(n2, 0)
            pe.wait_ge(ple_lo, PLE_KT)

            def ple_tile(m):
                u = U_PLE + m // 4
                if m % 4 == 0:
                    pe.wait_ge(w_lo, u * 2 + 2)
                for h in range(2):
                    pe.wait_ge(tile_out[h], O_PLE + m)
                    product(bank[h][:], u % 2, p_hi, p_lo, range(PLE_KT), (2 * (m % 4), 2 * (m % 4) + 1),
                            h).then_inc(tile_done[h], 1)

            ple_tile(0)
            mean(n2, 1)
            ple_tile(1)
            pe.wait_ge(down_out[1], NGRP * KT)
            squares(n2, 0, range(KT))
            squares(n2, 1, range(KT))
            for m in range(2, KT):
                ple_tile(m)
            for h in range(2):
                half(U_GATE, O_GATE, U_GATE % 2, a_hi, a_lo, h, n2.lo)
            for j in range(1, KT):
                tile(U_GATE + j, O_GATE + j, (U_GATE + j) % 2, a_hi, a_lo)

        @block.scalar
        def _(act):
            settle = settler(act)

            act.dma_start(cst[:], cols).then_inc(cols_in, 16)

            def square(ns, h, j, mean):
                i = h * KT + j
                if mean:
                    act.wait_ge(ns.centred, i + 1)
                else:
                    act.wait_ge(xT_in[h][j], 16)
                if i >= 2:
                    act.wait_ge(ns.sq_used, i - 1)
                nc.scalar.activation(sq[i % 2][:], z[:, j, hs(h)], ACT.Square).then_inc(ns.sq, 1)

            def root(ns, h, eps):
                log_mean_square(ns, h, eps)
                one_over(ns, h)

            def log_mean_square(ns, h, eps):
                act.wait_ge(ns.sq_used, (h + 1) * KT)
                act.wait_ge(mean_made, 3)
                nc.scalar.activation(nrm[:, hs(h)], score[1][:, hs(h)], ACT.Ln, bias=eps[:]).then_inc(ns.std, 1)

            def one_over(ns, h):
                act.wait_ge(ns.std, h + 1)
                nc.scalar.activation(nrm[:, hs(h)], nrm[:, hs(h)], ACT.Exp, scale=-0.5).then_inc(ns.rstd, 1)

            def norm_hi(ns, h, j, hi, bias):
                i = h * KT + j
                act.wait_ge(ns.y, i + 1)
                if bias is None:
                    nc.scalar.activation(hi[:, j, hs(h)], z[:, j, hs(h)], ACT.Copy).then_inc(ns.hi, 1)
                else:
                    nc.scalar.activation(hi[:, j, hs(h)], z[:, j, hs(h)], ACT.Identity, bias=col(bias + j)).then_inc(ns.hi, 1)

            def copy_tile(dst, t):
                for h in range(2):
                    act.wait_ge(tile_done[h], t + 1)
                    nc.scalar.activation(dst[:, hs(h)], bank[h][:], ACT.Copy).then_inc(tile_out[h], 1)

            def v_hi(at, v, src, h, n):
                act.wait_ge(at.v_flip, n + 1)
                nc.scalar.activation(v[:, 4 * h:4 * h + 4, :, 0:DH],
                                     src.rearrange("p (b h d) -> p b h d", h=2, d=DH), ACT.Copy).then_inc(at.v_hi, 1)

            def raw_and_square(src, t, n, h, raw, square):
                act.wait_ge(tile_done[h], t + 1)
                nc.scalar.activation(raw[:, hs(h)], src[:], ACT.Copy).then_inc(tile_out[h], 1)
                act.wait_ge(tile_out[h], t + 1)
                nc.scalar.activation(square[:, hs(h)], raw[:, hs(h)], ACT.Square).then_inc(sw.q_sq, 1)

            def log_mean(src, n, h, square):
                act.wait_ge(sw.q_ms, n * 2 + (h + 1))
                nc.scalar.activation(square[:, hs(h)], src, ACT.Ln, bias=eps_rms[:]).then_inc(sw.q_std, 1)

            def one_over_root(n, square):
                for h in range(2):
                    act.wait_ge(sw.q_std, n * 2 + (h + 1))
                    settle()
                    nc.scalar.activation(square[:, hs(h)], square[:, hs(h)], ACT.Exp, scale=-0.5).then_inc(sw.q_rstd, 1)

            def normed_hi(dst, n, raw):
                act.wait_ge(sw.q_n, n + 1)
                for hh, rows in enumerate(head_rows):
                    nc.scalar.activation(dst[hh][rows, :], raw[rows, :], ACT.Copy).then_inc(sw.q_hi, 1)

            def keys_twice(t):
                for hh, rows in enumerate(head_rows):
                    act.wait_ge(sw.q_hi, 2 * t + hh + 1)
                    nc.scalar.activation(s_k[t][hh][head_rows[1 - hh], :], s_k[t][hh][rows, :].bitcast(F32),
                                         ACT.Copy).then_inc(sw.k_twice, 1)

            def window_hi(j):
                act.wait_ge(sw.og, 3 * j + 3)
                act.wait_ge(sw.pv, NW * (NPAIR - 1 if j < 4 else NPAIR))
                nc.scalar.activation(b_lo[:, j, :], s_o[:, j, :], ACT.Copy).then_inc(sw.o_hi, 1)

            def window_pair(it, pp):
                last_pair = isinstance(it, int) and it * 2 + pp == NPAIR - 1
                st = it * (2 * NW) + pp * NW
                pair = it * 2 + pp
                u0 = U_PAIR + 3 * pp - (1 if last_pair else 0)
                n = it * 2 + (pp + 3)

                def expo(s):
                    hh, g = WSTEPS[s]
                    act.wait_ge(sw.flipped, st * 2 + max(2 * s - 2, 0))
                    act.wait_ge(sw.neg_max, st + (s + 1))
                    for j in range(4):
                        cols = slice(j * 2 * P, (j + 1) * 2 * P)
                        one = slice(4 * (s % 2) + j, 4 * (s % 2) + j + 1)
                        nc.scalar.activation(sp[s % 2][:, cols], score[s % 2][:, cols], ACT.Exp, bias=neg_max[:, one],
                                             scale=SCALE, accum_out=row_sum[:, one]).then_inc(sw.exp, 1)
                    four = slice(4 * (s % 2), 4 * (s % 2) + 4)
                    settle()
                    nc.scalar.activation(sink_exp[:, four], neg_max[:, four], ACT.Exp,
                                         bias=col(it * 4 + (2 * pp + hh + C_SINK))).then_inc(sw.sink, 1)

                def high(s):
                    for c in range(2):
                        act.wait_ge(sw.pv, st + s)
                        act.wait_ge(sw.flipped, st * 2 + (2 * s + c + 1))
                        nc.scalar.activation(sp_hi[:, hs(c)], flips[c][:], ACT.Copy).then_inc(sw.hi, 1)

                def fold(s):
                    act.wait_ge(sw.o, st + s)
                    act.wait_ge(sw.pv, st + (s + 1))
                    nc.scalar.activation(s_fold[0:DH, :], pv[DH:P, :], ACT.Copy).then_inc(sw.fold, 1)

                def query(h):
                    if not last_pair:
                        raw_and_square(bank[0], it * 6 + u0, n, h, s_raw, s_sq)

                def gate_a(h):
                    act.wait_ge(tile_done[h], it * 6 + (u0 + 2))
                    nc.scalar.activation(s_z[:, hs(h)], bank[0][:], ACT.Tanh, scale=0.5).then_inc(sw.z_tanh, 1)

                def gate_b(h):
                    act.wait_ge(tile_done[h], it * 6 + (u0 + 3))
                    settle()
                    nc.scalar.activation(s_g[:, hs(h)], bank[0][:], ACT.Tanh, scale=0.5,
                                         bias=half_gate[:, bass.ds(pair, 1)]).then_inc(tile_out[h], 1)

                expo(0)
                query(0)
                expo(1)
                if last_pair:
                    act.wait_ge(sw.og, it * 6 + 3 * pp)
                    gate_a(0)
                high(0)
                if last_pair:
                    window_hi(0)
                    window_hi(1)
                query(1)
                fold(0)
                high(1)
                if not last_pair:
                    for h in range(2):
                        log_mean(bank[0][:], n, h, s_sq)
                    one_over_root(n, s_sq)
                expo(2)
                fold(1)
                if last_pair:
                    window_hi(2)
                    window_hi(3)
                if not last_pair:
                    act.wait_ge(sw.og, it * 6 + 3 * pp)
                    gate_a(0)
                high(2)
                expo(3)
                gate_a(1)
                fold(2)
                if not last_pair:
                    normed_hi(s_q, n, s_raw)
                act.wait_ge(sw.g_out, it * 32 + 16 * pp)
                gate_b(0)
                high(3)
                gate_b(1)
                for h in range(2):
                    act.wait_ge(tile_out[h], it * 6 + (u0 + 3))
                act.dma_start(g_scr[pair, :, :], s_g[:]).then_inc(sw.g_out, 16)
                fold(3)

            def forget_out(it, pp, i, src=bank[0]):
                c, h = i // 2, i % 2
                act.wait_ge(tile_done[h], it * 6 + (U_FOX + 3 * pp + c + 1))
                if c < 2:
                    x = (f_q, f_k)[c][pp]
                    for hh, rows in enumerate(head_rows):
                        nc.scalar.activation(x[hh][rows, hs(h)], src[rows, :], ACT.Copy).then_inc(fx.q_hi, 1)
                    if c == 1:
                        for hh, rows in enumerate(head_rows):
                            act.wait_ge(fx.q_hi, it * 16 + (8 * pp + 2 * i + hh + 1))
                            nc.scalar.activation(x[hh][head_rows[1 - hh], hs(h)], x[hh][rows, hs(h)].bitcast(F32),
                                                 ACT.Copy).then_inc(fx.k_twice, 1)
                else:
                    nc.scalar.activation(f_raw[:, hs(h)], src[:], ACT.Copy).then_inc(tile_out[h], 1)

            def sums_in(it, pp, hh):
                row = bass.ds(it * 4 + (2 * pp + hh), 1)
                act.dma_start(fc[hh][:], c_scr[row, :].partition_broadcast(P)).then_inc(c_in[hh], 16)

            def forget_hi(j):
                act.wait_ge(fx.o, 4 * (NPAIR - 1 if j < 4 else NPAIR))
                nc.scalar.activation(a_lo[:, j, :], f_o[:, j, :], ACT.Copy).then_inc(fx.o_hi, 1)

            def forget_pair(it, pp, fills):
                st, ch, gr = it * (2 * NST) + pp * NST, it * (2 * NCH) + pp * NCH, it * 8 + 4 * pp
                following = (it, 1) if pp == 0 else (it + 1, 0)

                def expo(s):
                    w = (STEPS[s][1] + 1) * P
                    one = slice(s % 4, s % 4 + 1)
                    act.wait_ge(fx.neg_max, st + (s + 1))
                    nc.scalar.activation(fp[s % 3][:, 0:w], fp[s % 3][:, 0:w], ACT.Exp, bias=neg_max[:, one],
                                         accum_out=row_sum[:, one]).then_inc(fx.exp, 1)

                def normalise(s):
                    w = (STEPS[s][1] + 1) * P
                    act.wait_ge(fx.inv, st + (s + 1))
                    nc.scalar.activation(fp[s % 3][:, 0:w], fp[s % 3][:, 0:w], ACT.Copy,
                                         scale=row_inv[:, s % 4:s % 4 + 1]).then_inc(fx.prob, 1)

                def high(n):
                    s, blk, nb = CHUNKS[n]
                    if s % 2 == 0:
                        act.wait_ge(fx.pv, it * 16 + (8 * pp + s // 2))
                    act.wait_ge(fx.flipped, ch + (n + 1))
                    nc.scalar.activation(fp_hi[:, blk:blk + nb, s % 2, :],
                                         flips[n % 2][:, 0:nb * P].rearrange("p (b c) -> p b c", c=P),
                                         ACT.Copy).then_inc(fx.hi, 1)

                def fold(s):
                    act.wait_ge(fx.o, gr + s // 4)
                    act.wait_ge(fx.pv, it * 16 + (8 * pp + (s + 1) // 2))
                    nc.scalar.activation(f_fold[0:DH, :], pv[DH:P, :], ACT.Copy).then_inc(fx.fold, 1)

                expo(0)
                normalise(0)
                expo(1)
                forget_out(it, pp, 5)
                act.wait_ge(fx.pv, it * 16 + 8 * pp)
                for h in range(2):
                    v_hi(fx, fv, flips[h][:], h, it * 4 + (2 * pp + h))
                for s in range(NST):
                    if fills and s in LEAVES:
                        forget_out(*following, LEAVES[s])
                    if s + 1 < NST:
                        normalise(s + 1)
                    if s and s % 4 == 0:
                        fold(s - 1)
                    for n in CHUNKS_OF[s]:
                        high(n)
                    if s + 2 < NST:
                        expo(s + 2)
                    if not fills and s in (0, 1, 2, 9):
                        forget_hi(min(s, 3))
                    if fills and s == NST - 1:
                        forget_out(*following, 4)
                    if fills and s in (9, 15):
                        act.wait_ge(fx.max, st + (8 if s == 9 else 16))
                        sums_in(*following, s // 15)
                fold(NST - 1)

            for j in range(KT):
                square(n0, 0, j, False)
            root(n0, 0, eps_rms)
            act.wait_ge(cols_in, 16)
            for j in range(KT):
                square(n0, 1, j, False)
                norm_hi(n0, 0, j, a_hi, None)
            root(n0, 1, eps_rms)

            def copy_half(dst, t, h):
                act.wait_ge(tile_done[h], t + 1)
                nc.scalar.activation(dst[:, hs(h)], bank[h][:], ACT.Copy).then_inc(tile_out[h], 1)

            act.wait_ge(n0.y, KT + 1)
            copy_half(cv_v, 0, 0)
            for j in range(KT):
                norm_hi(n0, 1, j, a_hi, None)
            copy_half(cv_v, 0, 1)

            def conv_tile(i):
                for h in range(2):
                    act.wait_ge(tile_done[h], i * 4 + 4)
                    nc.scalar.activation(cv_g[:, hs(h)], bank[h][:], ACT.Silu).then_inc(tile_out[h], 1)
                for h in range(2):
                    act.wait_ge(conv_o, i * 2 + (h + 1))
                    settle()
                    nc.scalar.activation(b_hi[:, i, hs(h)], cv_o[:, hs(h)], ACT.Copy).then_inc(conv_hi, 1)

            conv_tile(0)
            with act.Fori(1, KT) as i:
                act.wait_ge(conv_o, i * 2)
                copy_tile(cv_v, i * 4)
                conv_tile(i)
            act.wait_ge(conv_lo, 2 * KT)
            with act.Fori(0, KT) as j:
                act.wait_ge(mix_done, j * 2)
                for h in range(2):
                    act.wait_ge(tile_done[h], j * 2 + (U_MIX + 1))
                    settle()
                    nc.scalar.activation(mix_g[:, hs(h)], bank[h][:], ACT.Sigmoid,
                                         bias=col(j + C_GATEB)).then_inc(tile_out[h], 1)
                copy_tile(mix_y, j * 2 + (U_MIX + 1))
                act.wait_ge(mix_done, j * 2 + 2)
                act.dma_start(t_scr[j, :, :], mix_t[:]).then_inc(t_stored, 16)
            act.wait_ge(t_stored, 16 * KT)
            def early_square(c):
                for h in range(2):
                    raw_and_square(bank[h], U_SWA + c, c, h, early[2 * c], early[2 * c + 1])

            def early_root(c):
                for h in range(2):
                    log_mean(score[0][:, hs(h)], c, h, early[2 * c + 1])
                one_over_root(c, early[2 * c + 1])

            early_square(0)
            early_square(1)
            early_root(0)
            early_square(2)
            normed_hi(s_k[0], 0, early[0])
            early_root(1)
            copy_tile(early[6], U_SWA + 3)
            normed_hi(s_k[1], 1, early[2])
            keys_twice(0)
            early_root(2)
            normed_hi(s_q, 2, early[4])
            copy_tile(early[7], U_SWA + 4)
            for t in range(2):
                for h in range(2):
                    v_hi(sw, sv[t], v_flips[t][h], h, 2 * t + h)
            keys_twice(1)
            act.wait_ge(half_made, 1)
            with act.Fori(0, NPAIR // 2 - 1) as it:
                for pp in range(2):
                    act.wait_ge(sw.q_lo, it * 4 + (2 * pp + 6))
                    window_pair(it, pp)
            for pp in range(2):
                act.wait_ge(sw.q_lo, 2 * (NPAIR + 1 + pp))
                window_pair(NPAIR // 2 - 1, pp)
            for j in range(4, NPAIR):
                window_hi(j)
            act.wait_ge(sw.g_out, 16 * NPAIR)
            act.wait_ge(sw.o_lo, NPAIR)
            m_t, m_g = (m_t0, m_t1), (m_g0, m_g1)
            for s in range(2):
                act.dma_start(m_t[s][:], t_scr[s, :, :]).then_inc(mt_in[s], 16)
                act.dma_start(m_g[s][:], g_scr[s, :, :]).then_inc(mg_in[s], 16)

            def merged_hi(j):
                for h in range(2):
                    act.wait_ge(m_sum, j * 2 + (h + 1))
                    settle()
                    nc.scalar.activation(a_hi[:, j, hs(h)], m_m[:, hs(h)], ACT.Copy).then_inc(m_hi, 1)

            with act.Fori(0, KT // 2 - 1) as it:
                for c in range(2):
                    merged_hi(it * 2 + c)
                    act.dma_start(m_t[c][:], t_scr[it * 2 + (2 + c), :, :]).then_inc(mt_in[c], 16)
                    act.dma_start(m_g[c][:], g_scr[it * 2 + (2 + c), :, :]).then_inc(mg_in[c], 16)
            for j in (KT - 2, KT - 1):
                merged_hi(j)
            x_ins = (x_in0, x_in1)
            for s in range(2):
                act.dma_start(x_ins[s][:], xT[s, :, :]).then_inc(x_in[s], 16)

            def layer_hi(j):
                for h in range(2):
                    act.wait_ge(tile_out[h], j + (U_OUT + 1))
                    settle()
                    nc.scalar.activation(b_hi[:, j, hs(h)], x_sum[:, hs(h)], ACT.Copy).then_inc(x_hi, 1)

            with act.Fori(0, KT // 2 - 1) as it:
                for c in range(2):
                    layer_hi(it * 2 + c)
                    act.dma_start(x_ins[c][:], xT[it * 2 + (2 + c), :, :]).then_inc(x_in[c], 16)
            for j in (KT - 2, KT - 1):
                layer_hi(j)
            act.wait_ge(x_lo, 2 * KT)
            for h in range(2):
                act.wait_ge(tile_done[h], U_F + 1)
                nc.scalar.activation(fp0[0:16, hs(h)], bank[h][0:16, :], ACT.Identity,
                                     bias=cst[0:16, C_BF:C_BF + 1]).then_inc(tile_out[h], 1)
            for h in range(2):
                act.wait_ge(tile_out[h], U_F + 1)
            nc.scalar.activation(fp1[0:16, :], fp0[0:16, :], ACT.Abs).then_inc(f_step, 1)
            act.wait_ge(f_step, 1)
            nc.scalar.activation(fp1[0:16, :], fp1[0:16, :], ACT.Exp, scale=-1.0).then_inc(f_step, 1)
            act.wait_ge(f_step, 2)
            nc.scalar.activation(fp1[0:16, :], fp1[0:16, :], ACT.Ln, bias=1.0).then_inc(f_step, 1)
            forget_out(0, 0, 0)
            act.wait_ge(f_step, 6)
            act.dma_start(c_scr, fp1[0:16, :]).then_inc(c_stored, 16)
            forget_out(0, 0, 1, bank[1])
            act.wait_ge(c_stored, 16)
            for hh in range(2):
                sums_in(0, 0, hh)
            for i in range(2, 5):
                forget_out(0, 0, i, bank[i % 2])
            with act.Fori(0, NPAIR // 2 - 1) as it:
                for pp in range(2):
                    forget_pair(it, pp, True)
            for pp in range(2):
                forget_pair(NPAIR // 2 - 1, pp, pp == 0)
            for j in range(4, NPAIR):
                forget_hi(j)
            def gate_half(t, c, h):
                act.wait_ge(tile_done[h], t + (2 * c + 2))
                nc.scalar.activation(up_g[:, 2 + h * HALF:2 + (h + 1) * HALF], bank[h][:], ACT.Copy).then_inc(tile_out[h], 1)

            for h in range(2):
                for j in range(KT):
                    square(n1, h, j, True)
                if h == 1:
                    act.wait_ge(n1.lo, KT)
                    copy_half(up_u, T_FFN, 0)
                root(n1, h, eps_ln)
                if h == 1:
                    act.wait_ge(ffn_pad, 1)
                    gate_half(T_FFN, 0, 0)
                for j in range(KT):
                    norm_hi(n1, h, j, b_hi, C_LN1B)
            copy_half(up_u, T_FFN, 1)
            gate_half(T_FFN, 0, 1)

            def residual(tiles):
                act.wait_ge(shift_made, 1)
                for j in tiles:
                    act.wait_ge(n1.lo, KT + j + 1)
                    nc.scalar.activation(z[:, j, :], z[:, j, :], ACT.Identity, scale=ALPHA, bias=shift[:, j:j + 1]).then_inc(z_alpha, 1)

            def up(t, n, parity):
                for c in range(2):
                    if not isinstance(n, int) or c:
                        act.wait_ge(up_prod, (n + c) * 2)
                        copy_tile(up_u, t + 2 * c)
                        for h in range(2):
                            gate_half(t, c, h)
                    act.wait_ge(up_conv, (n + c) * 3 + 3)
                    nc.scalar.activation(up_y[:], up_y[:], ACT.Gelu).then_inc(up_gelu, 1)
                    for h in range(2):
                        act.wait_ge(up_prod, (n + c) * 2 + (h + 1))
                        nc.scalar.activation(a_hi[:, 2 * parity + c, hs(h)], up_o[:, hs(h)], ACT.Copy).then_inc(up_hi, 1)
                    if isinstance(n, int):
                        residual(range(3, 6) if c == 0 else range(6, KT))

            residual(range(3))
            up(T_FFN, 0, 0)
            with act.Fori(0, (NGRP - 1) // 2) as it:
                for g in range(2):
                    up(it * 24 + (T_FFN + 4 + 12 * g), it * 4 + (2 * g + 2), (g + 1) % 2)
            act.wait_ge(up_lo, 2 * FT)
            for k in range(PLE_KT):
                act.dma_start(p_raw[:, k, :], pT[k, :, :]).then_inc(p_in, 16)
            act.wait_ge(p_in, 16 * PLE_KT)
            for k in range(PLE_KT):
                nc.scalar.activation(p_hi[:, k, :], p_raw[:, k, :], ACT.Copy).then_inc(ple_hi, 1)
            for j in range(KT):
                square(n2, 0, j, True)
                if j == 1:
                    for m in range(2):
                        copy_tile(ple[:, m, :], T_PLE + m)
            for j in range(KT):
                square(n2, 1, j, True)
            for h in range(2):
                log_mean_square(n2, h, eps_ln)
            for h in range(2):
                one_over(n2, h)
            for j in range(KT):
                if j % 2 == 0:
                    copy_tile(ple[:, 2 + j // 2, :], T_PLE + 2 + j // 2)
                norm_hi(n2, 0, j, a_hi, C_LN2B)
            for j in range(KT):
                if j in (0, 2):
                    copy_tile(ple[:, 6 + j // 2, :], T_PLE + 6 + j // 2)
                norm_hi(n2, 1, j, a_hi, C_LN2B)
            for j in range(KT):
                for h in range(2):
                    if j:
                        act.wait_ge(g_done, 2 * j - 1 + h)
                    act.wait_ge(tile_done[h], T_GATE + j + 1)
                    nc.scalar.activation(g_sig[:, hs(h)], bank[h][:], ACT.Sigmoid, bias=col(C_PLEB + j)).then_inc(tile_out[h], 1)
                act.wait_ge(g_sum, 2 * j + 2)
                act.dma_start(out[j, :, :], g_out[:]).then_inc(out_stored, 16)
            act.wait_ge(out_stored, 16 * KT)

        @block.vector
        def _(dve):
            v = nc.vector

            settle = settler(dve)

            def centre(ns, h, j):
                dve.wait_ge(ns.mean, h + 1)
                v.tensor_tensor(z[:, j, hs(h)], z[:, j, hs(h)], score[0][:, hs(h)], ALU.subtract).then_inc(ns.centred, 1)

            def scaled(ns, h, j, gain):
                dve.wait_ge(ns.rstd, h + 1)
                dve.wait_ge(ns.sq, h * KT + j + 1)
                v.scalar_tensor_tensor(z[:, j, hs(h)], z[:, j, hs(h)], col(gain + j), nrm[:, hs(h)], ALU.mult,
                                       ALU.mult).then_inc(ns.y, 1)

            def norm_lo(ns, h, j, hi, lo, bias):
                dve.wait_ge(ns.hi, h * KT + j + 1)
                if bias is None:
                    v.tensor_tensor(lo[:, j, hs(h)], z[:, j, hs(h)], hi[:, j, hs(h)].bitcast(F32),
                                    ALU.subtract).then_inc(ns.lo, 1)
                else:
                    v.scalar_tensor_tensor(lo[:, j, hs(h)], z[:, j, hs(h)], col(bias + j), hi[:, j, hs(h)].bitcast(F32),
                                           ALU.add, ALU.subtract).then_inc(ns.lo, 1)

            def scaled_and_lo(ns, h, hi, lo, gain, bias, tiles):
                for j in tiles:
                    if j == 0:
                        scaled(ns, h, 0, gain)
                    if j + 1 < KT:
                        scaled(ns, h, j + 1, gain)
                    norm_lo(ns, h, j, hi, lo, bias)

            def v_lo(at, dst, src, h, n):
                dve.wait_ge(at.v_hi, n + 1)
                v.tensor_tensor(dst[:, 4 * h:4 * h + 4, :, DH:P], src.rearrange("p (b h d) -> p b h d", h=2, d=DH),
                                dst[:, 4 * h:4 * h + 4, :, 0:DH].bitcast(F32), ALU.subtract).then_inc(at.v_lo, 1)

            def normed(n, gain, raw, square):
                dve.wait_ge(sw.q_rstd, n * 2 + 2)
                v.scalar_tensor_tensor(raw[:], raw[:], col(gain), square[:], ALU.mult, ALU.mult).then_inc(sw.q_n, 1)

            def normed_lo(n, hi, raw, lo=None):
                for hh, rows in enumerate(head_rows):
                    dve.wait_ge(sw.q_hi, n * 2 + (hh + 1))
                    dst = hi[hh][head_rows[1 - hh], :] if lo is None else lo[rows, :]
                    v.tensor_tensor(dst, raw[rows, :], hi[hh][rows, :].bitcast(F32), ALU.subtract).then_inc(sw.q_lo, 1)

            def window_lo(j):
                dve.wait_ge(sw.o_hi, j + 1)
                v.tensor_tensor(b_hi[:, j, :], s_o[:, j, :], b_lo[:, j, :].bitcast(F32), ALU.subtract).then_inc(sw.o_lo, 1)

            def window_pair(it, pp):
                last_pair = isinstance(it, int) and it * 2 + pp == NPAIR - 1
                st = it * (2 * NW) + pp * NW
                pair = it * 2 + pp
                u0 = U_PAIR + 3 * pp - (1 if last_pair else 0)
                n = it * 2 + (pp + 3)

                def maxima(s):
                    hh, g = WSTEPS[s]
                    four = slice(4 * (s % 2), 4 * (s % 2) + 4)
                    dve.wait_ge(sw.scored, st + (s + 1))
                    v.reduce_max(mx[:, four], score[s % 2][:].rearrange("p (j k) -> p j k", j=4), AX).then_inc(sw.max, 1)
                    dve.wait_ge(sw.max, st + (s + 1))
                    v.tensor_scalar(neg_max[:, four], mx[:, four], -SCALE, neg_sink[:, bass.ds(it * 4 + (2 * pp + hh), 1)],
                                    ALU.mult, ALU.min).then_inc(sw.neg_max, 1)

                def normalise(s):
                    four = slice(4 * (s % 2), 4 * (s % 2) + 4)
                    dve.wait_ge(sw.sink, st + (s + 1))
                    dve.wait_ge(sw.exp, st * 4 + (4 * s + 4))
                    v.tensor_tensor(row_sum[:, four], row_sum[:, four], sink_exp[:, four], ALU.add).then_inc(sw.total, 1)
                    dve.wait_ge(sw.total, st + (s + 1))
                    v.reciprocal(row_inv[:, four], row_sum[:, four]).then_inc(sw.inv, 1)
                    dve.wait_ge(sw.inv, st + (s + 1))
                    p4 = sp[s % 2][:].rearrange("p (j k) -> p j k", j=4)
                    v.tensor_tensor(p4, p4, row_inv[:, four].unsqueeze(2).to_broadcast([P, 4, 2 * P]),
                                    ALU.mult).then_inc(sw.prob, 1)

                def low(s):
                    for c in range(2):
                        dve.wait_ge(sw.hi, st * 2 + (2 * s + c + 1))
                        v.tensor_tensor(sp_lo[:, hs(c)], flips[c][:], sp_hi[:, hs(c)].bitcast(F32), ALU.subtract).then_inc(sw.lo, 1)

                def add(s):
                    hh, g = WSTEPS[s]
                    dve.wait_ge(sw.fold, st + (s + 1))
                    v.tensor_tensor(s_o[hh * DH:(hh + 1) * DH, pair, hs(g)], pv[0:DH, :], s_fold[0:DH, :],
                                    ALU.add).then_inc(sw.o, 1)

                def gate(h):
                    dve.wait_ge(sw.z_tanh, it * 4 + (2 * pp + h + 1))
                    v.scalar_tensor_tensor(s_z[:, hs(h)], s_z[:, hs(h)], 1.0, bank[0][:], ALU.add, ALU.mult).then_inc(tile_out[h], 1)

                def gated(rows, cols, steps):
                    dve.wait_ge(sw.o, st + steps)
                    for h in range(2):
                        dve.wait_ge(tile_out[h], it * 6 + (u0 + 2))
                    v.scalar_tensor_tensor(s_o[rows, pair, cols], s_o[rows, pair, cols], 0.5, s_z[rows, cols], ALU.mult,
                                           ALU.mult).then_inc(sw.og, 1)

                maxima(0)
                normalise(0)
                maxima(1)
                if last_pair:
                    gate(0)
                low(0)
                normalise(1)
                if last_pair:
                    window_lo(0)
                    window_lo(1)
                add(0)
                maxima(2)
                low(1)
                normalise(2)
                if not last_pair:
                    gate(0)
                add(1)
                maxima(3)
                if not last_pair:
                    normed(n, C_QG, s_raw, s_sq)
                low(2)
                normalise(3)
                gate(1)
                add(2)
                if last_pair:
                    window_lo(2)
                    window_lo(3)
                else:
                    normed_lo(n, s_q, s_raw)
                gated(head_rows[0], slice(0, S), 2)
                gated(head_rows[1], hs(0), 3)
                low(3)
                add(3)
                gated(head_rows[1], hs(1), 4)

            def forget_out(it, pp, i, src=bank[0]):
                c, h = i // 2, i % 2
                if c < 2:
                    for hh, rows in enumerate(head_rows):
                        x = (f_q, f_k)[c][pp][hh]
                        dst = f_klo[pp][rows, hs(h)] if c else x[head_rows[1 - hh], hs(h)]
                        dve.wait_ge(fx.q_hi, it * 16 + (8 * pp + 2 * i + hh + 1))
                        v.tensor_tensor(dst, src[rows, :], x[rows, hs(h)].bitcast(F32),
                                        ALU.subtract).then_inc(tile_out[h] if hh else fx.q_lo, 1)

            def forget_lo(j):
                dve.wait_ge(fx.o_hi, j + 1)
                v.tensor_tensor(a_hi[:, j, :], f_o[:, j, :], a_lo[:, j, :].bitcast(F32), ALU.subtract).then_inc(fx.o_lo, 1)

            def forget_pair(it, pp, fills):
                st, ch, gr = it * (2 * NST) + pp * NST, it * (2 * NCH) + pp * NCH, it * 8 + 4 * pp
                following = (it, 1) if pp == 0 else (it + 1, 0)

                def maxima(s):
                    hh, qb = STEPS[s]
                    w = (qb + 1) * P
                    one = slice(s % 4, s % 4 + 1)
                    if qb == 0:
                        dve.wait_ge(c_in[hh], it * 32 + (16 * pp + 16))
                    dve.wait_ge(fx.flipped, ch + (CHUNKS_OF[s - 3][-1] + 1 if s >= 3 else 0))
                    dve.wait_ge(fx.scored, st + (s + 1))
                    settle()
                    v.tensor_tensor_reduce(out=fp[s % 3][:, 0:w], in0=score[s % 2][:, 0:w], in1=fc[hh][:, 0:w],
                                           scale=SCALE, scalar=-3.0e38, op0=ALU.subtract, op1=ALU.max,
                                           accum_out=mx[:, one]).then_inc(fx.max, 1)
                    dve.wait_ge(fx.max, st + (s + 1))
                    v.tensor_scalar(neg_max[:, one], mx[:, one], -1.0, None, ALU.mult).then_inc(fx.neg_max, 1)

                def inverse(s):
                    one = slice(s % 4, s % 4 + 1)
                    dve.wait_ge(fx.exp, st + (s + 1))
                    v.reciprocal(row_inv[:, one], row_sum[:, one]).then_inc(fx.inv, 1)

                def low(n):
                    s, blk, nb = CHUNKS[n]
                    dve.wait_ge(fx.hi, ch + (n + 1))
                    v.tensor_tensor(fp_lo[:, blk:blk + nb, s % 2, :],
                                    flips[n % 2][:, 0:nb * P].rearrange("p (b c) -> p b c", c=P),
                                    fp_hi[:, blk:blk + nb, s % 2, :].bitcast(F32), ALU.subtract).then_inc(fx.lo, 1)

                def add(s):
                    hh, qb = STEPS[s]
                    dve.wait_ge(fx.fold, gr + (s // 4 + 1))
                    v.tensor_tensor(f_o[hh * DH:(hh + 1) * DH, it * 2 + pp, hs(qb // 4)], pv[0:DH, :],
                                    f_fold[0:DH, :], ALU.add).then_inc(fx.o, 1)

                maxima(0)
                inverse(0)
                maxima(1)
                inverse(1)
                for h in range(2):
                    v_lo(fx, fv, flips[h][:], h, it * 4 + (2 * pp + h))
                for s in range(NST):
                    if fills and s in LEAVES:
                        forget_out(*following, LEAVES[s])
                    if s + 2 < NST:
                        maxima(s + 2)
                    if s and s % 4 == 0:
                        add(s - 1)
                    for n in CHUNKS_OF[s]:
                        low(n)
                    if s + 2 < NST:
                        inverse(s + 2)
                    if not fills and s in (0, 1, 2, 9):
                        forget_lo(min(s, 3))
                add(NST - 1)

            dve.wait_ge(cols_in, 16)
            v.tensor_scalar(half_gate[:], cst[:, C_GATEB + KT:C_GATEB + 2 * KT], 0.5, None, ALU.mult).then_inc(half_made, 1)
            v.tensor_scalar(shift[:], cst[:, C_LN1B:C_LN1B + KT], ALPHA, None, ALU.mult).then_inc(shift_made, 1)
            v.tensor_scalar(neg_sink[:], cst[:, C_SINK:C_SINK + 2 * NPAIR], -1.0, None, ALU.mult).then_inc(conv_step, 1)
            for h in range(2):
                scaled_and_lo(n0, h, a_hi, a_lo, C_NORM, None, range(KT))
            dve.wait_ge(n0.lo, 2 * KT)
            v.memset(cv_u[:, 0:2], 0.0).then_inc(conv_step, 1)
            with dve.Fori(0, KT) as i:
                for h in range(2):
                    dve.wait_ge(tile_out[h], i * 4 + 1)
                    dve.wait_ge(tile_done[h], i * 4 + 2)
                    v.tensor_tensor(cv_u[:, 2 + h * HALF:2 + (h + 1) * HALF], bank[h][:], cv_v[:, hs(h)],
                                    ALU.mult).then_inc(tile_out[h], 1)
                for h in range(2):
                    dve.wait_ge(tile_out[h], i * 4 + 2)
                v.tensor_scalar(cv_y[:], cv_u[:, 0:S], col(i * 3 + C_CONV), None, ALU.mult).then_inc(conv_step, 1)
                for k in (1, 2):
                    dve.wait_ge(conv_step, i * 3 + (2 + k))
                    v.scalar_tensor_tensor(cv_y[:], cv_u[:, k:k + S], col(i * 3 + (C_CONV + k)), cv_y[:], ALU.mult,
                                           ALU.add).then_inc(conv_step, 1)
                dve.wait_ge(conv_step, i * 3 + 5)
                for h in range(2):
                    dve.wait_ge(tile_done[h], i * 4 + 3)
                    v.tensor_tensor(cv_y[:, hs(h)], bank[h][:], cv_y[:, hs(h)], ALU.mult).then_inc(tile_out[h], 1)
                for h in range(2):
                    dve.wait_ge(tile_out[h], i * 4 + 4)
                    v.tensor_tensor(cv_o[:, hs(h)], cv_y[:, hs(h)], cv_g[:, hs(h)], ALU.mult).then_inc(conv_o, 1)
                for h in range(2):
                    dve.wait_ge(conv_hi, i * 2 + (h + 1))
                    v.tensor_tensor(b_lo[:, i, hs(h)], cv_o[:, hs(h)], b_hi[:, i, hs(h)].bitcast(F32),
                                    ALU.subtract).then_inc(conv_lo, 1)
            with dve.Fori(0, KT) as j:
                dve.wait_ge(t_stored, j * 16)
                for h in range(2):
                    dve.wait_ge(tile_out[h], j * 2 + (U_MIX + 2))
                    v.tensor_tensor(mix_t[:, hs(h)], mix_y[:, hs(h)], mix_g[:, hs(h)], ALU.mult).then_inc(mix_done, 1)
            for c, (gain, hi, lo) in enumerate(((C_KG, s_k[0], sk_lo[0]), (C_KG, s_k[1], sk_lo[1]), (C_QG, s_q, None))):
                normed(c, gain, early[2 * c], early[2 * c + 1])
                normed_lo(c, hi, early[2 * c], lo)
            for t in range(2):
                for h in range(2):
                    v_lo(sw, sv[t], v_flips[t][h], h, 2 * t + h)
            with dve.Fori(0, NPAIR // 2 - 1) as it:
                for pp in range(2):
                    window_pair(it, pp)
            for pp in range(2):
                window_pair(NPAIR // 2 - 1, pp)
            for j in range(4, NPAIR):
                window_lo(j)
            m_t, m_g = (m_t0, m_t1), (m_g0, m_g1)
            with dve.Fori(0, KT // 2) as it:
                for c in range(2):
                    dve.wait_ge(mg_in[c], it * 16 + 16)
                    dve.wait_ge(mt_in[c], it * 16 + 16)
                    dve.wait_ge(m_lo, it * 4 + 2 * c)
                    for h in range(2):
                        dve.wait_ge(tile_done[h], it * 2 + (U_AOUT + c + 1))
                        v.scalar_tensor_tensor(m_m[:, hs(h)], m_g[c][:, hs(h)], 1.0, bank[h][:], ALU.add,
                                               ALU.mult).then_inc(tile_out[h], 1)
                    for h in range(2):
                        dve.wait_ge(tile_out[h], it * 2 + (U_AOUT + c + 1))
                        v.scalar_tensor_tensor(m_m[:, hs(h)], m_m[:, hs(h)], 0.5, m_t[c][:, hs(h)], ALU.mult,
                                               ALU.add).then_inc(m_sum, 1)
                    for h in range(2):
                        dve.wait_ge(m_hi, it * 4 + (2 * c + h + 1))
                        v.tensor_tensor(a_lo[:, it * 2 + c, hs(h)], m_m[:, hs(h)], a_hi[:, it * 2 + c, hs(h)].bitcast(F32),
                                        ALU.subtract).then_inc(m_lo, 1)
            x_ins = (x_in0, x_in1)
            with dve.Fori(0, KT // 2) as it:
                for c in range(2):
                    dve.wait_ge(x_in[c], it * 16 + 16)
                    dve.wait_ge(x_lo, it * 4 + 2 * c)
                    for h in range(2):
                        dve.wait_ge(tile_done[h], it * 2 + (U_OUT + c + 1))
                        v.tensor_tensor(x_sum[:, hs(h)], bank[h][:], x_ins[c][:, hs(h)], ALU.add).then_inc(tile_out[h], 1)
                    for h in range(2):
                        dve.wait_ge(x_hi, it * 4 + (2 * c + h + 1))
                        v.tensor_tensor(b_lo[:, it * 2 + c, hs(h)], x_sum[:, hs(h)], b_hi[:, it * 2 + c, hs(h)].bitcast(F32),
                                        ALU.subtract).then_inc(x_lo, 1)
            forget_out(0, 0, 0)
            dve.wait_ge(f_step, 3)
            v.tensor_scalar(fp0[0:16, :], fp0[0:16, :], 0.0, None, ALU.min).then_inc(f_step, 1)
            dve.wait_ge(f_step, 4)
            v.tensor_tensor_scan(fp0[0:16, :], fp0[0:16, :], fp1[0:16, :], 0.0, ALU.add, ALU.subtract).then_inc(f_step, 1)
            dve.wait_ge(f_step, 5)
            v.tensor_scalar(fp1[0:16, :], fp0[0:16, :], 1.0 / SCALE, None, ALU.mult).then_inc(f_step, 1)
            forget_out(0, 0, 1, bank[1])
            dve.wait_ge(c_stored, 16)
            for i in range(2, 4):
                forget_out(0, 0, i, bank[i % 2])
            with dve.Fori(0, NPAIR // 2 - 1) as it:
                for pp in range(2):
                    forget_pair(it, pp, True)
            for pp in range(2):
                forget_pair(NPAIR // 2 - 1, pp, pp == 0)
            for j in range(4, NPAIR):
                forget_lo(j)
            dve.wait_ge(fx.o_lo, NPAIR)
            v.memset(acc[:], 0.0).then_inc(z_part, 1)
            v.memset(up_g[:, 0:2], 0.0).then_inc(ffn_pad, 1)

            def out_half(j, i, c, h, summed):
                done = T_FOUT + h * KT // 2 + 1
                dve.wait_ge(tile_done[c], i + done)
                v.scalar_tensor_tensor(z[:, j, hs(h)], b_hi[:, j, hs(h)].bitcast(F32), ALPHA, bank[c][:], ALU.mult,
                                       ALU.add).then_inc(tile_out[c], 1)
                dve.wait_ge(tile_out[c], i + done)
                v.scalar_tensor_tensor(z[:, j, hs(h)], b_lo[:, j, hs(h)].bitcast(F32), ALPHA, z[:, j, hs(h)], ALU.mult,
                                       ALU.add).then_inc(z_part, 1)
                dve.wait_ge(z_part, summed + 2)
                dve.wait_ge(n1.acc, summed)
                v.tensor_tensor(acc[:, hs(h)], acc[:, hs(h)], z[:, j, hs(h)], ALU.add).then_inc(n1.acc, 1)

            with dve.Fori(0, KT // 2) as it:
                for c in range(2):
                    out_half(it * 2 + c, it, c, 0, it * 2 + c)
            for j in range(KT):
                out_half(j, j // 2, j % 2, 1, KT + j)
                if j < 4:
                    for k in (2 * j, 2 * j + 1):
                        centre(n1, 0, k)
                else:
                    scaled_and_lo(n1, 0, b_hi, b_lo, C_LN1G, C_LN1B, (2 * j - 8, 2 * j - 7))
            for j in range(KT):
                centre(n1, 1, j)
            scaled_and_lo(n1, 1, b_hi, b_lo, C_LN1G, C_LN1B, range(KT))

            def convolved(before, n, c):
                f = n + c
                for h in range(2):
                    dve.wait_ge(tile_out[h], before + (2 * c + 2))
                v.tensor_scalar(up_y[:], up_g[:, 0:S], col(f * 3 + C_FCW), col(f + C_FCB), ALU.mult,
                                ALU.add).then_inc(up_conv, 1)
                for k in (1, 2):
                    dve.wait_ge(up_conv, f * 3 + k)
                    v.scalar_tensor_tensor(up_y[:], up_g[:, k:k + S], col(f * 3 + (C_FCW + k)), up_y[:], ALU.mult,
                                           ALU.add).then_inc(up_conv, 1)

            def gated(n, c, parity):
                f = n + c
                dve.wait_ge(up_gelu, f + 1)
                for h in range(2):
                    v.tensor_tensor(up_o[:, hs(h)], up_y[:, hs(h)], up_u[:, hs(h)], ALU.mult).then_inc(up_prod, 1)
                for h in range(2):
                    dve.wait_ge(up_hi, f * 2 + (h + 1))
                    v.tensor_tensor(a_lo[:, 2 * parity + c, hs(h)], up_o[:, hs(h)],
                                    a_hi[:, 2 * parity + c, hs(h)].bitcast(F32), ALU.subtract).then_inc(up_lo, 1)

            def down(t, m):
                for h in range(2):
                    dve.wait_ge(tile_done[h], t + (m + 1))
                    v.tensor_tensor(z[:, m, hs(h)], z[:, m, hs(h)], down_bank[h][m % 2], ALU.add).then_inc(down_out[h], 1)

            for c in range(2):
                convolved(T_FFN, 0, c)
                gated(0, c, 0)
            dve.wait_ge(z_alpha, KT)
            with dve.Fori(0, (NGRP - 1) // 2) as it:
                for g in range(2):
                    n = it * 4 + (2 * g + 2)
                    before = it * 8 + (T_FFN + 4 + 4 * g)
                    t = it * 24 + (T_FFN + 8 + 12 * g)
                    convolved(before, n, 0)
                    gated(n, 0, (g + 1) % 2)
                    convolved(before, n, 1)
                    for m in range(2):
                        down(t, m)
                    gated(n, 1, (g + 1) % 2)
                    for m in range(2, KT):
                        down(t, m)
            dve.wait_ge(up_lo, 2 * FT)
            for h in range(2):
                for m in range(KT):
                    dve.wait_ge(tile_done[h], T_PLE - KT + m + 1)
                    v.tensor_tensor(z[:, m, hs(h)], z[:, m, hs(h)], down_bank[h][m % 2], ALU.add).then_inc(down_out[h], 1)
                    dve.wait_ge(down_out[h], (NGRP - 1) * KT + m + 1)
                    if m:
                        dve.wait_ge(n2.acc, h * KT + m)
                        v.tensor_tensor(acc[:, hs(h)], acc[:, hs(h)], z[:, m, hs(h)], ALU.add).then_inc(n2.acc, 1)
                    else:
                        v.tensor_copy(acc[:, hs(h)], z[:, m, hs(h)]).then_inc(n2.acc, 1)
                if h == 0:
                    for k in range(PLE_KT):
                        dve.wait_ge(ple_hi, k + 1)
                        v.tensor_tensor(p_lo[:, k, :], p_raw[:, k, :], p_hi[:, k, :].bitcast(F32),
                                        ALU.subtract).then_inc(ple_lo, 1)
            for h in range(2):
                for j in range(KT):
                    centre(n2, h, j)
            for h in range(2):
                scaled_and_lo(n2, h, a_hi, a_lo, C_LN2G, C_LN2B, range(KT))
            for j in range(KT):
                if j:
                    dve.wait_ge(out_stored, 16 * j)
                for h in range(2):
                    dve.wait_ge(tile_out[h], O_GATE + j + 1)
                    v.tensor_tensor(g_out[:, hs(h)], ple[:, j, hs(h)], g_sig[:, hs(h)], ALU.mult).then_inc(g_done, 1)
                for h in range(2):
                    dve.wait_ge(g_done, 2 * j + h + 1)
                    v.scalar_tensor_tensor(g_out[:, hs(h)], g_out[:, hs(h)], col(C_LN2B + j), z[:, j, hs(h)], ALU.add,
                                           ALU.add).then_inc(g_sum, 1)


def lay_out(a):
    a = {k: np.asarray(v) for k, v in a.items()}

    def units(w):
        n = w.shape[1] // P
        return w.reshape(KT, P, n, P).transpose(2, 1, 0, 3).reshape(n, P, KT * P)

    def quarters(w):
        return w.reshape(2, P, 2, 4, P).transpose(2, 1, 3, 0, 4).reshape(2, P, KT * P)

    order = [h for p in range(NPAIR) for h in (8 * (p % 2) + p // 2, 8 * (p % 2) + 4 + p // 2)]
    by_pair = np.concatenate([np.arange(h * DH, (h + 1) * DH) for h in order])

    w_in, conv_out, attn_out, w_out = (a[k][0] for k in ("w_in", "w_conv_out", "w_attn_out", "w_out"))
    kv = P * 2
    at = np.cumsum([0, D, D, D, D, D, kv, kv, D, D, D])
    v_c, b_c, c_c, z_c, q, k, v, z_a, g_a, g_b = (w_in[:, at[i]:at[i + 1]] for i in range(10))
    v_c, b_c, c_c, z_c, g_a, g_b, k, v = (units(w) for w in (v_c, b_c, c_c, z_c, g_a, g_b, k, v))
    q, z_a = units(q[:, by_pair]), units(z_a[:, by_pair])
    conv_out, attn_out, w_out = units(conv_out), units(attn_out[by_pair]), units(w_out)
    seq = []
    for i in range(KT):
        seq += [v_c[i], c_c[i], b_c[i], z_c[i]]
    for i in range(KT):
        seq += [g_a[i], conv_out[i]]
    seq += [k[0], k[1], q[0], v[0], v[1]]
    for p in range(NPAIR):
        seq += ([q[p + 1]] if p + 1 < NPAIR else []) + [z_a[p], g_b[p]]
    seq += [*attn_out, *w_out]
    w2 = a["attn_w_in_2"][0]
    seq += [*units(np.pad(w2[:, 3 * D:], ((0, 0), (0, P - 2 * NPAIR))))]
    fq, fk, fv = (units(w2[:, i * D:(i + 1) * D]) for i in range(3))
    for p in range(NPAIR):
        seq += [fq[p], fk[p], fv[p]]
    seq += [*units(a["attn_w_out_2"][0])] * 2
    w_up, w_down = a["ffn_w_up_2"][0], a["ffn_w_down_2"][0]
    u, g = units(w_up[:, :FFN]), units(w_up[:, FFN:])
    down = [quarters(w_down[n * 2 * P:(n + 1) * 2 * P]) for n in range(NGRP)]
    for n in range(NGRP):
        seq += [u[2 * n], g[2 * n], u[2 * n + 1], g[2 * n + 1]]
        if n:
            seq += [*down[n - 1]]
    seq += [*down[-1], *quarters(a["ple_w_proj_2"][0]), *units(a["ple_w_gate_2"][0])]
    weights = np.stack(seq)
    assert weights.shape[0] == U_END

    def columns(vec):
        return vec.reshape(-1, P).T

    def taps(w):
        return w.reshape(3, -1, P).transpose(2, 1, 0).reshape(P, -1)

    cols = np.concatenate([
        columns(a["norm_g"][0]), taps(a["conv_w"][0]), columns(np.tile(a["q_norm_g"][0], 2)),
        columns(np.tile(a["k_norm_g"][0], 2)), columns(a["gate_b"][0]), taps(a["ffn_conv_w_2"][0]),
        columns(a["ffn_conv_b_2"][0]), columns(a["ln_mix_g_2"][0]), columns(a["ln_mix_b_2"][0]),
        columns(a["ln_ffn_g_2"][0]), columns(a["ln_ffn_b_2"][0]), columns(a["ple_b_gate_2"][0]),
        columns(np.pad(a["attn_b_f_2"][0], (0, P - 2 * NPAIR))), np.tile(a["sinks"][0][order], (P, 1))], axis=1)
    assert cols.shape == (P, N_COLS)

    def feature_major(x):
        return np.ascontiguousarray(x.T.reshape(-1, P, S))

    return {"in_x": feature_major(a["x"][0]), "in_w": weights, "in_cols": np.ascontiguousarray(cols),
            "in_p": feature_major(a["p_2"][0, 0])}


def kernel(**inputs):
    import concourse.bacc as _bacc
    from concourse import mybir as _mybir
    from concourse.bass_utils import run_bass_kernel_spmd as _run

    arrays = lay_out(inputs)
    nc = _bacc.Bacc("TRN2", target_bir_lowering=False, num_devices=1)
    f32 = _mybir.dt.float32
    ins = {k: nc.dram_tensor(k, a.shape, f32, kind="ExternalInput").ap() for k, a in arrays.items()}
    out = nc.dram_tensor("out_y", (KT, P, S), f32, kind="ExternalOutput").ap()
    t_scr = nc.dram_tensor("t_scr", (KT, P, S), f32, kind="Internal").ap()
    g_scr = nc.dram_tensor("g_scr", (KT, P, S), f32, kind="Internal").ap()
    c_scr = nc.dram_tensor("c_scr", (2 * NPAIR, S), f32, kind="Internal").ap()
    build(nc, ins["in_x"], ins["in_w"], ins["in_cols"], ins["in_p"], out, t_scr, g_scr, c_scr)
    r = _run(nc, [arrays], core_ids=[0])
    return np.ascontiguousarray(r.results[0]["out_y"].reshape(D, S).T).reshape(1, S, D)
```
